# Optimizing a Trainium2 kernel written in Bass

```python
import jax, jax.numpy as jnp
from jax import lax
import numpy as np

D_MODEL = 1024
BATCH = 1
SEQ = 256
DEPTH = 2

CHUNK = 64
N_A_LAYERS = DEPTH // 2
N_B_LAYERS = DEPTH - N_A_LAYERS
GMLP_BLOCK = 128
GMLP_WIDTH = D_MODEL
GMLP_GROUPS = 8
GMLP_GROUP_DIM = GMLP_WIDTH // GMLP_GROUPS
N_HEADS = 16
HEAD_DIM = D_MODEL // N_HEADS
LEFT_CHUNKS = 8
BAND = (LEFT_CHUNKS + 1) * CHUNK
PAD = LEFT_CHUNKS * CHUNK
REL_CLIP = 128
REL_SIZE = 2 * REL_CLIP + 1
D_FF = ((8 * D_MODEL // 3 + 127) // 128) * 128
CONV_WIDTH = 3
EPS = 1e-6
NEG_INF = -1e30


def rmsnorm(x, g):
    xf = x.astype(jnp.float32)
    y = xf * lax.rsqrt(jnp.mean(xf * xf, axis=-1, keepdims=True) + EPS)
    return (y * g.astype(jnp.float32)).astype(x.dtype)

def gmlp_mixer(h, w_in, v_norm_g, w_s, b_s, w_out):
    B, S, _ = h.shape
    z = jax.nn.gelu(h @ w_in)
    u, v = jnp.split(z, 2, axis=-1)
    v = rmsnorm(v, v_norm_g)
    pos_chunk = jnp.arange(GMLP_BLOCK) // CHUNK
    mask = pos_chunk[:, None] >= pos_chunk[None, :]
    w = jnp.where(mask[None], w_s, 0)
    v = v.reshape(B, S // GMLP_BLOCK, GMLP_BLOCK, GMLP_GROUPS, GMLP_GROUP_DIM)
    s = jnp.einsum('gij,bnjgc->bnigc', w, v) + b_s.T[None, None, :, :, None]
    out = u * s.reshape(B, S, GMLP_WIDTH)
    return out @ w_out

def chunk_attention(h, k, v, w_q, rel_bias, w_o):
    B, S, _ = h.shape
    nc = S // CHUNK
    scale = HEAD_DIM ** -0.5
    q = (h @ w_q).reshape(B, nc, CHUNK, N_HEADS, HEAD_DIM) * scale
    qc = jnp.moveaxis(q, 1, 0)
    kp = jnp.pad(k, ((0, 0), (PAD, 0), (0, 0), (0, 0)))
    vp = jnp.pad(v, ((0, 0), (PAD, 0), (0, 0), (0, 0)))
    qi = jnp.arange(CHUNK)[:, None]
    kj = jnp.arange(BAND)[None, :]
    rel_idx = jnp.clip(qi - kj + PAD, -REL_CLIP, REL_CLIP) + REL_CLIP
    bias = rel_bias[:, rel_idx].astype(jnp.float32)

    def one_chunk(args):
        c, qb = args
        start = c * CHUNK
        kb = lax.dynamic_slice_in_dim(kp, start, BAND, axis=1)
        vb = lax.dynamic_slice_in_dim(vp, start, BAND, axis=1)
        sc = jnp.einsum('bqhd,bkhd->bhqk', qb, kb).astype(jnp.float32) + bias
        valid = (start - PAD + jnp.arange(BAND)) >= 0
        sc = jnp.where(valid[None, None, None, :], sc, NEG_INF)
        p = jax.nn.softmax(sc, axis=-1).astype(vb.dtype)
        return jnp.einsum('bhqk,bkhd->bqhd', p, vb)

    o = lax.map(one_chunk, (jnp.arange(nc), qc))
    o = jnp.moveaxis(o, 0, 1).reshape(B, S, N_HEADS * HEAD_DIM)
    return o @ w_o

def conv_ffn(h, w_in, conv_w, conv_b, w_down):
    a = h @ w_in
    C = a.shape[-1]
    a = lax.conv_general_dilated(
        a, conv_w[:, None, :].astype(a.dtype), window_strides=(1,),
        padding=[(CONV_WIDTH - 1, 0)], dimension_numbers=('NWC', 'WIO', 'NWC'),
        feature_group_count=C) + conv_b
    up, gate = jnp.split(a, 2, axis=-1)
    return (jax.nn.silu(gate) * up) @ w_down

def first_inputs(seed: int = 0) -> dict:
    key = jax.random.key(seed)
    ks = jax.random.split(key, 20)
    nrm = lambda k, shape, s: jax.random.normal(k, shape, jnp.float32) * s
    gain = lambda k, shape: 1.0 + nrm(k, shape, 0.02)
    HD = N_HEADS * HEAD_DIM
    return {
        "x": nrm(ks[0], (BATCH, SEQ, D_MODEL), 1.0),
        "a_norm_g": gain(ks[1], (N_A_LAYERS, D_MODEL)),
        "a_w_in": nrm(ks[2], (N_A_LAYERS, D_MODEL, 2 * GMLP_WIDTH), D_MODEL ** -0.5),
        "a_v_norm_g": gain(ks[3], (N_A_LAYERS, GMLP_WIDTH)),
        "a_w_s": nrm(ks[4], (N_A_LAYERS, GMLP_GROUPS, GMLP_BLOCK, GMLP_BLOCK), GMLP_BLOCK ** -0.5),
        "a_b_s": 1.0 + nrm(ks[5], (N_A_LAYERS, GMLP_GROUPS, GMLP_BLOCK), 0.01),
        "a_w_out": nrm(ks[6], (N_A_LAYERS, GMLP_WIDTH, D_MODEL), GMLP_WIDTH ** -0.5),
        "kv_norm_g": gain(ks[7], (D_MODEL,)),
        "w_kv": nrm(ks[8], (D_MODEL, 2 * HD), D_MODEL ** -0.5),
        "b_norm_g": gain(ks[9], (N_B_LAYERS, D_MODEL)),
        "b_w_q": nrm(ks[10], (N_B_LAYERS, D_MODEL, HD), D_MODEL ** -0.5),
        "b_rel_bias": nrm(ks[11], (N_B_LAYERS, N_HEADS, REL_SIZE), 0.5),
        "b_w_o": nrm(ks[12], (N_B_LAYERS, HD, D_MODEL), HD ** -0.5),
        "f_norm_g": gain(ks[13], (DEPTH, D_MODEL)),
        "f_w_in": nrm(ks[14], (DEPTH, D_MODEL, 2 * D_FF), D_MODEL ** -0.5),
        "f_conv_w": nrm(ks[15], (DEPTH, CONV_WIDTH, 2 * D_FF), CONV_WIDTH ** -0.5),
        "f_conv_b": nrm(ks[16], (DEPTH, 2 * D_FF), 0.01),
        "f_w_down": nrm(ks[17], (DEPTH, D_FF, D_MODEL), D_FF ** -0.5),
        "final_norm_g": gain(ks[18], (D_MODEL,)),
    }

def first_block(x, a_norm_g, a_w_in, a_v_norm_g, a_w_s, a_b_s, a_w_out,
              kv_norm_g, w_kv, b_norm_g, b_w_q, b_rel_bias, b_w_o,
              f_norm_g, f_w_in, f_conv_w, f_conv_b, f_w_down, final_norm_g):
    B, S, _ = x.shape
    h = x
    k_shared = v_shared = None
    for l in range(DEPTH):
        if l < N_A_LAYERS:
            h = h + gmlp_mixer(rmsnorm(h, a_norm_g[l]), a_w_in[l], a_v_norm_g[l],
                               a_w_s[l], a_b_s[l], a_w_out[l])
        else:
            if l == N_A_LAYERS:
                kv = rmsnorm(h, kv_norm_g) @ w_kv
                k_shared, v_shared = jnp.split(kv, 2, axis=-1)
                k_shared = k_shared.reshape(B, S, N_HEADS, HEAD_DIM)
                v_shared = v_shared.reshape(B, S, N_HEADS, HEAD_DIM)
            j = l - N_A_LAYERS
            h = h + chunk_attention(rmsnorm(h, b_norm_g[j]), k_shared, v_shared,
                                    b_w_q[j], b_rel_bias[j], b_w_o[j])
        h = h + conv_ffn(rmsnorm(h, f_norm_g[l]), f_w_in[l], f_conv_w[l],
                         f_conv_b[l], f_w_down[l])
    return rmsnorm(h, final_norm_g)


HEAD_DIM_2 = 64
N_HEADS_2 = D_MODEL // HEAD_DIM_2
FOX_HEADS = N_HEADS_2 // 2
SWA_HEADS = N_HEADS_2 - FOX_HEADS
SWA_KV_HEADS = max(1, SWA_HEADS // 4)
SWA_WINDOW = 128
Q_BLOCK = 128
DSA_HEADS = N_HEADS_2
DSA_KV_HEADS = max(1, DSA_HEADS // 4)
IDX_HEADS = 8
IDX_DIM = 64
DSA_TOPK_MAX = 256
D_FF_2 = 2816
N_EXPERTS = 8
TOP_K = 2
D_FF_EXPERT = 1408
ROPE_THETA = 10000.0
NORM_EPS = 1e-6
N_EVEN = (DEPTH + 1) // 2
N_ODD = DEPTH // 2

EVEN_SPLITS = (FOX_HEADS * HEAD_DIM_2, FOX_HEADS * HEAD_DIM_2, FOX_HEADS * HEAD_DIM_2, FOX_HEADS,
               SWA_HEADS * HEAD_DIM_2, SWA_KV_HEADS * HEAD_DIM_2, SWA_KV_HEADS * HEAD_DIM_2)
EVEN_IN = sum(EVEN_SPLITS)
ODD_SPLITS = (DSA_HEADS * HEAD_DIM_2, DSA_KV_HEADS * HEAD_DIM_2, DSA_KV_HEADS * HEAD_DIM_2,
              IDX_HEADS * IDX_DIM, IDX_DIM, IDX_HEADS)
ODD_IN = sum(ODD_SPLITS)


def _split(t, sizes):
    return jnp.split(t, np.cumsum(sizes)[:-1].tolist(), axis=-1)

def rms_norm(x, g):
    xf = x.astype(jnp.float32)
    y = xf * lax.rsqrt(jnp.mean(xf * xf, axis=-1, keepdims=True) + NORM_EPS)
    return (y * g.astype(jnp.float32)).astype(x.dtype)

def ada_modulation(c, w, b):
    mod = jax.nn.silu(c) @ w + b
    return jnp.split(mod[:, None, :], 6, axis=-1)

def rope_tables(positions, dim):
    half = dim // 2
    inv_freq = ROPE_THETA ** (-jnp.arange(half, dtype=jnp.float32) / half)
    ang = positions.astype(jnp.float32)[..., None] * inv_freq
    return jnp.cos(ang)[:, :, None, :], jnp.sin(ang)[:, :, None, :]

def apply_rope(t, cos, sin):
    half = t.shape[-1] // 2
    tf = t.astype(jnp.float32)
    t1, t2 = tf[..., :half], tf[..., half:]
    return jnp.concatenate([t1 * cos - t2 * sin, t2 * cos + t1 * sin], axis=-1).astype(t.dtype)

def swiglu(h, w_gate, w_up, w_down):
    return (jax.nn.silu(h @ w_gate) * (h @ w_up)) @ w_down

def forgetting_attention(q, k, v, log_f):
    B, S, H, D = q.shape
    cum = jnp.cumsum(log_f.astype(jnp.float32), axis=1).transpose(0, 2, 1)
    kpos = jnp.arange(S)
    scale = D ** -0.5

    def block(i):
        start = i * Q_BLOCK
        qi = lax.dynamic_slice_in_dim(q, start, Q_BLOCK, axis=1)
        ci = lax.dynamic_slice_in_dim(cum, start, Q_BLOCK, axis=2)
        s = jnp.einsum('bqhd,bkhd->bhqk', qi, k, preferred_element_type=jnp.float32) * scale
        s = s + ci[..., :, None] - cum[..., None, :]
        qpos = start + jnp.arange(Q_BLOCK)
        s = jnp.where(kpos[None, :] <= qpos[:, None], s, -jnp.inf)
        p = jax.nn.softmax(s, axis=-1)
        return jnp.einsum('bhqk,bkhd->bqhd', p.astype(v.dtype), v)

    out = lax.map(block, jnp.arange(S // Q_BLOCK))
    return jnp.moveaxis(out, 0, 1).reshape(B, S, H, D)

def sliding_window_sink_attention(q, k, v, sinks):
    B, S, H, D = q.shape
    KVH = k.shape[2]
    G = H // KVH
    W = SWA_WINDOW
    nb = S // W
    qb = q.reshape(B, nb, W, KVH, G, D)

    def band_keys(t):
        tb = t.reshape(B, nb, W, KVH, D)
        prev = jnp.concatenate([jnp.zeros_like(tb[:, :1]), tb[:, :-1]], axis=1)
        return jnp.concatenate([prev, tb], axis=2)

    kk, vv = band_keys(k), band_keys(v)
    s = jnp.einsum('bnqhgd,bnshd->bnhgqs', qb, kk, preferred_element_type=jnp.float32) * D ** -0.5
    rel = (jnp.arange(W)[:, None] + W) - jnp.arange(2 * W)[None, :]
    band = (rel >= 0) & (rel < W)
    not_pad = (jnp.arange(nb)[:, None, None] > 0) | (jnp.arange(2 * W) >= W)[None, None, :]
    valid = band[None] & not_pad
    s = jnp.where(valid[None, :, None, None], s, -jnp.inf)
    sink = sinks.astype(jnp.float32).reshape(KVH, G)[None, None, :, :, None, None]
    m = jnp.maximum(jnp.max(s, axis=-1, keepdims=True), sink)
    e = jnp.exp(s - m)
    p = e / (jnp.sum(e, axis=-1, keepdims=True) + jnp.exp(sink - m))
    out = jnp.einsum('bnhgqs,bnshd->bnqhgd', p.astype(v.dtype), vv)
    return out.reshape(B, S, H, D)

def dsa_attention(q, k, v, iq, ik, iw):
    B, S, H, D = q.shape
    KVH = k.shape[2]
    G = H // KVH
    topk = min(DSA_TOPK_MAX, S // 4)
    kpos = jnp.arange(S)
    scale = D ** -0.5
    gather = jax.vmap(lambda tb, ib: tb[ib])

    def block(i):
        start = i * Q_BLOCK
        qi = lax.dynamic_slice_in_dim(q, start, Q_BLOCK, axis=1).reshape(B, Q_BLOCK, KVH, G, D)
        iqi = lax.dynamic_slice_in_dim(iq, start, Q_BLOCK, axis=1)
        iwi = lax.dynamic_slice_in_dim(iw, start, Q_BLOCK, axis=1).astype(jnp.float32)
        qpos = start + jnp.arange(Q_BLOCK)
        logits = jnp.einsum('bqhd,bsd->bqhs', iqi, ik, preferred_element_type=jnp.float32)
        score = jnp.einsum('bqh,bqhs->bqs', iwi, jax.nn.relu(logits))
        score = jnp.where((kpos[None, :] <= qpos[:, None])[None], score, -jnp.inf)
        _, idx = lax.top_k(score, topk)
        sel_valid = idx <= qpos[None, :, None]
        ks = gather(k, idx)
        vs = gather(v, idx)
        s = jnp.einsum('bqhgd,bqthd->bhgqt', qi, ks, preferred_element_type=jnp.float32) * scale
        s = jnp.where(sel_valid[:, None, None], s, -jnp.inf)
        p = jax.nn.softmax(s, axis=-1)
        o = jnp.einsum('bhgqt,bqthd->bqhgd', p.astype(v.dtype), vs)
        return o.reshape(B, Q_BLOCK, H, D)

    out = lax.map(block, jnp.arange(S // Q_BLOCK))
    return jnp.moveaxis(out, 0, 1).reshape(B, S, H, D)

def moe_swiglu(h, router_w, router_b, w_gate, w_up, w_down):
    B, S, Dm = h.shape
    t = h.reshape(B * S, Dm)
    logits = (t @ router_w).astype(jnp.float32) + router_b.astype(jnp.float32)
    top_vals, top_idx = lax.top_k(logits, TOP_K)
    gates = jax.nn.softmax(top_vals, axis=-1)
    combine = jnp.sum(jax.nn.one_hot(top_idx, N_EXPERTS, dtype=jnp.float32) * gates[..., None], axis=1)
    combine = combine.astype(h.dtype)
    out = jnp.zeros_like(t)
    for e in range(N_EXPERTS):
        out = out + combine[:, e:e + 1] * swiglu(t, w_gate[e], w_up[e], w_down[e])
    return out.reshape(B, S, Dm)

def even_layer(x, c, cos, sin, ada_w, ada_b, norm_mix, norm_ffn, w_in, forget_b, sinks, w_out,
               ffn_gate, ffn_up, ffn_down):
    B, S, _ = x.shape
    sh_m, sc_m, g_m, sh_f, sc_f, g_f = ada_modulation(c, ada_w, ada_b)
    h = rms_norm(x, norm_mix) * (1 + sc_m) + sh_m
    fq, fk, fv, fgl, sq, sk, sv = _split(h @ w_in, EVEN_SPLITS)
    heads = lambda t, n: t.reshape(B, S, n, HEAD_DIM_2)
    log_f = jax.nn.log_sigmoid((fgl + forget_b).astype(jnp.float32))
    o_fox = forgetting_attention(heads(fq, FOX_HEADS), heads(fk, FOX_HEADS), heads(fv, FOX_HEADS), log_f)
    o_swa = sliding_window_sink_attention(apply_rope(heads(sq, SWA_HEADS), cos, sin),
                                          apply_rope(heads(sk, SWA_KV_HEADS), cos, sin),
                                          heads(sv, SWA_KV_HEADS), sinks)
    mix = jnp.concatenate([o_fox.reshape(B, S, -1), o_swa.reshape(B, S, -1)], axis=-1) @ w_out
    x = x + g_m * mix
    h = rms_norm(x, norm_ffn) * (1 + sc_f) + sh_f
    return x + g_f * swiglu(h, ffn_gate, ffn_up, ffn_down)

def odd_layer(x, c, cos, sin, ada_w, ada_b, norm_mix, norm_ffn, w_in, w_out,
              router_w, router_b, exp_gate, exp_up, exp_down):
    B, S, _ = x.shape
    sh_m, sc_m, g_m, sh_f, sc_f, g_f = ada_modulation(c, ada_w, ada_b)
    h = rms_norm(x, norm_mix) * (1 + sc_m) + sh_m
    q, k, v, iq, ik, iw = _split(h @ w_in, ODD_SPLITS)
    q = apply_rope(q.reshape(B, S, DSA_HEADS, HEAD_DIM_2), cos, sin)
    k = apply_rope(k.reshape(B, S, DSA_KV_HEADS, HEAD_DIM_2), cos, sin)
    v = v.reshape(B, S, DSA_KV_HEADS, HEAD_DIM_2)
    iq = apply_rope(iq.reshape(B, S, IDX_HEADS, IDX_DIM), cos, sin)
    ik = apply_rope(ik.reshape(B, S, 1, IDX_DIM), cos, sin)[:, :, 0]
    iw = iw * (IDX_HEADS ** -0.5 * IDX_DIM ** -0.5)
    o = dsa_attention(q, k, v, iq, ik, iw)
    x = x + g_m * (o.reshape(B, S, -1) @ w_out)
    h = rms_norm(x, norm_ffn) * (1 + sc_f) + sh_f
    return x + g_f * moe_swiglu(h, router_w, router_b, exp_gate, exp_up, exp_down)

def second_inputs(seed: int = 0) -> dict:
    key = jax.random.key(seed)
    ks = iter(jax.random.split(key, 40))
    D = D_MODEL

    def nrm(shape, s):
        return jax.random.normal(next(ks), shape, jnp.float32) * s

    x = nrm((BATCH, SEQ, D), 1.0)
    c = nrm((BATCH, D), 1.0)
    offset = jax.random.randint(next(ks), (BATCH, 1), 0, 4096, dtype=jnp.int32)
    positions = offset + jnp.arange(SEQ, dtype=jnp.int32)[None, :]
    return {
        'x': x, 'c': c, 'positions': positions,
        'e_ada_w': nrm((N_EVEN, D, 6 * D), 0.5 * D ** -0.5),
        'e_ada_b': nrm((N_EVEN, 6 * D), 0.02),
        'e_norm_mix': 1.0 + nrm((N_EVEN, D), 0.05),
        'e_norm_ffn': 1.0 + nrm((N_EVEN, D), 0.05),
        'e_w_in': nrm((N_EVEN, D, EVEN_IN), D ** -0.5),
        'e_forget_b': 3.0 + nrm((N_EVEN, FOX_HEADS), 1.0),
        'e_sinks': nrm((N_EVEN, SWA_HEADS), 1.0),
        'e_w_out': nrm((N_EVEN, D, D), D ** -0.5),
        'e_ffn_gate': nrm((N_EVEN, D, D_FF_2), D ** -0.5),
        'e_ffn_up': nrm((N_EVEN, D, D_FF_2), D ** -0.5),
        'e_ffn_down': nrm((N_EVEN, D_FF_2, D), D_FF_2 ** -0.5),
        'o_ada_w': nrm((N_ODD, D, 6 * D), 0.5 * D ** -0.5),
        'o_ada_b': nrm((N_ODD, 6 * D), 0.02),
        'o_norm_mix': 1.0 + nrm((N_ODD, D), 0.05),
        'o_norm_ffn': 1.0 + nrm((N_ODD, D), 0.05),
        'o_w_in': nrm((N_ODD, D, ODD_IN), D ** -0.5),
        'o_w_out': nrm((N_ODD, D, D), D ** -0.5),
        'o_router_w': nrm((N_ODD, D, N_EXPERTS), D ** -0.5),
        'o_router_b': nrm((N_ODD, N_EXPERTS), 0.01),
        'o_exp_gate': nrm((N_ODD, N_EXPERTS, D, D_FF_EXPERT), D ** -0.5),
        'o_exp_up': nrm((N_ODD, N_EXPERTS, D, D_FF_EXPERT), D ** -0.5),
        'o_exp_down': nrm((N_ODD, N_EXPERTS, D_FF_EXPERT, D), D_FF_EXPERT ** -0.5),
        'final_norm': 1.0 + nrm((D,), 0.05),
    }

def second_block(x, c, positions,
              e_ada_w, e_ada_b, e_norm_mix, e_norm_ffn, e_w_in, e_forget_b, e_sinks, e_w_out,
              e_ffn_gate, e_ffn_up, e_ffn_down,
              o_ada_w, o_ada_b, o_norm_mix, o_norm_ffn, o_w_in, o_w_out,
              o_router_w, o_router_b, o_exp_gate, o_exp_up, o_exp_down,
              final_norm):
    cos, sin = rope_tables(positions, HEAD_DIM_2)
    for layer in range(DEPTH):
        i = layer // 2
        if layer % 2 == 0:
            x = even_layer(x, c, cos, sin, e_ada_w[i], e_ada_b[i], e_norm_mix[i], e_norm_ffn[i],
                           e_w_in[i], e_forget_b[i], e_sinks[i], e_w_out[i],
                           e_ffn_gate[i], e_ffn_up[i], e_ffn_down[i])
        else:
            x = odd_layer(x, c, cos, sin, o_ada_w[i], o_ada_b[i], o_norm_mix[i], o_norm_ffn[i],
                          o_w_in[i], o_w_out[i], o_router_w[i], o_router_b[i],
                          o_exp_gate[i], o_exp_up[i], o_exp_down[i])
    return rms_norm(x, final_norm)


def setup_inputs(seed=0):
    out = dict(first_inputs(seed))
    for name, value in second_inputs(seed + 1).items():
        if name != "x":
            out[name + "_2"] = value
    return out


def reference(
    x, a_norm_g, a_w_in, a_v_norm_g, a_w_s, a_b_s, a_w_out, kv_norm_g, w_kv, b_norm_g, b_w_q,
    b_rel_bias, b_w_o, f_norm_g, f_w_in, f_conv_w, f_conv_b, f_w_down, final_norm_g, c_2,
    positions_2, e_ada_w_2, e_ada_b_2, e_norm_mix_2, e_norm_ffn_2, e_w_in_2, e_forget_b_2,
    e_sinks_2, e_w_out_2, e_ffn_gate_2, e_ffn_up_2, e_ffn_down_2, o_ada_w_2, o_ada_b_2,
    o_norm_mix_2, o_norm_ffn_2, o_w_in_2, o_w_out_2, o_router_w_2, o_router_b_2, o_exp_gate_2,
    o_exp_up_2, o_exp_down_2, final_norm_2,
):
    x = first_block(
        x, a_norm_g, a_w_in, a_v_norm_g, a_w_s, a_b_s, a_w_out, kv_norm_g, w_kv, b_norm_g,
        b_w_q, b_rel_bias, b_w_o, f_norm_g, f_w_in, f_conv_w, f_conv_b, f_w_down, final_norm_g,
    )
    return second_block(
        x, c_2, positions_2, e_ada_w_2, e_ada_b_2, e_norm_mix_2, e_norm_ffn_2, e_w_in_2,
        e_forget_b_2, e_sinks_2, e_w_out_2, e_ffn_gate_2, e_ffn_up_2, e_ffn_down_2, o_ada_w_2,
        o_ada_b_2, o_norm_mix_2, o_norm_ffn_2, o_w_in_2, o_w_out_2, o_router_w_2, o_router_b_2,
        o_exp_gate_2, o_exp_up_2, o_exp_down_2, final_norm_2,
    )


_drawn_inputs = setup_inputs


def setup_inputs(seed=0):
    import zlib

    import numpy as np

    out = dict(_drawn_inputs(seed))
    spreads = {}
    factors = {'a_v_norm_g': 3.639,
     'a_b_s': 3.695,
     'kv_norm_g': 4.077,
     'b_norm_g': 8.0,
     'f_conv_b': 3.828,
     'e_norm_mix_2': 3.711,
     'e_sinks_2': 6.449,
     'o_norm_mix_2': 3.004,
     'o_router_b_2': 20.397,
     'o_norm_ffn_2': 3.457}
    for name, (base, spread) in spreads.items():
        noise = np.random.default_rng([zlib.crc32(name.encode()), seed]).standard_normal(out[name].shape)
        drawn = base * np.exp(spread * noise) if base else spread * noise
        out[name] = __import__('jax').numpy.asarray(drawn.astype(out[name].dtype))
    for name, factor in factors.items():
        out[name] = (out[name] * factor).astype(out[name].dtype)
    return out
```

```python
from contextlib import ExitStack

import concourse.bass as bass
from concourse import mybir

F32 = mybir.dt.float32
F32R = mybir.dt.float32r
I32 = mybir.dt.int32
U32 = mybir.dt.uint32
ALU = mybir.AluOpType
ACT = mybir.ActivationFunctionType
AXX = mybir.AxisListType.X

P = 128
D = 1024
S = 256
NT = S // P
KT = D // P
DH = 64
NH = D // DH
FF = 2816
FK = FF // P
FE = 1408
NE = 8
W = 512
SLOT = 2048
RAW = 6
SPL = 3
AHEAD = 2
EXP = 18
EPS = 1e-6
NEG = -1e30
GONE = -3e38
E_IN = 2312
O_IN = 2120
TOPK = S // 4
REL = 128
ROPE_THETA = 10000.0
PI = 3.14159265358979
TWO_PI_A = 6.28125
TWO_PI_B = 0.0019340515136718750
TWO_PI_C = 2 * 3.141592653589793 - 6.28125 - 0.0019340515136718750
ROUND = 12582912.0

C_GA, C_GKV, C_GB, C_GF0, C_GF1, C_GEM, C_GEF, C_GOM, C_GOF = (KT * n for n in range(9))
C_CW = 9 * KT
C_CB = C_CW + 2 * 3 * 2 * FK
C_BS = C_CB + 2 * 2 * FK
C_AB = C_BS + KT
C_C = C_AB + 2 * 6 * KT
C_END = C_C + KT
R_FB, R_SK, R_RB, R_IF = 0, 8, 16, 24
R_END = R_IF + DH // 2


def stream_plan():
    plan = []
    at = {}

    def proj(name, n):
        at[name] = len(plan)
        for c in range(0, n, W):
            w = min(W, n - c)
            plan.extend([(4 * w, 1)] * 2)

    def gated(name, kt, pairs=1):
        at[name] = len(plan)
        for _ in range(pairs):
            plan.extend([(SLOT, 2)] * (2 * (kt // 2)))
            if kt % 2:
                plan.extend([(SLOT // 2, 2)] * 2)
            plan.extend([(SLOT, 1)] * (kt // 2))
            if kt % 2:
                plan.append((SLOT // 2, 1))

    proj("gmlp_in", 2 * D)
    proj("gmlp_out", D)
    gated("ffn0", FK)
    proj("kv", 2 * D)
    proj("q", D)
    proj("attn_out", D)
    gated("ffn1", FK)
    proj("e_ada", 6 * D)
    proj("e_in", E_IN)
    proj("e_out", D)
    gated("e_ffn", FK)
    proj("o_ada", 6 * D)
    proj("o_in", O_IN)
    proj("o_out", D)
    gated("moe", FE // P, NE)
    at["spare"] = len(plan)
    plan.extend([(SLOT, 2)] * AHEAD)
    gated("more", FE // P, NE)
    at["end"] = len(plan)
    landed, counts = [], [0] * RAW
    for s, (_, n) in enumerate(plan):
        counts[s % RAW] += 16 * n
        landed.append(counts[s % RAW])
    return plan, at, landed


class Tally:

    def __init__(self):
        self.n, self.per, self.i = {}, {}, None

    def up(self, name, k=1):
        self.n[name] = self.n.get(name, 0) + k
        return self(name)

    def __call__(self, name, less=0):
        v = self.n.get(name, 0) - less
        return v if self.i is None or not self.per.get(name) else self.i * self.per[name] + v

    def loop(self, i, **per):
        self.i, self.per, self.start = i, per, dict(self.n)

    def end(self, turns):
        for k in set(self.n) | set(self.per):
            made = self.n.get(k, 0) - self.start.get(k, 0)
            assert made == self.per.get(k, 0), (k, made)
            self.n[k] = self.n.get(k, 0) + made * (turns - 1)
        self.i = None


def build_program(nc, x_in, cols_in, rows_in, vg_in, fg1_in, fg_in, adab_in, pos_in, ws_in, toep_in, rw_in,
                  w_in, w_out, w_kv, w_q, w_o, f_in, f_down,
                  e_ada, e_in, e_out, e_gate, e_up, e_down,
                  o_ada, o_in, o_out, x_gate, x_up, x_down, out):
    plan, AT, LANDED = stream_plan()
    ctx = ExitStack()
    with ctx:
        def sb(name, shape, dt=F32):
            return ctx.enter_context(nc.sbuf_tensor(name, shape, dt))

        sems = {}

        def sem(name):
            if name not in sems:
                sems[name] = ctx.enter_context(nc.semaphore(name))
            return sems[name]

        h = sb("h", [P, NT, D])
        tok = sb("tok", [P, 3 * NT * D])
        xhi = sb("xhi", [P, KT, S], F32R)
        xlo = sb("xlo", [P, KT, S], F32R)
        raw = sb("raw", [P, RAW, SLOT])
        whi = sb("whi", [P, SPL, SLOT], F32R)
        wlo = sb("wlo", [P, SPL, SLOT], F32R)
        gates = sb("gates", [P, 2, D])
        ident = sb("ident", [P, P])
        ones = sb("ones", [P, P])
        tri = sb("tri", [P, P])
        causal = sb("causal", [P, S])
        window = sb("window", [P, S])
        cols = sb("cols", [P, C_END])
        rows = sb("rows", [P, R_END])
        rw = sb("rw", [P, KT, NE])
        scl = sb("scl", [P, 2, KT])
        shf = sb("shf", [P, 2, KT])
        cs = sb("cs", [P, KT])
        st = sb("st", [P, 64])
        cosT = sb("cosT", [P, NT, DH // 2])
        sinT = sb("sinT", [P, NT, DH // 2])
        posi = sb("posi", [P, NT], I32)
        ps = ctx.enter_context(nc.psum_tensor("ps", [P, 8, 512], F32))
        comb = sb("comb", [P, NT, NE + 1])
        member = sb("member", [P, NT, NE])
        place = sb("place", [P, NT, 2 * NE])
        count = sb("count", [1, NE], I32)
        iotai = sb("iotai", [P, P], I32)
        iota = sb("iota", [P, P])
        mx8 = sb("mx8", [P, NT, 8])
        ix8 = sb("ix8", [P, NT, 8], U32)
        idxf = sb("idxf", [P, NT, 8])
        g2 = sb("g2", [P, NT, 4])
        eqe = sb("eqe", [P, NT, NE])
        rot = sb("rot", [P, 4, NT * DH // 2])
        with nc.sbuf_tensor("ahi", [P, FK, S], F32R) as ahi, nc.sbuf_tensor("alo", [P, FK, S], F32R) as alo:
            pass
        af = sb("attn_scratch", [P, FK * S])[:, :]
        lf = sb("head_scratch", [P, FK * S])[:, :]

        TA, TB, TC = (tok[:, n * NT * D:(n + 1) * NT * D].rearrange("p (t d) -> p t d", t=NT) for n in range(3))
        te = tok[:, 0:NT * E_IN].rearrange("p (t d) -> p t d", t=NT)
        to = tok[:, 0:NT * O_IN].rearrange("p (t d) -> p t d", t=NT)
        xT_c = tok[:, 2 * NT * D:3 * NT * D].rearrange("p (k s) -> p k s", k=KT)
        ab = tok[:, 2048:3072].rearrange("p (t c) -> p t c", t=NT)
        conv = tok[:, 3072:4096].rearrange("p (f s) -> p f s", f=4)
        sg = tok[:, 4096:4608].rearrange("p (f s) -> p f s", f=2)
        modrow = tok[0:1, 4096:6144]
        bias = af[:, 0:NH * S].rearrange("p (h k) -> p h k", h=NH)
        sm = af[:, 4096:4608].rearrange("p (b k) -> p b k", b=2)
        pr = af[:, 4608:5120].rearrange("p (b k) -> p b k", b=2)
        pT = af[:, 5120:5632].rearrange("p (b k) -> p b k", b=2)
        qT = lf[:, 0:2048].rearrange("p (k s) -> p k s", k=KT)
        kT = lf[:, 2048:4096].rearrange("p (k s) -> p k s", k=KT)
        iqT = lf[:, 4096:5120].rearrange("p (k s) -> p k s", k=4)
        ikT = lf[:, 5120:5376]
        ws = lf[:, 0:1024].rearrange("p (g j) -> p g j", g=KT)
        wsT = lf[:, 1024:2048].rearrange("p (g i) -> p g i", g=KT)
        vg = lf[:, 2048:3072]
        xT_b = lf[:, 0:2048].rearrange("p (k s) -> p k s", k=KT)
        kd = af[:, 0:1024].rearrange("p (t j c d) -> p t j c d", t=NT, j=4, c=2)
        ikd = af[:, 1024:1280].rearrange("p (t c d) -> p t c d", t=NT, c=2)
        rt = [af[:, 1280 + n * 640:1280 + (n + 1) * 640] for n in range(4)]
        sel8 = af[0:8, 1280:2304].rearrange("p (h i) -> p h i", h=8)
        ncT = af[0:8, 2304:2560]
        lgf = af[:, 3840:3920].rearrange("p (n t h) -> p n t h", n=5, t=NT)
        cum = af[:, 3920:3936].rearrange("p (t h) -> p t h", t=NT)
        score = af[:, 1280:1792].rearrange("p (t k) -> p t k", t=NT)
        left = af[:, 1792:2304].rearrange("p (t k) -> p t k", t=NT)
        relu = af[:, 2304:2816].rearrange("p (b k) -> p b k", b=2)
        gt = af[:, 2816:3328].rearrange("p (t k) -> p t k", t=NT)
        eq = af[:, 3328:3840].rearrange("p (t k) -> p t k", t=NT)
        dsab = af[:, 0:512].rearrange("p (t k) -> p t k", t=NT)
        adab = tok[:, 0:2048].rearrange("p (m d) -> p m d", m=2)
        macc = TB
        xg = lf[:, FE // P * S:FE // P * S + KT * P].rearrange("p (k s) -> p k s", k=KT)
        sgx = tok[:, 4096:4352]
        abx = lf[:, 4096:4608].rearrange("p (b c) -> p b c", b=2)
        ysb = tok[:, 4608:5632]
        G = tok[:, 5632:5888].rearrange("p (t j) -> p t j", t=NT)
        GT = tok[:, 5888:6144].rearrange("p (t i) -> p t i", t=NT)
        rt_logit = st[:, 32:48].rearrange("p (t e) -> p t e", t=NT)

        def pair(n, w=W):
            return ps[:, 2 * n:2 * n + 2, 0:w]

        def trb(b):
            return ps[:, 6 + b, :].rearrange("p (k s) -> p k s", k=2)

        block = ctx.enter_context(nc.Block())

        CHUNKED = [dict(q=hh // 2, k=hh // 2, v=("c", hh * DH), mask="bias", h=hh) for hh in range(NH)]
        EVEN = ([dict(q=hh // 2, k=hh // 2, v=("e", 1024 + hh * DH), mask="fox", h=hh) for hh in range(8)]
                + [dict(q=hh // 2, k=4 + (hh - 8) // 4, v=("e", 2184 + (hh - 8) // 4 * DH), mask="swa", h=hh)
                   for hh in range(8, NH)])
        ODD = [dict(q=hh // 2, k=hh // 4, v=("o", 1280 + hh // 4 * DH), mask="dsa", h=hh) for hh in range(NH)]

        def v_of(a, kk):
            where, c = a["v"]
            src = {"c": TC, "e": te, "o": to}[where]
            return src[:, kk, c:c + DH]

        @block.sync
        def _(sp):
            sp.dma_start(h[:, :, :], x_in.rearrange("o (t p) d -> p (o t) d", p=P)).then_inc(sem("x_landed"), 16)
            sp.dma_start(cols[:, :], cols_in).then_inc(sem("consts_landed"), 16)
            pos = [0]

            def load(parts, i=None, per=0):
                s = pos[0]
                pos[0] += 1
                parts = list(parts)
                assert len(parts) == plan[s][1]
                if s >= RAW:
                    sp.wait_ge(sem("lo_done"), s - RAW + 1 if i is None else i * per + (s - RAW + 1))
                for dst, src in parts:
                    sp.dma_start(dst(s % RAW), src).then_inc(sem(f"landed{s % RAW}"), 16)

            def rows_of(w, hf, c, n, at=0, width=None):
                width = width or n
                src = w.rearrange("(k p) n -> p k n", p=P)[:, 4 * hf:4 * hf + 4, c]
                return (lambda s: raw[:, s, 0:4 * width].rearrange("p (k n) -> p k n", k=4)[:, :, at:at + n], src)

            def proj(w, n):
                for c in range(0, n, W):
                    m = min(W, n - c)
                    for hf in range(2):
                        load([rows_of(w, hf, slice(c, c + m), m)])

            def down(w, kt, i=None, per=0, e=None):
                wv = w.rearrange("(k p) n -> p k n", p=P)
                for k in range(0, kt, 2):
                    m = min(2, kt - k)
                    load([(lambda s, m=m: raw[:, s, 0:m * D].rearrange("p (k n) -> p k n", k=m), wv[:, k:k + m, :])],
                         i, per)

            def gated_ffn(up, gate, kt):
                def chunk(c, i=None, per=0):
                    for hf in range(2):
                        load([rows_of(up[0], hf, c(up[1]), 256, 0, W), rows_of(gate[0], hf, c(gate[1]), 256, 256, W)],
                             i, per)
                n = kt // 2
                chunk(lambda o: slice(o, o + 256))
                with sp.Fori(0, (n - 2) // 3) as i:
                    for j in range(1, 4):
                        chunk(lambda o: bass.ds(i * 768 + (o + 256 * j), 256), i, 6)
                pos[0] += 6 * ((n - 2) // 3 - 1)
                chunk(lambda o: slice(o + (n - 1) * 256, o + n * 256))

            def conv_ffn(layer):
                gated_ffn((f_in[layer], 0), (f_in[layer], FF), FK)
                down(f_down[layer], FK)

            proj(w_in, 2 * D)
            proj(w_out, D)
            conv_ffn(0)
            proj(w_kv, 2 * D)
            proj(w_q, D)
            proj(w_o, D)
            conv_ffn(1)

            def ada(w):
                with sp.Fori(0, 2) as i:
                    for c in range(6):
                        for hf in range(2):
                            load([rows_of(w, hf, bass.ds(i * 3072 + c * W, W), W)], i, 12)
                pos[0] += 12
            ada(e_ada)
            proj(e_in, E_IN)
            proj(e_out, D)
            gated_ffn((e_up, 0), (e_gate, 0), FK)
            down(e_down, FK)
            ada(o_ada)
            proj(o_in, O_IN)
            proj(o_out, D)
            assert pos[0] == AT["moe"]
            ug, uu, ud = (w.rearrange("e d f -> (e d) f") for w in (x_gate, x_up, x_down))

            def expert(i):
                def part(w, r0, nr, c, n, at, width, rows_per):
                    src = w[bass.ds(i * rows_per + r0, nr * P), :].rearrange("(k p) n -> p k n", p=P)[:, :, c:c + n]
                    return (lambda s: raw[:, s, 0:nr * width].rearrange("p (k n) -> p k n", k=nr)[:, :, at:at + n], src)
                for c in range(0, FE, 256):
                    m = min(256, FE - c)
                    for hf in range(2):
                        load([part(uu, hf * 4 * P, 4, c, m, 0, 2 * m, D), part(ug, hf * 4 * P, 4, c, m, m, 2 * m, D)],
                             i, EXP)
                for k in range(0, FE // P, 2):
                    m = min(2, FE // P - k)
                    load([part(ud, k * P, m, 0, D, 0, D, FE)], i, EXP)
                pos[0] -= EXP

            with sp.Fori(0, NE) as i:
                expert(i)
            pos[0] += EXP * NE
            assert pos[0] == AT["spare"]
            for hf in range(2):
                load([rows_of(x_up[0], hf, slice(0, 256), 256, 0, W), rows_of(x_gate[0], hf, slice(0, 256), 256, 256, W)])
            assert pos[0] == AT["more"]
            sp.wait_ge(sem("counted"), 1)
            with sp.Fori(0, NE) as i:
                n = sp.value_load(count[0:1, bass.ds(i, 1)])
                with sp.If(n > P):
                    expert(i)
                with sp.Else():
                    for s in range(pos[0], pos[0] + RAW):
                        step = LANDED[s + EXP] - LANDED[s]
                        sp.wait_ge(sem(f"landed{s % RAW}"), i * step + (LANDED[s] - 16 * plan[s][1]))
                        sp.sem_inc(sem(f"landed{s % RAW}"), step)
            sp.wait_ge(sem("y_copied"), 2 * NE + 1)
            sp.wait_ge(sem("y_psum"), 2 * (2 * NE + 1))
            sp.dma_start(TC[:, 0, :], fg_in.to_broadcast([P, D])).then_inc(sem("fg_landed"), 16)
            for t in range(NT):
                sp.wait_ge(sem("y_ready"), t + 1)
                sp.dma_start(out[0, t * P:(t + 1) * P, :], TA[:, t, :]).then_inc(sem("stored"), 16)
            sp.wait_ge(sem("stored"), 16 * NT)

        @block.gpsimd
        def _(g):
            g.memset(ident[:, :], 0.0).then_inc(sem("pool"), 1)
            g.memset(ones[:, :], 1.0).then_inc(sem("pool"), 1)
            g.memset(causal[:, :], 0.0).then_inc(sem("pool"), 1)
            g.memset(window[:, :], 0.0).then_inc(sem("pool"), 1)
            g.iota(iotai[:, :], [[1, P]], base=0, channel_multiplier=0).then_inc(sem("pool"), 1)
            g.wait_ge(sem("pool"), 5)
            g.affine_select(out=ident[:, :], in_=ident[:, :], compare_op=ALU.not_equal, fill=1.0, base=0,
                            pattern=[[-1, P]], channel_multiplier=1).then_inc(sem("consts"), 1)
            g.affine_select(out=tri[:, :], in_=ones[:, :], compare_op=ALU.is_ge, fill=0.0, base=0,
                            pattern=[[1, P]], channel_multiplier=-1).then_inc(sem("consts"), 1)
            g.affine_select(out=causal[:, P:S], in_=causal[:, P:S], compare_op=ALU.is_ge, fill=NEG, base=0,
                            pattern=[[-1, P]], channel_multiplier=1).then_inc(sem("consts"), 1)
            g.affine_select(out=window[:, P:S], in_=window[:, P:S], compare_op=ALU.is_ge, fill=NEG, base=0,
                            pattern=[[-1, P]], channel_multiplier=1).then_inc(sem("consts"), 1)
            g.affine_select(out=window[:, 0:P], in_=window[:, 0:P], compare_op=ALU.is_gt, fill=NEG, base=0,
                            pattern=[[1, P]], channel_multiplier=-1).then_inc(sem("consts"), 1)
            g.wait_ge(sem("h_added"), 4)
            g.dma_start(bias, toep_in).then_inc(sem("toep_landed"), 16)
            g.wait_ge(sem("toep_landed"), 16)
            g.memset(bias[0:DH, :, P + DH:S], NEG).then_inc(sem("bias_ready"), 1)
            g.wait_ge(sem("rope_done"), 1)
            g.memset(sel8, 0.0).then_inc(sem("pool"), 1)
            g.wait_ge(sem("pool"), 6)
            g.affine_select(out=sel8, in_=sel8, compare_op=ALU.not_equal, fill=1.0, base=0,
                            pattern=[[-1, 8], [0, P]], channel_multiplier=1).then_inc(sem("sel_ready"), 1)

        @block.tensor
        def _(pe):
            T = Tally()
            pos = [0]
            late_x = [False]

            def mm3(o, xh, xl, wh, wl, start, stop):
                pe.matmul(o, xh, wh, start=start, stop=False)
                pe.matmul(o, xh, wl, start=False, stop=False)
                return pe.matmul(o, xl, wh, start=False, stop=stop)

            def val(s, i, per):
                return s if i is None else i * per + s

            def proj(pr_, width, tiles=NT, i=None, per=0, back=2):
                if T.n.get("acc", 0) - back > 0:
                    pe.wait_ge(sem("acc_free"), T("acc", back))
                for hf in range(2):
                    s = pos[0]
                    pos[0] += 1
                    if hf and late_x[0]:
                        pe.wait_ge(sem("x_ready"), T.up("x_ready", 2))
                        late_x[0] = False
                    pe.wait_ge(sem("lo_done"), val(s + 1, i, per))
                    wh = whi[:, s % SPL, 0:4 * width].rearrange("p (k n) -> p k n", k=4)
                    wl = wlo[:, s % SPL, 0:4 * width].rearrange("p (k n) -> p k n", k=4)
                    for t in range(tiles):
                        for k in range(4):
                            kk = 4 * hf + k
                            last = mm3(ps[:, 2 * pr_ + t, 0:width], xhi[:, kk, t * P:(t + 1) * P],
                                       xlo[:, kk, t * P:(t + 1) * P], wh[:, k, :], wl[:, k, :],
                                       kk == 0, kk == KT - 1)
                    last.then_inc(sem("w_used"), 1)
                T.up("acc")

            def down(kt, late=None):
                pe.wait_ge(sem("acc_free"), T("acc"))
                for j in range((kt + 1) // 2):
                    if j == 2:
                        late()
                    s = pos[0]
                    pos[0] += 1
                    pe.wait_ge(sem("a_ready"), T.up("a_ready"))
                    pe.wait_ge(sem("lo_done"), s + 1)
                    for t in range(NT):
                        for k in range(2 * j, min(2 * j + 2, kt)):
                            o = (k - 2 * j) * D
                            for n in range(2):
                                a, b = o + n * W, o + (n + 1) * W
                                last = mm3(ps[:, 2 * n + t, :], ahi[:, k, t * P:(t + 1) * P],
                                           alo[:, k, t * P:(t + 1) * P], whi[:, s % SPL, a:b], wlo[:, s % SPL, a:b],
                                           k == 0, k == kt - 1)
                    last.then_inc(sem("w_used"), 1)
                T.up("acc", 2)

            def tail(src, wait=None):
                pe.wait_ge(sem("tr_free"), T("tr"))
                for t in range(NT):
                    if t and wait:
                        wait()
                    for k in range(4):
                        last = pe.transpose(trb(k // 2)[:, k % 2, t * P:(t + 1) * P], src[:, t, k * P:(k + 1) * P], ident[:, :])
                        if t and k % 2:
                            last.then_inc(sem("tr"), 1)
                            T.up("tr")
                for r in range(2):
                    pe.wait_ge(sem("tr_free"), T("tr", 1))
                    for t in range(NT):
                        for k in range(2):
                            kk = 4 + 2 * r + k
                            last = pe.transpose(trb(r)[:, k, t * P:(t + 1) * P], src[:, t, kk * P:(kk + 1) * P], ident[:, :])
                    last.then_inc(sem("tr"), 1)
                    T.up("tr")

            def rounds(srcs):
                for r in range(0, len(srcs), 2):
                    if T.n.get("tr", 0) - (r > 0) > 0:
                        pe.wait_ge(sem("tr_free"), T("tr", 1 if r else 0))
                    for k in range(r, min(r + 2, len(srcs))):
                        for t in range(NT):
                            last = pe.transpose(trb(r // 2 % 2)[:, k - r, t * P:(t + 1) * P], srcs[k](t), ident[:, :])
                    last.then_inc(sem("tr"), 1)
                    T.up("tr")

            def norm_tail(src):
                pe.wait_ge(sem("xn"), T.up("xn"))
                tail(src, lambda: pe.wait_ge(sem("xn"), T.up("xn")))

            def x_ready():
                pe.wait_ge(sem("x_ready"), T.up("x_ready", 2))
                late_x[0] = True

            def transposes(n, i=None):
                pe.wait_ge(sem("tok_ready"), T.up("tok_ready"))
                pe.wait_ge(sem("tr_free"), T("tr"))
                for f in range(n):
                    for t in range(NT):
                        last = pe.transpose(ps[:, 6 + f // 2, (f % 2) * S + t * P:(f % 2) * S + (t + 1) * P],
                                            ab[:, t, f * P:(f + 1) * P], ident[:, :])
                last.then_inc(sem("tr"), 1)
                T.up("tr")

            def gated_ffn(n_tr):
                n = FK // 2
                x_ready()
                proj(2, W, back=0)
                turns = (n - 2) // 3
                with pe.Fori(0, turns) as i:
                    T.loop(i, acc=3, tok_ready=3, tr=3)
                    for j in range(3):
                        proj(j, W, i=i, per=6)
                        transposes(n_tr)
                    T.end(turns)
                pos[0] += 6 * (turns - 1)
                proj(0, W)
                transposes(n_tr)
                down(FK, lambda: transposes(n_tr))

            def attention(units):
                for a in ("s", "n", "pt", "pv", "oc"):
                    T.n.setdefault("att_" + a, 0)
                b = {a: T.n["att_" + a] for a in ("s", "n", "pt", "pv", "oc")}
                U = [(a, t) for a in units for t in range(NT)]

                def scores(u):
                    a, t = U[u]
                    nk = (t + 1) * P
                    if u >= 2:
                        pe.wait_ge(sem("att_a"), b["s"] + u - 1)
                    r0 = a["h"] % 2 * DH
                    o = ps[:, u % 2, 0:nk]
                    m = pe.matmul(o, qT[r0:r0 + DH, a["q"], t * P:(t + 1) * P], kT[r0:r0 + DH, a["k"], 0:nk],
                                  start=True, stop=a["mask"] != "fox")
                    if a["mask"] == "fox":
                        m = pe.matmul(o, sel8[:, a["h"], :], ncT[:, 0:nk], start=False, stop=True)
                    m.then_inc(sem("att_s"), 1)

                def turn(u):
                    a, t = U[u]
                    pe.wait_ge(sem("att_n"), b["n"] + u + 1)
                    if u >= 2:
                        pe.wait_ge(sem("att_c"), b["pt"] + u - 1)
                    for kk in range(t + 1):
                        m = pe.transpose(ps[:, 6 + u % 2, kk * P:(kk + 1) * P], pr[:, u % 2, kk * P:(kk + 1) * P],
                                         ident[:, :])
                    m.then_inc(sem("att_pt"), 1)

                def values(u):
                    a, t = U[u]
                    pe.wait_ge(sem("att_c"), b["pt"] + u + 1)
                    p_ = a["h"] // 2
                    if u % 4 == 0 and p_ >= 2:
                        pe.wait_ge(sem("att_o"), b["oc"] + p_ - 1)
                    r0 = a["h"] % 2 * DH
                    for kk in range(t + 1):
                        m = pe.matmul(ps[r0:r0 + DH, 2 + p_ % 2, t * P:(t + 1) * P], v_of(a, kk),
                                      pT[:, u % 2, kk * P:(kk + 1) * P], start=kk == 0, stop=kk == t)
                    m.then_inc(sem("att_pv"), 1)

                n = len(U)
                for i in range(n + 3):
                    if i < n:
                        scores(i)
                    if 0 <= i - 2 < n:
                        turn(i - 2)
                    if 0 <= i - 3 < n:
                        values(i - 3)
                for a in ("s", "n", "pt", "pv"):
                    T.up("att_" + a, n)
                T.up("att_oc", NH // 2)
                pe.wait_ge(sem("att_o"), T("att_oc"))

            T.up("mod_taken")
            pe.wait_ge(sem("consts"), 1)
            pe.wait_ge(sem("ws_landed"), 16)
            for g in range(KT):
                m = pe.transpose(ps[:, g // 4, (g % 4) * P:(g % 4 + 1) * P], ws[:, g, :], ident[:, :])
            m.then_inc(sem("wsT_psum"), 1)
            norm_tail(TA)
            x_ready()
            pe.wait_ge(sem("wsT_ready"), 1)
            for c in range(4):
                proj(c % 3, W)
            pe.wait_ge(sem("vn_ready"), NT)
            pe.wait_ge(sem("wsT_ready"), 2)
            pe.wait_ge(sem("acc_free"), 4)
            for g in range(KT):
                pe.matmul(ps[:, g // 2, (g % 2) * S:(g % 2 + 1) * S].rearrange("p (t c) -> p t c", t=NT),
                          wsT[:, g, :], TB[:, :, g * P:(g + 1) * P], start=True, stop=True).then_inc(sem("spatial"), 1)
            pe.wait_ge(sem("gz_ready"), KT)
            tail(TA)
            x_ready()
            for c in range(2):
                proj(c, W)
            norm_tail(TA)
            gated_ffn(4)
            norm_tail(TA)
            x_ready()
            for c in range(4):
                proj(c % 3, W, back=2 if c else 0)
            tail(TA)
            x_ready()
            for c in range(2):
                proj(1 + c, W)
            pe.wait_ge(sem("acc_free"), T("acc"))
            rounds([(lambda t, k=k: TB[:, t, k * P:(k + 1) * P]) for k in range(KT)])
            rounds([(lambda t, k=k: TA[:, t, k * P:(k + 1) * P]) for k in range(KT)])
            pe.wait_ge(sem("tr_free"), T("tr"))
            attention(CHUNKED)
            for c in range(2):
                proj(c, W, back=c)
            norm_tail(TA)
            gated_ffn(4)

            def ada():
                pe.wait_ge(sem("c_ready"), T.up("c_ready"))
                with pe.Fori(0, 2) as i:
                    T.loop(i, acc=6, mod_taken=1)
                    for c in range(6):
                        proj(c % 3, W, tiles=1, i=i, per=12, back=0 if c == 0 else 2)
                        if c == 0:
                            pe.wait_ge(sem("mod_taken"), T("mod_taken"))
                        if 1 <= c <= 4:
                            pe.wait_ge(sem("acc_free"), T("acc", 1))
                            for j in range(4):
                                n = (c - 1) * 4 + j
                                m = pe.matmul(ps[:, 6, n:n + 1], modrow[:, n * P:(n + 1) * P], ident[0:1, 0:1],
                                              start=True, stop=True)
                    m.then_inc(sem("mod_psum"), 1)
                    T.up("mod_taken")
                    T.end(2)
                pos[0] += 12
                pe.wait_ge(sem("mod_taken"), T("mod_taken"))

            def turned(srcs):
                rounds(srcs)

            ada()
            norm_tail(TA)
            x_ready()
            for n, w in enumerate([W] * 4 + [E_IN - 4 * W]):
                proj(n % 3, w, back=0 if n == 0 else 2)
            pe.wait_ge(sem("acc_free"), T("acc"))
            pe.wait_ge(sem("logf"), 1)
            lgt = lgf[:, 4]
            pe.matmul(ps[:, 0, 0:8], tri[:, :], lgt[:, 0, :], start=True, stop=True)
            pe.matmul(ps[:, 0, 8:16], ones[:, :], lgt[:, 0, :], start=True, stop=False)
            pe.matmul(ps[:, 0, 8:16], tri[:, :], lgt[:, 1, :], start=False, stop=True)
            pe.matmul(ps[0:8, 1, 0:P], lgt[:, 0, :], tri[:, :], start=True, stop=True)
            pe.matmul(ps[0:8, 1, P:S], lgt[:, 0, :], ones[:, :], start=True, stop=False)
            pe.matmul(ps[0:8, 1, P:S], lgt[:, 1, :], tri[:, :], start=False, stop=True).then_inc(sem("cum_psum"), 1)
            pe.wait_ge(sem("kd_ready"), 1)
            tile_of = lambda c: (lambda t: te[:, t, c:c + P])
            rounds([tile_of(n * P) for n in range(4)] + [tile_of(1544 + n * P) for n in range(4)])
            rounds([tile_of(512 + n * P) for n in range(4)]
                   + [(lambda t, j=j: kd[:, t, j].rearrange("p c d -> p (c d)")) for j in range(2)])
            pe.wait_ge(sem("tr_free"), T("tr"))
            pe.wait_ge(sem("cum_ready"), 2)
            pe.wait_ge(sem("sel_ready"), 1)
            attention(EVEN)
            for c in range(2):
                proj(c, W, back=c)
            norm_tail(TA)
            gated_ffn(2)
            ada()
            norm_tail(TA)
            x_ready()
            for n, w in enumerate([W] * 4 + [O_IN - 4 * W]):
                proj(n % 3, w, back=0 if n == 0 else 2)
            pe.wait_ge(sem("acc_free"), T("acc"))
            pe.wait_ge(sem("kd_ready"), 2)
            tile_of = lambda c: (lambda t: to[:, t, c:c + P])
            rounds([tile_of(1536 + n * P) for n in range(4)] + [lambda t: ikd[:, t].rearrange("p c d -> p (c d)")])
            pe.wait_ge(sem("tr_free"), T("tr"))
            for u in range(16):
                t, ih = u // 8, u % 8
                if u >= 4:
                    pe.wait_ge(sem("ix_read"), u - 3)
                r0 = ih % 2 * DH
                pe.matmul(ps[:, u % 4, 0:(t + 1) * P], iqT[r0:r0 + DH, ih // 2, t * P:(t + 1) * P],
                          ikT[r0:r0 + DH, 0:(t + 1) * P], start=True, stop=True).then_inc(sem("ix_psum"), 1)
            rounds([tile_of(n * P) for n in range(8)])
            rounds([(lambda t, j=j: kd[:, t, j].rearrange("p c d -> p (c d)")) for j in range(4)])
            pe.wait_ge(sem("tr_free"), T("tr"))
            pe.wait_ge(sem("ix_read"), 16)
            attention(ODD)
            for c in range(2):
                proj(c, W, back=c)
            norm_tail(TA)
            pe.wait_ge(sem("x_ready"), T.up("x_ready", 4))
            pe.wait_ge(sem("acc_free"), T("acc"))
            for t in range(NT):
                for k in range(KT):
                    m = pe.matmul(ps[:, 5, t * NE:(t + 1) * NE], xT_c[:, k, t * P:(t + 1) * P], rw[:, k, :],
                                  start=k == 0, stop=k == KT - 1)
            m.then_inc(sem("router"), 1)
            pe.wait_ge(sem("logits_taken"), 1)
            pe.wait_ge(sem("member"), 1)
            pe.matmul(ps[:, 5, 32:32 + NE], tri[:, :], member[:, 0, :], start=True, stop=True)
            pe.matmul(ps[:, 5, 40:40 + NE], ones[:, :], member[:, 0, :], start=True, stop=False)
            pe.matmul(ps[:, 5, 40:40 + NE], tri[:, :], member[:, 1, :], start=False, stop=True)
            pe.matmul(ps[:, 5, 48:48 + NE], ones[:, :], member[:, 0, :], start=True, stop=False)
            pe.matmul(ps[:, 5, 48:48 + NE], ones[:, :], member[:, 1, :], start=False, stop=True).then_inc(sem("ranks"), 1)
            T.n.update(x_acc=0, x_tr=0, x_g=0, x_y=0, x_s=0, x_a=0)

            def gather():
                pe.wait_ge(sem("places"), T.up("x_g"))
                pe.wait_ge(sem("g_taken"), T("x_g"))
                for b in range(2):
                    for k in range(4):
                        for t in range(NT):
                            m = pe.matmul(ps[:, 5 + 2 * b, k * P:(k + 1) * P], TA[:, t, (4 * b + k) * P:(4 * b + k + 1) * P],
                                          G[:, t, :], start=t == 0, stop=t == NT - 1)
                    m.then_inc(sem("g_psum"), 1)

            def turn_places():
                pe.wait_ge(sem("x_tr_free"), T("x_tr", -1))
                for t in range(NT):
                    m = pe.transpose(ps[:, 6, t * P:(t + 1) * P], G[:, t, :], ident[:, :])
                m.then_inc(sem("x_tr"), 1)
                T.up("x_tr")

            def scatter():
                pe.wait_ge(sem("y_copied"), T.up("x_y"))
                for n in range(2):
                    for t in range(NT):
                        b = (5, 7, 3, 4)[2 * n + t]
                        m = pe.matmul(ps[:, b, :], GT[:, t, :], ysb[:, n * W:(n + 1) * W], start=True, stop=True)
                    m.then_inc(sem("y_psum"), 1)

            def hidden(j, i):
                w = W if j < 5 else 256
                for hf in range(2):
                    s = pos[0]
                    pos[0] += 1
                    pe.wait_ge(sem("lo_done"), i * EXP + (s + 1))
                    wh = whi[:, s % SPL, 0:4 * w].rearrange("p (k n) -> p k n", k=4)
                    wl = wlo[:, s % SPL, 0:4 * w].rearrange("p (k n) -> p k n", k=4)
                    for k in range(4):
                        kk = 4 * hf + k
                        m = mm3(ps[:, (2, 0, 1)[j % 3], 0:w], xhi[:, kk, 0:P], xlo[:, kk, 0:P], wh[:, k, :], wl[:, k, :],
                                kk == 0, kk == KT - 1)
                    m.then_inc(sem("w_used"), 1)

            def turn(j):
                pe.wait_ge(sem("x_tok"), T.up("x_acc") + 1)
                pe.wait_ge(sem("x_tr_free"), T("x_tr", -1))
                for f in range(2 if j < 5 else 1):
                    m = pe.transpose(ps[:, 6, f * P:(f + 1) * P], abx[:, j % 2, f * P:(f + 1) * P], ident[:, :])
                m.then_inc(sem("x_tr"), 1)
                T.up("x_tr")

            def out_of(i):
                for j in range(6):
                    s = pos[0]
                    pos[0] += 1
                    pe.wait_ge(sem("x_a"), T.up("x_a"))
                    pe.wait_ge(sem("lo_done"), i * EXP + (s + 1))
                    for k in range(2 * j, min(2 * j + 2, FE // P)):
                        for n in range(2):
                            a = (k - 2 * j) * D + n * W
                            m = mm3(ps[:, 3 + n, :], ahi[:, k, 0:P], alo[:, k, 0:P], whi[:, s % SPL, a:a + W],
                                    wlo[:, s % SPL, a:a + W], k == 0, k == FE // P - 1)
                    m.then_inc(sem("w_used"), 1)

            gather()
            with pe.Fori(0, NE) as i:
                T.loop(i, x_acc=6, x_tr=7, x_g=1, x_y=1, x_a=6, x_s=1)
                pe.wait_ge(sem("xg_ready"), T.up("x_s"))
                hidden(0, i)
                scatter()
                hidden(1, i)
                turn(0)
                turn_places()
                for j in range(2, 6):
                    hidden(j, i)
                    if j == 5:
                        pe.wait_ge(sem("y_added"), T("x_y"))
                        gather()
                    turn(j - 1)
                turn(5)
                out_of(i)
                T.end(NE)
            pos[0] += EXP * (NE - 1)
            scatter()
            pe.wait_ge(sem("lo_done"), AT["more"])
            pe.drain()
            pe.sem_inc(sem("w_used"), AHEAD)
            pos[0] += AHEAD
            pe.wait_ge(sem("counted"), 1)
            with pe.Fori(0, NE) as i:
                T.loop(i, x_acc=6, x_tr=7, x_g=1, x_y=1, x_a=6, x_s=1)
                n = pe.value_load(count[0:1, bass.ds(i, 1)])
                with pe.If(n > P):
                    pe.wait_ge(sem("y_added"), T("x_y"))
                    gather()
                    turn_places()
                    pe.wait_ge(sem("xg_ready"), T.up("x_s"))
                    for j in range(6):
                        hidden(j, i)
                        if j:
                            turn(j - 1)
                    turn(5)
                    out_of(i)
                    scatter()
                with pe.Else():
                    pe.drain()
                    for name, k in (("g_psum", 2), ("x_tr", 7), ("w_used", EXP), ("y_psum", 2)):
                        pe.sem_inc(sem(name), k)
                T.end(NE)

        @block.scalar
        def _(act):
            T = Tally()
            act.dma_start(ws, ws_in.rearrange("o g i j -> i (o g) j")).then_inc(sem("ws_landed"), 16)
            act.dma_start(gates[:, 0, :], fg1_in.to_broadcast([P, D])).then_inc(sem("fg1_landed"), 16)
            act.dma_start(vg, vg_in.to_broadcast([P, D])).then_inc(sem("consts_landed"), 16)
            act.dma_start(rows[:, :], rows_in.to_broadcast([P, R_END])).then_inc(sem("consts_landed"), 16)
            act.dma_start(posi[:, :], pos_in).then_inc(sem("consts_landed"), 16)
            act.dma_start(rw[:, :, :], rw_in.rearrange("(k p) e -> p k e", p=P)).then_inc(sem("consts_landed"), 16)
            pos = [0]
            used = [0]

            top = [AT["end"]]

            def split(n, i=None, per=0):
                while pos[0] < min(n, top[0]):
                    s = pos[0]
                    pos[0] += 1
                    w = plan[s][0]
                    step = LANDED[s + per] - LANDED[s] if i is not None else 0
                    act.wait_ge(sem(f"landed{s % RAW}"), LANDED[s] if i is None else i * step + LANDED[s])
                    if s >= SPL:
                        act.wait_ge(sem("w_used"), s - SPL + 1 if i is None else i * per + (s - SPL + 1))
                    act.activation(whi[:, s % SPL, 0:w], raw[:, s % RAW, 0:w], ACT.Copy).then_inc(sem("hi_done"), 1)

            def chunk(i=None, per=0):
                used[0] += 2
                split(used[0] + AHEAD, i, per)
                act.wait_ge(sem("w_used"), used[0] if i is None else i * per + used[0])

            def stats(src, added=True):
                for t in range(NT):
                    if added:
                        act.wait_ge(sem("h_added"), T.up("h_added"))
                    if t:
                        act.wait_ge(sem("sq"), T("sq"))
                    T.up("sq")
                    act.activation(ps[:, 6:8, :], src[:, t, :].rearrange("p (a b) -> p a b", a=2),
                                   ACT.Square, accum_out=st[:, t:t + 1]).then_inc(sem("sq"), 1)
                for t in range(NT):
                    act.wait_ge(sem("ms"), T.up("ms"))
                    act.activation(st[:, 4 + t:5 + t], st[:, 2 + t:3 + t], ACT.Sqrt).then_inc(sem("rms"), 1)

            def tail(dst, scale=None, shift=None):
                for r in range(4):
                    act.wait_ge(sem("tr"), T.up("tr"))
                    if scale is None:
                        act.activation(dst[:, 2 * r:2 * r + 2, :], trb(r % 2), ACT.Copy).then_inc(sem("tr_free"), 1)
                        continue
                    for j in range(2):
                        k = 2 * r + j
                        kw = {} if shift is None else dict(bias=shift[:, k:k + 1])
                        m = act.activation(dst[:, k, :], trb(r % 2)[:, j, :], ACT.Identity, scale=scale[:, k:k + 1], **kw)
                    m.then_inc(sem("tr_free"), 1)

            def copies(dsts, scale=1.0):
                for r, d in enumerate(dsts):
                    act.wait_ge(sem("tr"), T.up("tr"))
                    src = trb(r % 2) if d.shape[1] == 2 else trb(r % 2)[:, 0:1, :]
                    act.activation(d, src, ACT.Copy, scale=scale).then_inc(sem("tr_free"), 1)

            def take(n, dst, func=ACT.Copy, w=W, scale=1.0):
                chunk()
                act.activation(dst, pair(n, w), func, scale=scale).then_inc(sem("acc_free"), 1)

            def residual():
                for _ in range(2):
                    used[0] += 2
                    split(used[0] + AHEAD)
                T.up("acc", 2)

            def down(kt, i=None, per=0):
                used[0] += (kt + 1) // 2
                split(used[0] + AHEAD, i, per)

            def conv_ffn(layer):
                n = FK // 2
                cw = C_CW + layer * 3 * 2 * FK
                cb = C_CB + layer * 2 * FK

                def evac(pr_, i=None, first=False):
                    chunk(i, 6)
                    if not first:
                        act.wait_ge(sem("tr"), T("tr", -1))
                    act.activation(ab, pair(pr_), ACT.Copy).then_inc(sem("tok_ready"), 1)

                def convolve(j, i=None):
                    act.wait_ge(sem("tr"), T.up("tr"))
                    act.wait_ge(sem("conv_used"), T("conv_used"))
                    for f in range(4):
                        c = (f % 2) + (f // 2) * FK + 2 * j
                        if i is None:
                            sc, bi = cols[:, cw + 4 * FK + c:cw + 4 * FK + c + 1], cols[:, cb + c:cb + c + 1]
                        else:
                            sc, bi = cols[:, bass.ds(i * 6 + (cw + 4 * FK + c), 1)], cols[:, bass.ds(i * 6 + (cb + c), 1)]
                        m = act.activation(conv[:, f, :], ps[:, 6 + f // 2, (f % 2) * S:(f % 2 + 1) * S], ACT.Identity,
                                           scale=sc, bias=bi)
                    m.then_inc(sem("conv_a"), 1)
                    act.wait_ge(sem("conv_b"), T.up("conv_b"))
                    act.activation(sg, conv[:, 2:4, :], ACT.Silu).then_inc(sem("silu"), 1)
                    T.up("conv_used")

                evac(2, first=True)
                turns = (n - 2) // 3
                with act.Fori(0, turns) as i:
                    T.loop(i, tr=3, conv_b=3, conv_used=3)
                    for j in range(3):
                        evac(j, i)
                        convolve(j, i)
                    T.end(turns)
                pos[0] += 6 * (turns - 1)
                used[0] += 6 * (turns - 1)
                evac(0)
                convolve(n - 2)
                split(used[0] + 4)
                convolve(n - 1)
                down(FK)

            def evac_gated(pr_, m, i=None, per=0):
                chunk(i, per)
                if T.n.get("sg_used", 0):
                    act.wait_ge(sem("sg_used"), T("sg_used"))
                act.activation(sg[:, :, 0:m], pair(pr_, 2 * m)[:, :, m:2 * m], ACT.Silu).then_inc(sem("silu"), 1)
                T.up("sg_used")

            def turned_gated(f):
                return f

            def gated_ffn():
                n = FK // 2
                evac_gated(2, 256)
                turns = (n - 2) // 3
                with act.Fori(0, turns) as i:
                    T.loop(i, sg_used=3)
                    for j in range(3):
                        evac_gated(j, 256, i, 6)
                    T.end(turns)
                pos[0] += 6 * (turns - 1)
                used[0] += 6 * (turns - 1)
                evac_gated(0, 256)
                down(FK)
                T.up("tr", n)

            def attention(units):
                U = [(a, t) for a in units for t in range(NT)]
                b = T.n.get("att", 0)

                def exps(u):
                    a, t = U[u]
                    act.wait_ge(sem("att_m"), b + u + 1)
                    if u >= 2:
                        act.wait_ge(sem("att_pt"), b + u - 1)
                    nk = (t + 1) * P
                    m = act.activation(pr[:, u % 2, 0:nk], sm[:, u % 2, 0:nk], ACT.Exp, bias=st[:, 8 + u % 2:9 + u % 2],
                                       accum_out=st[:, 10 + u % 2:11 + u % 2])
                    if a["mask"] == "swa":
                        c = R_SK + a["h"] - 8
                        m = act.activation(st[:, 12 + u % 2:13 + u % 2], rows[:, c:c + 1], ACT.Exp,
                                           bias=st[:, 8 + u % 2:9 + u % 2])
                    m.then_inc(sem("att_e"), 1)

                def copy(u):
                    a, t = U[u]
                    act.wait_ge(sem("att_pt"), b + u + 1)
                    if u >= 2:
                        act.wait_ge(sem("att_pv"), b + u - 1)
                    nk = (t + 1) * P
                    act.activation(pT[:, u % 2, 0:nk], ps[:, 6 + u % 2, 0:nk], ACT.Copy).then_inc(sem("att_c"), 1)

                n = len(U)
                for i in range(n + 2):
                    if i < n:
                        exps(i)
                    if 0 <= i - 2 < n:
                        copy(i - 2)
                T.up("att", n)

            T.up("conv_used")
            split(2)
            act.wait_ge(sem("x_landed"), 16)
            stats(h, False)
            act.wait_ge(sem("wsT_psum"), 1)
            act.activation(wsT.rearrange("p (b g) i -> p b (g i)", b=2), ps[:, 0:2, :], ACT.Copy).then_inc(sem("wsT_ready"), 1)
            act.wait_ge(sem("consts_landed"), 16 * 5)
            tail(xT_c, cols[:, C_GA:C_GA + KT])
            for n in range(4):
                dst = (TA if n < 2 else TB)[:, :, (n % 2) * W:(n % 2 + 1) * W]
                take(n % 3, dst, ACT.Gelu_apprx_tanh)
                T.up("acc")
            act.wait_ge(sem("acc_free"), 4)
            stats(TB, False)
            tail(xT_c)
            residual()
            stats(h)
            tail(xT_c, cols[:, C_GF0:C_GF0 + KT])
            conv_ffn(0)
            stats(h)
            tail(xT_c, cols[:, C_GKV:C_GKV + KT])
            for n in range(4):
                dst = (TB if n < 2 else TC)[:, :, (n % 2) * W:(n % 2 + 1) * W]
                take(n % 3, dst)
            tail(xT_b, cols[:, C_GB:C_GB + KT])
            for n in range(2):
                take(1 + n, TA[:, :, n * W:(n + 1) * W])
            copies([kT[:, 2 * r:2 * r + 2, :] for r in range(4)])
            copies([qT[:, 2 * r:2 * r + 2, :] for r in range(4)], scale=DH ** -0.5)
            attention(CHUNKED)
            residual()
            stats(h)
            tail(xT_c, cols[:, C_GF1:C_GF1 + KT])
            conv_ffn(1)
            stats(h)

            def ada(layer, gains):
                act.wait_ge(sem("xlo_free"), T.up("xlo_free"))
                act.activation(cs[:, :], cols[:, C_C:C_C + KT], ACT.Silu).then_inc(sem("cs"), 1)
                act.dma_start(adab, adab_in[layer:layer + 1, :].to_broadcast([P, 2 * D]).rearrange("p (m d) -> p m d", m=2))\
                    .then_inc(sem("adab_landed"), 16)
                with act.Fori(0, 2) as i:
                    for c in range(6):
                        chunk(i, 12)
                        if c < 4:
                            act.activation(modrow[:, c * W:(c + 1) * W], ps[0:1, 2 * (c % 3), :], ACT.Copy)\
                                .then_inc(sem("acc_free"), 1)
                pos[0] += 12
                used[0] += 12

            act.wait_ge(sem("angle"), 1)
            act.activation(sinT[:, :, :].rearrange("p t f -> p (t f)"), rot[:, 1, :], ACT.Sin).then_inc(sem("tables"), 1)
            act.activation(cosT[:, :, :].rearrange("p t f -> p (t f)"), rot[:, 3, :], ACT.Sin).then_inc(sem("tables"), 1)
            ada(0, None)
            act.wait_ge(sem("mod_taken"), 3)
            act.wait_ge(sem("h_normed"), NT)
            stats(h, False)
            tail(xT_c, scl[:, 0, :], shf[:, 0, :])
            for n, w in enumerate([W] * 4 + [E_IN - 4 * W]):
                take(n % 3, te[:, :, n * W:n * W + w], w=w)
            act.wait_ge(sem("lgf"), 1)
            act.activation(lgf[:, 1], lgf[:, 2], ACT.Exp, scale=-1.0).then_inc(sem("lgf_act"), 1)
            act.wait_ge(sem("lgf"), 2)
            act.activation(lgf[:, 3], lgf[:, 2], ACT.Ln).then_inc(sem("lgf_act"), 1)
            act.wait_ge(sem("rope_done"), 1)
            for c in range(2):
                m = act.activation(kd[:, :, 0:2, c, :], te[:, :, 2056:2184].rearrange("p t (j d) -> p t j d", j=2), ACT.Copy)
            m.then_inc(sem("kd_ready"), 1)
            copies([qT[:, 2 * r:2 * r + 2, :] for r in range(4)], scale=DH ** -0.5)
            copies([kT[:, 2 * r:2 * r + 2, :] for r in range(3)])
            attention(EVEN)
            residual()
            stats(h)
            tail(xT_c, scl[:, 1, :], shf[:, 1, :])
            gated_ffn()
            ada(1, None)
            act.wait_ge(sem("mod_taken"), 5)
            stats(h)
            tail(xT_c, scl[:, 0, :], shf[:, 0, :])
            for n, w in enumerate([W] * 4 + [O_IN - 4 * W]):
                take(n % 3, to[:, :, n * W:n * W + w], w=w)
            act.wait_ge(sem("rope_done"), 2)
            for c in range(2):
                act.activation(ikd[:, :, c, :], to[:, :, 2048:2112], ACT.Copy)
                m = act.activation(kd[:, :, :, c, :], to[:, :, 1024:1280].rearrange("p t (j d) -> p t j d", j=4), ACT.Copy)
            m.then_inc(sem("kd_ready"), 1)
            copies([iqT[:, 0:2, :], iqT[:, 2:4, :], ikT.unsqueeze(1)])
            for u in range(16):
                t = u // 8
                act.wait_ge(sem("ix_psum"), u + 1)
                if u >= 2:
                    act.wait_ge(sem("ix_added"), u - 1)
                act.activation(relu[:, u % 2, 0:(t + 1) * P], ps[:, u % 4, 0:(t + 1) * P], ACT.Relu).then_inc(sem("ix_read"), 1)
            copies([qT[:, 2 * r:2 * r + 2, :] for r in range(4)], scale=DH ** -0.5)
            copies([kT[:, 2 * r:2 * r + 2, :] for r in range(2)])
            attention(ODD)
            residual()
            stats(h)
            tail(xT_c, scl[:, 1, :], shf[:, 1, :])
            act.wait_ge(sem("g2"), 1)
            act.activation(g2[:, :, 1], g2[:, :, 0], ACT.Exp).then_inc(sem("g2_act"), 1)
            T.n.update(x_tr=0, x_g=0, x_y=0, x_sg=0)

            def take_gathered():
                for b in range(2):
                    act.wait_ge(sem("g_psum"), T.up("x_g"))
                    for k in range(4):
                        kk = 4 * b + k
                        m = act.activation(xg[:, kk, :], ps[:, 5 + 2 * b, k * P:(k + 1) * P], ACT.Identity,
                                           scale=scl[:, 1, kk:kk + 1], bias=shf[:, 1, kk:kk + 1])
                    m.then_inc(sem("xg"), 1)

            def silu(j, i):
                m = 256 if j < 5 else P
                used[0] += 2
                split(used[0] + AHEAD, i, EXP)
                act.wait_ge(sem("w_used"), i * EXP + used[0])
                act.wait_ge(sem("x_tok"), T("x_sg", -1))
                act.activation(sgx[:, 0:m], ps[:, (2, 0, 1)[j % 3], m:2 * m], ACT.Silu).then_inc(sem("x_silu"), 1)
                T.up("x_sg")

            def places():
                act.wait_ge(sem("x_tr"), T.up("x_tr"))
                act.activation(GT, ps[:, 6, 0:S].rearrange("p (t i) -> p t i", t=NT), ACT.Copy).then_inc(sem("x_tr_free"), 1)

            def hi_of(j):
                f = 2 if j < 5 else 1
                act.wait_ge(sem("x_tr"), T.up("x_tr"))
                act.activation(ahi[:, 2 * j:2 * j + f, 0:P], ps[:, 6, 0:f * P].rearrange("p (f s) -> p f s", f=f), ACT.Copy)\
                    .then_inc(sem("x_hi"), 1)

            def output(i):
                used[0] += 6
                split(used[0] + AHEAD, i, EXP)
                act.wait_ge(sem("w_used"), i * EXP + used[0])
                act.wait_ge(sem("y_psum"), T("x_y", -2))
                act.activation(ysb.rearrange("p (n c) -> p n c", n=2), ps[:, 3:5, :], ACT.Copy).then_inc(sem("y_copied"), 1)
                T.up("x_y", 2)

            take_gathered()
            with act.Fori(0, NE) as i:
                T.loop(i, x_tr=7, x_g=2, x_y=2, x_sg=6)
                for j in range(6):
                    silu(j, i)
                    if j > 0:
                        hi_of(j - 1)
                    if j == 1:
                        places()
                take_gathered()
                hi_of(5)
                output(i)
                T.end(NE)
            pos[0] += EXP * (NE - 1)
            used[0] += EXP * (NE - 1) + AHEAD
            assert pos[0] == used[0] == AT["more"]
            act.wait_ge(sem("counted"), 1)
            with act.Fori(0, NE) as i:
                T.loop(i, x_tr=7, x_g=2, x_y=2, x_sg=6)
                n = act.value_load(count[0:1, bass.ds(i, 1)])
                with act.If(n > P):
                    top[0] = used[0] + EXP
                    take_gathered()
                    places()
                    for j in range(6):
                        silu(j, i)
                        if j > 0:
                            hi_of(j - 1)
                    hi_of(5)
                    output(i)
                with act.Else():
                    act.drain()
                    for name, k in (("xg", 2), ("hi_done", EXP), ("x_silu", 6), ("x_tr_free", 1), ("x_hi", 6), ("y_copied", 1)):
                        act.sem_inc(sem(name), k)
                T.end(NE)
            stats(h)

        @block.vector
        def _(dve):
            T = Tally()
            pos = [0]
            used = [0]

            def link(ins):
                ins.then_inc(sem("dve"), 1)
                dve.wait_ge(sem("dve"), T.up("dve"))

            top = [AT["end"]]

            def split(n, i=None, per=0):
                while pos[0] < min(n, top[0]):
                    s = pos[0]
                    pos[0] += 1
                    w = plan[s][0]
                    dve.wait_ge(sem("hi_done"), s + 1 if i is None else i * per + (s + 1))
                    dve.tensor_tensor(wlo[:, s % SPL, 0:w], raw[:, s % RAW, 0:w], whi[:, s % SPL, 0:w].bitcast(F32),
                                      ALU.subtract).then_inc(sem("lo_done"), 1)

            def chunk(i=None, per=0, wait=True):
                used[0] += 2
                split(used[0] + AHEAD, i, per)
                if wait:
                    dve.wait_ge(sem("w_used"), used[0] if i is None else i * per + used[0])

            def normalise(src, dst, gain=None, name="xn"):
                for t in range(NT):
                    dve.wait_ge(sem("sq"), T.up("sq"))
                    dve.tensor_scalar(st[:, 2 + t:3 + t], st[:, t:t + 1], 1.0 / D, EPS, ALU.mult, ALU.add).then_inc(sem("ms"), 1)
                for t in range(NT):
                    dve.wait_ge(sem("rms"), T.up("rms"))
                    link(dve.reciprocal(st[:, 6 + t:7 + t], st[:, 4 + t:5 + t]))
                    if gain is None:
                        m = dve.tensor_scalar(dst[:, t, :], src[:, t, :], st[:, 6 + t:7 + t], None, ALU.mult)
                    else:
                        m = dve.scalar_tensor_tensor(dst[:, t, :], src[:, t, :], st[:, 6 + t:7 + t], gain, ALU.mult, ALU.mult)
                    m.then_inc(sem(name), 1)

            def tail(src):
                if used[0]:
                    dve.wait_ge(sem("w_used"), used[0])
                for r in range(4):
                    dve.wait_ge(sem("tr_free"), T.up("tr"))
                    x = src[:, 2 * r:2 * r + 2, :]
                    link(dve.tensor_copy(xhi[:, 2 * r:2 * r + 2, :], x))
                    dve.tensor_tensor(xlo[:, 2 * r:2 * r + 2, :], x, xhi[:, 2 * r:2 * r + 2, :].bitcast(F32), ALU.subtract)\
                        .then_inc(sem("x_ready"), 1)

            def skip(n):
                for _ in range(n):
                    chunk(wait=False)

            def add_h(n, t, gate=None):
                hs = h[:, t, n * W:(n + 1) * W]
                if gate is None:
                    return dve.tensor_tensor(hs, ps[:, 2 * n + t, :], hs, ALU.add)
                tmp = TB[:, t, n * W:(n + 1) * W]
                link(dve.tensor_tensor(tmp, ps[:, 2 * n + t, :], gates[:, gate, n * W:(n + 1) * W], ALU.mult))
                return dve.tensor_tensor(hs, tmp, hs, ALU.add)

            def add_done():
                T.up("acc", 2)
                dve.wait_ge(sem("h_added"), T.up("h_added", NT))
                dve.sem_inc(sem("acc_free"), 2)

            def residual(gate=None):
                for n in range(2):
                    chunk()
                    for t in range(NT):
                        m = add_h(n, t, gate)
                        if n:
                            m.then_inc(sem("h_added"), 1)
                add_done()

            def down(kt, gate=None):
                used[0] += (kt + 1) // 2
                split(used[0] + AHEAD)
                dve.wait_ge(sem("w_used"), used[0])
                for t in range(NT):
                    for n in range(2):
                        m = add_h(n, t, gate)
                    m.then_inc(sem("h_added"), 1)
                add_done()

            def conv_ffn(layer):
                n = FK // 2
                cw = C_CW + layer * 3 * 2 * FK

                def convolve(j, i=None):
                    dve.wait_ge(sem("conv_a"), T.up("conv_a"))
                    for tap, d in ((1, 1), (0, 2)):
                        for f in range(4):
                            c = cw + tap * 2 * FK + (f % 2) + (f // 2) * FK + 2 * j
                            sc = cols[:, c:c + 1] if i is None else cols[:, bass.ds(i * 6 + c, 1)]
                            o = conv[:, f, d:S]
                            src = ps[:, 6 + f // 2, (f % 2) * S:(f % 2 + 1) * S - d]
                            m = dve.scalar_tensor_tensor(o, src, sc, o, ALU.mult, ALU.add)
                        if tap == 1:
                            link(m)
                        else:
                            m.then_inc(sem("conv_b"), 1)
                    dve.wait_ge(sem("conv_b"), T.up("conv_b"))
                    dve.sem_inc(sem("tr_free"), 1)
                    T.up("tr")
                    dve.wait_ge(sem("silu"), T.up("silu"))
                    m = dve.tensor_tensor(conv[:, 0:2, :], conv[:, 0:2, :], sg, ALU.mult)
                    link(m)
                    hi = ahi[:, 2 * j:2 * j + 2, :] if i is None else ahi[:, bass.ds(i * 6 + 2 * j, 2), :]
                    lo = alo[:, 2 * j:2 * j + 2, :] if i is None else alo[:, bass.ds(i * 6 + 2 * j, 2), :]
                    link(dve.tensor_copy(hi, conv[:, 0:2, :]))
                    dve.tensor_tensor(lo, conv[:, 0:2, :], hi.bitcast(F32), ALU.subtract).then_inc(sem("a_ready"), 1)
                    T.up("a_ready")
                    dve.wait_ge(sem("a_ready"), T("a_ready"))
                    dve.sem_inc(sem("conv_used"), 1)

                def evac(i=None):
                    chunk(i, 6, wait=False)
                    dve.wait_ge(sem("tok_ready"), T.up("tok_ready"))
                    dve.sem_inc(sem("acc_free"), 1)
                    T.up("acc")

                evac()
                turns = (n - 2) // 3
                with dve.Fori(0, turns) as i:
                    T.loop(i, tok_ready=3, conv_a=3, conv_b=3, silu=3, tr=3, dve=9, a_ready=3, acc=3)
                    for j in range(3):
                        evac(i)
                        convolve(j, i)
                    T.end(turns)
                pos[0] += 6 * (turns - 1)
                used[0] += 6 * (turns - 1)
                evac()
                convolve(n - 2)
                split(used[0] + 4)
                convolve(n - 1)
                down(FK)

            def turn_in(j, f, i=None):
                dve.wait_ge(sem("tr"), T.up("tr"))
                src = trb(0)[:, 0:f, :]
                hi = ahi[:, 2 * j:2 * j + f, :] if i is None else ahi[:, bass.ds(i * 6 + 2 * j, f), :]
                lo = alo[:, 2 * j:2 * j + f, :] if i is None else alo[:, bass.ds(i * 6 + 2 * j, f), :]
                link(dve.tensor_copy(hi, src))
                dve.tensor_tensor(lo, src, hi.bitcast(F32), ALU.subtract).then_inc(sem("a_ready"), 1)
                dve.wait_ge(sem("a_ready"), T.up("a_ready"))
                dve.sem_inc(sem("tr_free"), 1)

            def multiply(pr_, m, i=None, per=0, first=False):
                chunk(i, per, wait=False)
                dve.wait_ge(sem("silu"), T.up("silu"))
                if not first:
                    dve.wait_ge(sem("tr"), T("tr", -1))
                dve.tensor_tensor(ab[:, :, 0:m], pair(pr_, m), sg[:, :, 0:m], ALU.mult).then_inc(sem("tok_ready"), 1)
                dve.wait_ge(sem("tok_ready"), T.up("tok_ready"))
                dve.sem_inc(sem("acc_free"), 1)
                dve.sem_inc(sem("sg_used"), 1)
                T.up("acc")

            def gated_ffn(gate):
                n = FK // 2
                multiply(2, 256, first=True)
                turns = (n - 2) // 3
                with dve.Fori(0, turns) as i:
                    T.loop(i, tok_ready=3, silu=3, tr=3, dve=3, a_ready=3, acc=3)
                    for j in range(3):
                        multiply(j, 256, i, 6)
                        turn_in(j, 2, i)
                    T.end(turns)
                pos[0] += 6 * (turns - 1)
                used[0] += 6 * (turns - 1)
                multiply(0, 256)
                turn_in(n - 2, 2)
                split(used[0] + 4)
                turn_in(n - 1, 2)
                down(FK, gate)

            def attention(units):
                U = [(a, t) for a in units for t in range(NT)]
                b = T.n.get("att", 0)
                bo = T.n.get("att_o", 0)

                def mask(u):
                    a, t = U[u]
                    nk = (t + 1) * P
                    lo_ = S - nk
                    dve.wait_ge(sem("att_s"), b + u + 1)
                    if u >= 2:
                        dve.wait_ge(sem("att_e"), b + u - 1)
                    add = {"bias": lambda: bias[:, a["h"], lo_:S], "fox": lambda: causal[:, lo_:S],
                           "swa": lambda: window[:, lo_:S], "dsa": lambda: dsab[:, t, 0:nk]}[a["mask"]]()
                    o = sm[:, u % 2, 0:nk]
                    if a["mask"] == "fox":
                        m = dve.scalar_tensor_tensor(o, ps[:, u % 2, 0:nk], cum[:, t, a["h"]:a["h"] + 1], add, ALU.add, ALU.add)
                    else:
                        m = dve.tensor_tensor(o, ps[:, u % 2, 0:nk], add, ALU.add)
                    m.then_inc(sem("att_a"), 1)
                    dve.wait_ge(sem("att_a"), b + u + 1)
                    nm = st[:, 8 + u % 2:9 + u % 2]
                    m = dve.tensor_reduce(nm, o, AXX, ALU.max, negate=True)
                    if a["mask"] == "swa":
                        link(m)
                        c = a["h"] - 8
                        m = dve.tensor_tensor(nm, nm, st[:, 16 + c:17 + c], ALU.min)
                    m.then_inc(sem("att_m"), 1)

                def weigh(u):
                    a, t = U[u]
                    nk = (t + 1) * P
                    dve.wait_ge(sem("att_e"), b + u + 1)
                    rs = st[:, 10 + u % 2:11 + u % 2]
                    if a["mask"] == "swa":
                        link(dve.tensor_tensor(rs, rs, st[:, 12 + u % 2:13 + u % 2], ALU.add))
                    link(dve.reciprocal(st[:, 14 + u % 2:15 + u % 2], rs))
                    o = pr[:, u % 2, 0:nk]
                    dve.tensor_scalar(o, o, st[:, 14 + u % 2:15 + u % 2], None, ALU.mult).then_inc(sem("att_n"), 1)

                def gather(p_):
                    dve.wait_ge(sem("att_pv"), b + 4 * p_ + 4)
                    src = ps[:, 2 + p_ % 2, 0:S]
                    link(dve.tensor_copy(xhi[:, p_, :], src))
                    dve.tensor_tensor(xlo[:, p_, :], src, xhi[:, p_, :].bitcast(F32), ALU.subtract).then_inc(sem("att_o"), 1)

                n = len(U)
                for i in range(n + 5):
                    if i < n:
                        mask(i)
                    if 0 <= i - 1 < n:
                        weigh(i - 1)
                    if i >= 8 and i % 4 == 0 and (i - 8) // 4 < n // 4:
                        gather((i - 8) // 4)
                T.up("att", n)
                T.up("att_o", n // 4)

            def rope(v, heads, t):
                x1, x2 = v[:, :, 0:DH // 2], v[:, :, DH // 2:DH]
                w = heads * DH // 2
                cb = cosT[:, t, :].unsqueeze(1).to_broadcast([P, heads, DH // 2])
                sb_ = sinT[:, t, :].unsqueeze(1).to_broadcast([P, heads, DH // 2])
                r = [x[:, 0:w].rearrange("p (h d) -> p h d", h=heads) for x in rt]
                dve.tensor_tensor(r[0], x1, cb, ALU.mult)
                dve.tensor_tensor(r[1], x2, sb_, ALU.mult)
                dve.tensor_tensor(r[2], x2, cb, ALU.mult)
                link(dve.tensor_tensor(r[3], x1, sb_, ALU.mult))
                dve.tensor_tensor(x1, r[0], r[1], ALU.subtract)
                link(dve.tensor_tensor(x2, r[2], r[3], ALU.add))

            dve.sem_inc(sem("conv_used"), 1)
            dve.sem_inc(sem("mod_taken"), 1)
            split(2)
            normalise(h, TA)
            dve.wait_ge(sem("wsT_ready"), 1)
            dve.memset(wsT[DH:P, :, 0:DH], 0.0).then_inc(sem("wsT_ready"), 1)
            tail(xT_c)
            skip(4)
            T.up("acc", 4)
            dve.wait_ge(sem("acc_free"), 4)
            dve.wait_ge(sem("consts_landed"), 16 * 5)
            normalise(TB, TB, vg, "vn_ready")
            for g in range(KT):
                dve.wait_ge(sem("spatial"), g // 2 * 2 + 2)
                u = TA[:, :, g * P:(g + 1) * P]
                s_ = ps[:, g // 2, (g % 2) * S:(g % 2 + 1) * S].rearrange("p (t c) -> p t c", t=NT)
                dve.scalar_tensor_tensor(u, s_, cols[:, C_BS + g:C_BS + g + 1], u, ALU.add, ALU.mult).then_inc(sem("gz_ready"), 1)
            tail(xT_c)
            residual()
            normalise(h, TA)
            tail(xT_c)
            conv_ffn(0)
            normalise(h, TA)
            tail(xT_c)
            skip(4)
            T.up("acc", 4)
            tail(xT_b)
            skip(2)
            T.up("acc", 2)
            T.up("tr", 8)
            dve.wait_ge(sem("bias_ready"), 1)
            attention(CHUNKED)
            residual()
            normalise(h, TA)
            tail(xT_c)
            conv_ffn(1)
            dve.wait_ge(sem("fg1_landed"), 16)
            normalise(h, h, gates[:, 0, :], "h_normed")
            NF = DH // 2
            link(dve.tensor_copy(st[:, 24:26], posi[:, :]))
            for t in range(NT):
                m = dve.tensor_scalar(rot[:, 0, t * NF:(t + 1) * NF], rows[:, R_IF:R_IF + NF], st[:, 24 + t:25 + t], None, ALU.mult)
            link(m)
            for k, quarter in ((1, 0.0), (3, 0.25)):
                link(dve.tensor_scalar(rot[:, 2, :], rot[:, 0, :], 1.0 / (2 * PI), quarter, ALU.mult, ALU.add))
                link(dve.tensor_scalar(rot[:, 2, :], rot[:, 2, :], ROUND, -ROUND, ALU.add, ALU.add))
                link(dve.scalar_tensor_tensor(rot[:, k, :], rot[:, 2, :], -TWO_PI_A, rot[:, 0, :], ALU.mult, ALU.add))
                link(dve.scalar_tensor_tensor(rot[:, k, :], rot[:, 2, :], -TWO_PI_B, rot[:, k, :], ALU.mult, ALU.add))
                link(dve.scalar_tensor_tensor(rot[:, k, :], rot[:, 2, :], -TWO_PI_C, rot[:, k, :], ALU.mult, ALU.add))
                link(dve.tensor_scalar(rot[:, k, :], rot[:, k, :], quarter * 2 * PI, 3.1415925, ALU.add, ALU.min))
                m = dve.tensor_scalar(rot[:, k, :], rot[:, k, :], -3.1415925, None, ALU.max)
                if k == 1:
                    link(m)
            m.then_inc(sem("angle"), 1)
            dve.tensor_scalar(st[:, 16:24], rows[:, R_SK:R_SK + 8], -1.0, None, ALU.mult)
            dve.wait_ge(sem("pool"), 5)
            link(dve.tensor_copy(iota[:, :], iotai[:, :]))

            def ada(layer):
                dve.wait_ge(sem("w_used"), used[0])
                dve.sem_inc(sem("xlo_free"), 1)
                dve.wait_ge(sem("cs"), T.up("cs"))
                cb = cs[:, :].unsqueeze(2).to_broadcast([P, KT, P])
                link(dve.tensor_copy(xhi[:, :, 0:P], cb))
                dve.tensor_tensor(xlo[:, :, 0:P], cb, xhi[:, :, 0:P].bitcast(F32), ALU.subtract).then_inc(sem("c_ready"), 1)
                dve.wait_ge(sem("adab_landed"), T.up("adab_landed", 16))
                with dve.Fori(0, 2) as i:
                    T.loop(i, mod_psum=1, dve=2, mod_taken=1, acc=6)
                    for c in range(6):
                        chunk(i, 12, wait=c >= 4)
                        if c >= 4:
                            sl = slice((c - 4) * W, (c - 3) * W)
                            gsl = bass.ds(i * D + (c - 4) * W, W)
                            dve.tensor_tensor(gates[:, :, :].rearrange("p m d -> p (m d)")[:, gsl], ps[:, 2 * (c % 3), :],
                                              tok[:, gsl], ALU.add).then_inc(sem("acc_free"), 1)
                    dve.wait_ge(sem("mod_psum"), T.up("mod_psum"))
                    b0 = C_AB + layer * 6 * KT
                    g0 = C_GEM if layer == 0 else C_GOM
                    shv = shf[:, :, :].rearrange("p m k -> p (m k)")[:, bass.ds(i * KT, KT)]
                    scv = scl[:, :, :].rearrange("p m k -> p (m k)")[:, bass.ds(i * KT, KT)]
                    link(dve.tensor_tensor(shv, ps[:, 6, 0:KT], cols[:, bass.ds(i * 3 * KT + b0, KT)], ALU.add))
                    link(dve.tensor_tensor(scv, ps[:, 6, KT:2 * KT], cols[:, bass.ds(i * 3 * KT + (b0 + KT), KT)], ALU.add))
                    dve.scalar_tensor_tensor(scv, scv, 1.0, cols[:, bass.ds(i * KT + g0, KT)], ALU.add, ALU.mult)\
                        .then_inc(sem("mod_taken"), 1)
                    T.up("mod_taken")
                    T.up("acc", 6)
                    T.end(2)
                pos[0] += 12
                used[0] += 12
                dve.wait_ge(sem("acc_free"), T("acc"))

            ada(0)
            normalise(h, TA)
            tail(xT_c)
            skip(5)
            T.up("acc", 5)
            dve.wait_ge(sem("acc_free"), T("acc"))
            fb = rows[:, R_FB:R_FB + 8].unsqueeze(1).to_broadcast([P, NT, 8])
            link(dve.tensor_tensor(lgf[:, 0], te[:, :, 1536:1544], fb, ALU.add))
            link(dve.tensor_scalar(lgf[:, 1], lgf[:, 0], -1.0, None, ALU.mult))
            dve.tensor_tensor(lgf[:, 2], lgf[:, 0], lgf[:, 1], ALU.max).then_inc(sem("lgf"), 1)
            dve.wait_ge(sem("lgf_act"), 1)
            dve.tensor_scalar(lgf[:, 2], lgf[:, 1], 1.0, None, ALU.add).then_inc(sem("lgf"), 1)
            dve.wait_ge(sem("lgf_act"), 2)
            link(dve.tensor_scalar(lgf[:, 0], lgf[:, 0], 0.0, None, ALU.min))
            dve.tensor_tensor(lgf[:, 4], lgf[:, 0], lgf[:, 3], ALU.subtract).then_inc(sem("logf"), 1)
            dve.wait_ge(sem("cum_psum"), 1)
            dve.tensor_copy(cum, ps[:, 0, 0:16].rearrange("p (t h) -> p t h", t=NT)).then_inc(sem("cum_ready"), 1)
            dve.wait_ge(sem("tables"), 2)
            for t in range(NT):
                rope(te[:, t, 1544:2184].rearrange("p (h d) -> p h d", h=10), 10, t)
            dve.sem_inc(sem("rope_done"), 1)
            dve.tensor_scalar(ncT, ps[0:8, 1, 0:S], -1.0, None, ALU.mult).then_inc(sem("cum_ready"), 1)
            T.up("tr", 7)
            dve.wait_ge(sem("cum_ready"), 2)
            attention(EVEN)
            residual(0)
            normalise(h, TA)
            tail(xT_c)
            gated_ffn(1)
            ada(1)
            normalise(h, TA)
            tail(xT_c)
            skip(5)
            T.up("acc", 5)
            dve.wait_ge(sem("acc_free"), T("acc"))
            for t in range(NT):
                rope(to[:, t, 0:1280].rearrange("p (h d) -> p h d", h=20), 20, t)
                rope(to[:, t, 1536:2112].rearrange("p (h d) -> p h d", h=9), 9, t)
            link(dve.tensor_scalar(st[:, 48:64].rearrange("p (t h) -> p t h", t=NT), to[:, :, 2112:2120],
                                   8 ** -0.5 * DH ** -0.5, None, ALU.mult))
            dve.sem_inc(sem("rope_done"), 1)
            for u in range(16):
                t, ih = u // 8, u % 8
                nk = (t + 1) * P
                dve.wait_ge(sem("ix_read"), u + 1)
                iw = st[:, 48 + u:49 + u]
                if ih == 0:
                    m = dve.tensor_scalar(score[:, t, 0:nk], relu[:, u % 2, 0:nk], iw, None, ALU.mult)
                else:
                    m = dve.scalar_tensor_tensor(score[:, t, 0:nk], relu[:, u % 2, 0:nk], iw, score[:, t, 0:nk],
                                                 ALU.mult, ALU.add)
                m.then_inc(sem("ix_added"), 1)
                dve.wait_ge(sem("ix_added"), u + 1)
            for t in range(NT):
                nk = (t + 1) * P
                sc = score[:, t, 0:nk]
                link(dve.tensor_tensor(sc, sc, causal[:, S - nk:S], ALU.add))
                src = sc
                for r in range(TOPK // 8):
                    link(dve.max(mx8[:, t, :], src))
                    if r < TOPK // 8 - 1:
                        link(dve.match_replace(left[:, t, 0:nk], mx8[:, t, :], src, GONE))
                        src = left[:, t, 0:nk]
                thr = mx8[:, t, 7:8]
                link(dve.tensor_scalar(gt[:, t, 0:nk], sc, thr, None, ALU.is_gt))
                link(dve.tensor_scalar(eq[:, t, 0:nk], sc, thr, None, ALU.is_equal))
                link(dve.reduce_sum(g2[:, t, 0:1], gt[:, t, 0:nk], AXX))
                link(dve.tensor_tensor_scan(left[:, t, 0:nk], eq[:, t, 0:nk], eq[:, t, 0:nk], g2[:, t, 0:1],
                                            ALU.add, ALU.bypass))
                link(dve.tensor_scalar(left[:, t, 0:nk], left[:, t, 0:nk], float(TOPK), None, ALU.is_le))
                link(dve.tensor_tensor(eq[:, t, 0:nk], eq[:, t, 0:nk], left[:, t, 0:nk], ALU.mult))
                link(dve.tensor_tensor(gt[:, t, 0:nk], gt[:, t, 0:nk], eq[:, t, 0:nk], ALU.add))
                link(dve.tensor_scalar(gt[:, t, 0:nk], gt[:, t, 0:nk], -NEG, NEG, ALU.mult, ALU.add))
                if t == 0:
                    dve.wait_ge(sem("tr_free"), T.up("tr", 3 + 4 + 2))
                link(dve.tensor_tensor(dsab[:, t, 0:nk], gt[:, t, 0:nk], causal[:, S - nk:S], ALU.min))
            attention(ODD)
            residual(0)
            normalise(h, TA)
            tail(xT_c)
            dve.wait_ge(sem("router"), 1)
            rb = rows[:, R_RB:R_RB + NE].unsqueeze(1).to_broadcast([P, NT, NE])
            dve.tensor_tensor(rt_logit, ps[:, 5, 0:NT * NE].rearrange("p (t e) -> p t e", t=NT), rb, ALU.add)\
                .then_inc(sem("logits_taken"), 1)
            dve.wait_ge(sem("logits_taken"), 1)
            for t in range(NT):
                link(dve.max(mx8[:, t, :], rt_logit[:, t, :]))
                link(dve.max_index(ix8[:, t, :], mx8[:, t, :], rt_logit[:, t, :]))
            dve.tensor_copy(idxf[:, :, :], ix8[:, :, :])
            dve.tensor_tensor(g2[:, :, 0], mx8[:, :, 1], mx8[:, :, 0], ALU.subtract).then_inc(sem("g2"), 1)
            dve.wait_ge(sem("g2_act"), 1)
            link(dve.tensor_scalar(g2[:, :, 2], g2[:, :, 1], 1.0, None, ALU.add))
            link(dve.reciprocal(g2[:, :, 2], g2[:, :, 2]))
            link(dve.tensor_tensor(g2[:, :, 3], g2[:, :, 1], g2[:, :, 2], ALU.mult))
            link(dve.memset(comb[:, :, 0:1], 0.0))
            for t in range(NT):
                cb = comb[:, t, 1:1 + NE]
                link(dve.tensor_scalar(cb, iota[:, 0:NE], idxf[:, t, 0:1], g2[:, t, 2:3], ALU.is_equal, ALU.mult))
                link(dve.tensor_scalar(eqe[:, t, :], iota[:, 0:NE], idxf[:, t, 1:2], g2[:, t, 3:4], ALU.is_equal, ALU.mult))
                link(dve.tensor_tensor(cb, cb, eqe[:, t, :], ALU.add))
                link(dve.tensor_scalar(member[:, t, :], iota[:, 0:NE], idxf[:, t, 0:1], None, ALU.is_equal))
                link(dve.tensor_scalar(eqe[:, t, :], iota[:, 0:NE], idxf[:, t, 1:2], None, ALU.is_equal))
                m = dve.tensor_tensor(member[:, t, :], member[:, t, :], eqe[:, t, :], ALU.add)
                if t == 0:
                    link(m)
            m.then_inc(sem("member"), 1)
            link(dve.memset(macc, 0.0))
            link(dve.memset(tok[:, 4608:6144], 0.0))
            dve.wait_ge(sem("ranks"), 1)
            pl = place[:, :, 0:NE]
            link(dve.tensor_tensor(pl, ps[:, 5, 32:48].rearrange("p (t e) -> p t e", t=NT), member[:, :, :], ALU.mult))
            link(dve.tensor_scalar(pl, pl, -1.0, None, ALU.add))
            link(dve.tensor_scalar(place[:, :, NE:2 * NE], pl, -float(P), None, ALU.add))
            dve.tensor_copy(count[:, :], ps[0:1, 5, 48:48 + NE]).then_inc(sem("counted"), 1)
            dve.wait_ge(sem("counted"), 1)
            T.n.update(x_g=0, x_tr=0, x_xg=0, x_y=0, x_silu=0, x_tok=0, x_hi=0, x_a=0, x_added=0)

            def find_places(c):
                for t in range(NT):
                    m = dve.tensor_scalar(G[:, t, :], iota[:, :], place[:, t, c], None, ALU.is_equal)
                m.then_inc(sem("places"), 1)

            def split_gathered():
                for b in range(2):
                    dve.wait_ge(sem("xg"), T.up("x_xg"))
                    k = slice(4 * b, 4 * b + 4)
                    link(dve.tensor_copy(xhi[:, k, 0:P], xg[:, k, :]))
                    m = dve.tensor_tensor(xlo[:, k, 0:P], xg[:, k, :], xhi[:, k, 0:P].bitcast(F32), ALU.subtract)
                m.then_inc(sem("xg_ready"), 1)
                T.up("xg_ready")
                dve.wait_ge(sem("xg_ready"), T("xg_ready"))
                dve.sem_inc(sem("g_taken"), 1)

            def product(j, i):
                m = 256 if j < 5 else P
                used[0] += 2
                split(used[0] + AHEAD, i, EXP)
                dve.wait_ge(sem("x_silu"), T.up("x_silu"))
                dve.tensor_tensor(abx[:, j % 2, 0:m], ps[:, (2, 0, 1)[j % 3], 0:m], sgx[:, 0:m], ALU.mult).then_inc(sem("x_tok"), 1)

            def lo_of(j):
                f = 2 if j < 5 else 1
                dve.wait_ge(sem("x_hi"), T.up("x_hi"))
                dve.tensor_tensor(alo[:, 2 * j:2 * j + f, 0:P], ps[:, 6, 0:f * P].rearrange("p (f s) -> p f s", f=f),
                                  ahi[:, 2 * j:2 * j + f, 0:P].bitcast(F32), ALU.subtract).then_inc(sem("x_a"), 1)
                dve.wait_ge(sem("x_a"), T.up("x_a"))
                dve.sem_inc(sem("x_tr_free"), 1)

            def add_expert(i):
                for n in range(2):
                    dve.wait_ge(sem("y_psum"), T.up("x_y"))
                    for t in range(NT):
                        o = macc[:, t, n * W:(n + 1) * W]
                        m = dve.scalar_tensor_tensor(o, ps[:, (5, 7, 3, 4)[2 * n + t], :], comb[:, t, i], o, ALU.mult, ALU.add)
                m.then_inc(sem("y_added"), 1)

            for name in ("g_taken", "x_tr_free", "x_tok"):
                dve.sem_inc(sem(name), 1)
            T.n["xg_ready"] = 0
            find_places(bass.ds(0, 1))
            split_gathered()
            dve.sem_inc(sem("y_copied"), 1)
            with dve.Fori(0, NE) as i:
                T.loop(i, x_xg=2, x_silu=6, x_hi=6, x_a=6, x_y=2, dve=2, xg_ready=1, x_tr=0)
                product(0, i)
                add_expert(bass.ds(i, 1))
                for j in range(1, 6):
                    product(j, i)
                    lo_of(j - 1)
                    if j == 1:
                        dve.wait_ge(sem("x_tr_free"), i * 7 + 3)
                        find_places(bass.ds(i + 1, 1))
                split_gathered()
                lo_of(5)
                used[0] += 6
                split(used[0] + AHEAD, i, EXP)
                T.end(NE)
            pos[0] += EXP * (NE - 1)
            used[0] += EXP * (NE - 1) + AHEAD
            add_expert(slice(NE, NE + 1))
            with dve.Fori(0, NE) as i:
                T.loop(i, x_xg=2, x_silu=6, x_hi=6, x_a=6, x_y=2, dve=2, xg_ready=1)
                n = dve.value_load(count[0:1, bass.ds(i, 1)])
                with dve.If(n > P):
                    top[0] = used[0] + EXP
                    find_places(bass.ds(i + NE, 1))
                    split_gathered()
                    for j in range(6):
                        product(j, i)
                        if j:
                            lo_of(j - 1)
                    lo_of(5)
                    used[0] += 6
                    split(used[0], i, EXP)
                    add_expert(bass.ds(i + 1, 1))
                with dve.Else():
                    dve.drain()
                    for name, k in (("places", 1), ("dve", 2), ("xg_ready", 1), ("g_taken", 1), ("lo_done", EXP), ("x_tok", 6),
                                    ("x_a", 6), ("x_tr_free", 6), ("y_added", 1)):
                        dve.sem_inc(sem(name), k)
                T.end(NE)
            for t in range(NT):
                dve.wait_ge(sem("y_added"), 2 * NE + 1)
                link(dve.tensor_tensor(macc[:, t, :], macc[:, t, :], gates[:, 1, :], ALU.mult))
                dve.tensor_tensor(h[:, t, :], macc[:, t, :], h[:, t, :], ALU.add).then_inc(sem("h_added"), 1)
            dve.wait_ge(sem("fg_landed"), 16)
            normalise(h, TA, TC[:, 0, :], "y_ready")


_OUT = ((1, S, D), "float32")


def kernel(**inputs):
    import numpy as np
    import concourse.bacc as bacc
    from concourse.bass_utils import run_bass_kernel_spmd as run

    a = {k: np.asarray(v) for k, v in inputs.items()}

    def by_feature(v):
        v = v.reshape(-1, P)
        return v.T

    cols = np.concatenate([by_feature(v) for v in (
        a["a_norm_g"], a["kv_norm_g"], a["b_norm_g"], a["f_norm_g"][0], a["f_norm_g"][1],
        a["e_norm_mix_2"], a["e_norm_ffn_2"], a["o_norm_mix_2"], a["o_norm_ffn_2"],
        a["f_conv_w"], a["f_conv_b"], a["a_b_s"], a["e_ada_b_2"], a["o_ada_b_2"], a["c_2"])], axis=1)
    assert cols.shape == (P, C_END)
    half = DH // 2
    inv_freq = (ROPE_THETA ** (-np.arange(half, dtype=np.float32) / np.float32(half))).astype(np.float32)
    rows = np.concatenate([a["e_forget_b_2"].ravel(), a["e_sinks_2"].ravel(), a["o_router_b_2"].ravel(), inv_freq])[None]
    rel = np.clip(P + np.arange(P)[:, None] - np.arange(S)[None, :], -REL, REL) + REL
    adab = np.concatenate([a[n].reshape(6, D)[j] for n in ("e_ada_b_2", "o_ada_b_2") for j in (2, 5)]).reshape(2, 2 * D)
    arrays = {
        "x": a["x"], "cols": cols, "rows": rows, "vg": a["a_v_norm_g"], "fg1": a["final_norm_g"][None], "fg": a["final_norm_2"][None], "adab": adab,
        "positions": by_feature(a["positions_2"]), "w_s": a["a_w_s"], "toep": a["b_rel_bias"][0][:, rel].transpose(1, 0, 2), "router": a["o_router_w_2"][0],
        "w_in": a["a_w_in"][0], "w_out": a["a_w_out"][0], "w_kv": a["w_kv"], "w_q": a["b_w_q"][0], "w_o": a["b_w_o"][0],
        "f_in": a["f_w_in"], "f_down": a["f_w_down"],
        "e_ada": a["e_ada_w_2"][0], "e_in": a["e_w_in_2"][0], "e_out": a["e_w_out_2"][0], "e_gate": a["e_ffn_gate_2"][0],
        "e_up": a["e_ffn_up_2"][0], "e_down": a["e_ffn_down_2"][0],
        "o_ada": a["o_ada_w_2"][0], "o_in": a["o_w_in_2"][0], "o_out": a["o_w_out_2"][0], "x_gate": a["o_exp_gate_2"][0],
        "x_up": a["o_exp_up_2"][0], "x_down": a["o_exp_down_2"][0],
    }
    arrays = {k: np.ascontiguousarray(v) for k, v in arrays.items()}
    nc = bacc.Bacc("TRN2", target_bir_lowering=False, num_devices=1)
    args = [nc.dram_tensor(f"{n}_dram", v.shape, mybir.dt.from_np(v.dtype), kind="ExternalInput").ap() for n, v in arrays.items()]
    args.append(nc.dram_tensor("y", _OUT[0], F32, kind="ExternalOutput").ap())
    build_program(nc, *args)
    return run(nc, [{f"{n}_dram": v for n, v in arrays.items()}], core_ids=[0]).results[0]["y"]
```

```python
from contextlib import ExitStack

import concourse.bass as bass
from concourse import mybir

F32 = mybir.dt.float32
F32R = mybir.dt.float32r
I32 = mybir.dt.int32
U32 = mybir.dt.uint32
ALU = mybir.AluOpType
ACT = mybir.ActivationFunctionType
AXX = mybir.AxisListType.X

P = 128
D = 1024
S = 256
NT = S // P
KT = D // P
DH = 64
NH = D // DH
FF = 2816
FK = FF // P
FE = 1408
NE = 8
W = 512
SLOT = 2048
RAW = 6
SPL = 3
AHEAD = 2
EXP = 18
EPS = 1e-6
NEG = -1e30
GONE = -3e38
E_IN = 2312
O_IN = 2120
E_ORDER = (3, 4, 0, 1, 2)
G_ORDER = (2, 3, 0, 1)
O_ORDER = (3, 4, 0, 1, 2)
TOPK = S // 4
REL = 128
ROPE_THETA = 10000.0
PI = 3.14159265358979
TWO_PI_A = 6.28125
TWO_PI_B = 0.0019340515136718750
TWO_PI_C = 2 * 3.141592653589793 - 6.28125 - 0.0019340515136718750
ROUND = 12582912.0

C_GA, C_GKV, C_GB, C_GF0, C_GF1, C_GEM, C_GEF, C_GOM, C_GOF = (KT * n for n in range(9))
C_CW = 9 * KT
C_CB = C_CW + 2 * 3 * 2 * FK
C_BS = C_CB + 2 * 2 * FK
C_AB = C_BS + KT
C_C = C_AB + 2 * 6 * KT
C_END = C_C + KT
R_FB, R_SK, R_RB, R_IF = 0, 8, 16, 24
R_END = R_IF + DH // 2


def chunks_of(n, order=None):
    return [(c * W, min(W, n - c * W)) for c in order or range((n + W - 1) // W)]


def stream_plan():
    plan = []
    at = {}

    def proj(name, n, order=None):
        at[name] = len(plan)
        for _, w in chunks_of(n, order):
            plan.extend([(4 * w, 1)] * 2)

    def gated(name, kt, pairs=1):
        at[name] = len(plan)
        for _ in range(pairs):
            plan.extend([(SLOT, 2)] * (2 * (kt // 2)))
            if kt % 2:
                plan.extend([(SLOT // 2, 2)] * 2)
            plan.extend([(SLOT, 1)] * (kt // 2))
            if kt % 2:
                plan.append((SLOT // 2, 1))

    proj("gmlp_in", 2 * D, G_ORDER)
    proj("gmlp_out", D)
    gated("ffn0", FK)
    proj("kv", 2 * D)
    proj("q", D)
    proj("e_ada", 6 * D)
    proj("attn_out", D)
    gated("ffn1", FK)
    proj("e_in", E_IN, E_ORDER)
    proj("o_ada", 6 * D)
    proj("e_out", D)
    gated("e_ffn", FK)
    proj("o_in", O_IN, O_ORDER)
    proj("o_out", D)
    gated("moe", FE // P, NE)
    at["spare"] = len(plan)
    plan.extend([(SLOT, 2)] * AHEAD)
    gated("more", FE // P, NE)
    at["end"] = len(plan)
    landed, counts = [], [0] * RAW
    for s, (_, n) in enumerate(plan):
        counts[s % RAW] += 16 * n
        landed.append(counts[s % RAW])
    return plan, at, landed


class Tally:

    def __init__(self):
        self.n, self.per, self.i = {}, {}, None

    def up(self, name, k=1):
        self.n[name] = self.n.get(name, 0) + k
        return self(name)

    def __call__(self, name, less=0):
        v = self.n.get(name, 0) - less
        return v if self.i is None or not self.per.get(name) else self.i * self.per[name] + v

    def loop(self, i, **per):
        self.i, self.per, self.start = i, per, dict(self.n)

    def end(self, turns):
        for k in set(self.n) | set(self.per):
            made = self.n.get(k, 0) - self.start.get(k, 0)
            assert made == self.per.get(k, 0), (k, made)
            self.n[k] = self.n.get(k, 0) + made * (turns - 1)
        self.i = None


def build_program(nc, x_in, cols_in, rows_in, vg_in, fg1_in, fg_in, pos_in, ws_in, toep_in, rw_in,
                  w_in, w_out, w_kv, w_q, w_o, f_in, f_down,
                  e_ada, e_in, e_out, e_gate, e_up, e_down,
                  o_ada, o_in, o_out, x_gate, x_up, x_down, out):
    plan, AT, LANDED = stream_plan()
    ctx = ExitStack()
    with ctx:
        def sb(name, shape, dt=F32):
            return ctx.enter_context(nc.sbuf_tensor(name, shape, dt))

        sems = {}

        def sem(name):
            if name not in sems:
                sems[name] = ctx.enter_context(nc.semaphore(name))
            return sems[name]

        h = sb("h", [P, NT, D])
        tok = sb("tok", [P, 3 * NT * D])
        xhi = sb("xhi", [P, KT, S], F32R)
        xlo = sb("xlo", [P, KT, S], F32R)
        raw = sb("raw", [P, RAW, SLOT])
        whi = sb("whi", [P, SPL, SLOT], F32R)
        wlo = sb("wlo", [P, SPL, SLOT], F32R)
        gates = sb("gates", [P, 2, D])
        ident = sb("ident", [P, P])
        ones = sb("ones", [P, P])
        tri = sb("tri", [P, P])
        causal = sb("causal", [P, S])
        window = sb("window", [P, S])
        cols = sb("cols", [P, C_END])
        rows = sb("rows", [P, R_END])
        rw = sb("rw", [P, KT, NE])
        scl2 = sb("scl", [P, 2, 2, KT])
        shf2 = sb("shf", [P, 2, 2, KT])
        gcol = sb("gcol", [P, 2, 2, KT])
        cs = sb("cs", [P, KT])
        c2 = sb("c2", [P, KT, 2], F32R)
        st = sb("st", [P, 64])
        cosT = sb("cosT", [P, NT, DH // 2])
        sinT = sb("sinT", [P, NT, DH // 2])
        posi = sb("posi", [P, NT], I32)
        ps = ctx.enter_context(nc.psum_tensor("ps", [P, 8, 512], F32))
        comb = sb("comb", [P, NT, NE + 1])
        member = sb("member", [P, NT, NE])
        place = sb("place", [P, NT, 2 * NE])
        count = sb("count", [1, NE + 1], I32)
        iotai = sb("iotai", [P, P], I32)
        iota = sb("iota", [P, P])
        mx8 = sb("mx8", [P, NT, 8])
        ix8 = sb("ix8", [P, NT, 8], U32)
        idxf = sb("idxf", [P, NT, 8])
        g2 = sb("g2", [P, NT, 4])
        eqe = sb("eqe", [P, NT, NE])
        rot = sb("rot", [P, 4, NT * DH // 2])
        with nc.sbuf_tensor("ahi", [P, FK, S], F32R) as ahi, nc.sbuf_tensor("alo", [P, FK, S], F32R) as alo:
            pass
        af = sb("attn_scratch", [P, FK * S])[:, :]
        lf = sb("head_scratch", [P, FK * S])[:, :]

        TA, TB, TC = (tok[:, n * NT * D:(n + 1) * NT * D].rearrange("p (t d) -> p t d", t=NT) for n in range(3))
        te = tok[:, 0:NT * E_IN].rearrange("p (t d) -> p t d", t=NT)
        to = tok[:, 0:NT * O_IN].rearrange("p (t d) -> p t d", t=NT)
        xT_c = tok[:, 2 * NT * D:3 * NT * D].rearrange("p (k s) -> p k s", k=KT)
        ab = tok[:, 2048:3072].rearrange("p (t c) -> p t c", t=NT)
        conv = tok[:, 3072:4096].rearrange("p (f s) -> p f s", f=4)
        sg = tok[:, 4096:4608].rearrange("p (f s) -> p f s", f=2)
        gwide = TB.rearrange("p t (m i) -> p (t m) i", i=P)
        bias = af[:, 0:NH * S].rearrange("p (h k) -> p h k", h=NH)
        sm = pr = af[:, 4096:5120].rearrange("p (b k) -> p b k", b=4)
        pT = af[:, 5120:5632].rearrange("p (b k) -> p b k", b=2)
        qT = lf[:, 0:2048].rearrange("p (k s) -> p k s", k=KT)
        kT = lf[:, 2048:4096].rearrange("p (k s) -> p k s", k=KT)
        iqT = lf[:, 4096:5120].rearrange("p (k s) -> p k s", k=4)
        ikT = lf[:, 5120:5376]
        arow = lf[0:2, 4096:5120].rearrange("p (b c) -> p b c", b=2)
        ws = lf[:, 0:1024].rearrange("p (g j) -> p g j", g=KT)
        wsT = lf[:, 1024:2048].rearrange("p (g i) -> p g i", g=KT)
        vg = lf[:, 2048:3072]
        xT_b = lf[:, 0:2048].rearrange("p (k s) -> p k s", k=KT)
        kd = af[:, 0:1024].rearrange("p (t j c d) -> p t j c d", t=NT, j=4, c=2)
        ikd = af[:, 1024:1280].rearrange("p (t c d) -> p t c d", t=NT, c=2)
        rt = [af[:, 1280 + n * 640:1280 + (n + 1) * 640] for n in range(4)]
        sel8 = af[0:8, 1280:2304].rearrange("p (h i) -> p h i", h=8)
        ncT = af[0:8, 2304:2560]
        lgf = af[:, 3840:3920].rearrange("p (n t h) -> p n t h", n=5, t=NT)
        cum = af[:, 3920:3936].rearrange("p (t h) -> p t h", t=NT)
        rt_o = [af[:, 1280 + n * 288:1280 + (n + 1) * 288] for n in range(4)]
        score = af[:, 2432:2944].rearrange("p (t k) -> p t k", t=NT)
        left = af[:, 2944:3456].rearrange("p (t k) -> p t k", t=NT)
        relu = af[:, 3456:3968].rearrange("p (b k) -> p b k", b=2)
        gt = af[:, 3968:4480].rearrange("p (t k) -> p t k", t=NT)
        eq = af[:, 4480:4992].rearrange("p (t k) -> p t k", t=NT)
        dsab = score
        macc = TB
        xg = lf[:, FE // P * S:FE // P * S + KT * P].rearrange("p (k s) -> p k s", k=KT)
        sgx = tok[:, 4096:4352]
        abx = lf[:, 4096:4608].rearrange("p (b c) -> p b c", b=2)
        G = tok[:, 5632:5888].rearrange("p (t j) -> p t j", t=NT)
        GT = ahi[:, FE // P, :].rearrange("p (t i) -> p t i", t=NT)
        yhi, ylo = xhi[:, :, P:S], xlo[:, :, P:S]
        rt_logit = st[:, 32:48].rearrange("p (t e) -> p t e", t=NT)

        def pair(n, w=W):
            return ps[:, 2 * n:2 * n + 2, 0:w]

        def trb(b):
            return ps[:, 6 + b, :].rearrange("p (k s) -> p k s", k=2)

        block = ctx.enter_context(nc.Block())

        CHUNKED = [dict(q=hh // 2, k=hh // 2, v=("c", hh * DH), mask="bias", h=hh) for hh in range(NH)]
        EVEN = ([dict(q=hh // 2, k=hh // 2, v=("e", 1024 + hh * DH), mask="fox", h=hh) for hh in range(8)]
                + [dict(q=hh // 2, k=4 + (hh - 8) // 4, v=("e", 2184 + (hh - 8) // 4 * DH), mask="swa", h=hh)
                   for hh in range(8, NH)])
        ODD = [dict(q=hh // 2, k=hh // 4, v=("o", 1280 + hh // 4 * DH), mask="dsa", h=hh) for hh in range(NH)]

        ADA = 24

        def ada_due(i):
            return range(min(ADA, i * 3 // 4), min(ADA, (i + 1) * 3 // 4))

        def lo_made(s):
            by_pool = 0
            for first in (AT["e_ada"], AT["o_ada"]):
                if first <= s < first + ADA and (s - first) % 2:
                    return "pool_lo", by_pool + (s - first) // 2 + 1
                by_pool += max(0, min(s - first, ADA)) // 2
            return "lo_done", s + 1 - by_pool

        def wait_lo(eng, s, i=None, per=0):
            name, made = lo_made(s)
            assert i is None or name == "lo_done"
            eng.wait_ge(sem(name), made if i is None else i * per + made)

        neg_max, total, sink, weight = ((lambda u, c=c: st[:, c + u % 4:c + 1 + u % 4]) for c in (32, 36, 40, 44))

        def v_of(a, kk):
            where, c = a["v"]
            src = {"c": TC, "e": te, "o": to}[where]
            return src[:, kk, c:c + DH]

        @block.sync
        def _(sp):
            sp.dma_start(h[:, :, :], x_in.rearrange("o (t p) d -> p (o t) d", p=P)).then_inc(sem("x_landed"), 16)
            sp.dma_start(cols[:, :], cols_in).then_inc(sem("cols_landed"), 16)
            pos = [0]

            def load(parts, i=None, per=0):
                s = pos[0]
                pos[0] += 1
                parts = list(parts)
                assert len(parts) == plan[s][1]
                if s >= RAW:
                    wait_lo(sp, s - RAW, i, per)
                for dst, src in parts:
                    sp.dma_start(dst(s % RAW), src).then_inc(sem(f"landed{s % RAW}"), 16)

            def rows_of(w, hf, c, n, at=0, width=None):
                width = width or n
                src = w.rearrange("(k p) n -> p k n", p=P)[:, 4 * hf:4 * hf + 4, c]
                return (lambda s: raw[:, s, 0:4 * width].rearrange("p (k n) -> p k n", k=4)[:, :, at:at + n], src)

            def proj(w, n, order=None):
                for c, m in chunks_of(n, order):
                    for hf in range(2):
                        load([rows_of(w, hf, slice(c, c + m), m)])

            def down(w, kt, i=None, per=0, e=None):
                wv = w.rearrange("(k p) n -> p k n", p=P)
                for k in range(0, kt, 2):
                    m = min(2, kt - k)
                    load([(lambda s, m=m: raw[:, s, 0:m * D].rearrange("p (k n) -> p k n", k=m), wv[:, k:k + m, :])],
                         i, per)

            def gated_ffn(up, gate, kt):
                def chunk(c, i=None, per=0):
                    for hf in range(2):
                        load([rows_of(up[0], hf, c(up[1]), 256, 0, W), rows_of(gate[0], hf, c(gate[1]), 256, 256, W)],
                             i, per)
                n = kt // 2
                chunk(lambda o: slice(o, o + 256))
                with sp.Fori(0, (n - 2) // 3) as i:
                    for j in range(1, 4):
                        chunk(lambda o: bass.ds(i * 768 + (o + 256 * j), 256), i, 6)
                pos[0] += 6 * ((n - 2) // 3 - 1)
                chunk(lambda o: slice(o + (n - 1) * 256, o + n * 256))

            def conv_ffn(layer):
                gated_ffn((f_in[layer], 0), (f_in[layer], FF), FK)
                down(f_down[layer], FK)

            proj(w_in, 2 * D, G_ORDER)
            proj(w_out, D)
            conv_ffn(0)
            proj(w_kv, 2 * D)
            proj(w_q, D)

            proj(e_ada, 6 * D)
            proj(w_o, D)
            conv_ffn(1)
            proj(e_in, E_IN, E_ORDER)
            proj(o_ada, 6 * D)
            proj(e_out, D)
            gated_ffn((e_up, 0), (e_gate, 0), FK)
            down(e_down, FK)
            proj(o_in, O_IN, O_ORDER)
            proj(o_out, D)
            assert pos[0] == AT["moe"]
            ug, uu, ud = (w.rearrange("e d f -> (e d) f") for w in (x_gate, x_up, x_down))

            def expert(i):
                def part(w, r0, nr, c, n, at, width, rows_per):
                    src = w[bass.ds(i * rows_per + r0, nr * P), :].rearrange("(k p) n -> p k n", p=P)[:, :, c:c + n]
                    return (lambda s: raw[:, s, 0:nr * width].rearrange("p (k n) -> p k n", k=nr)[:, :, at:at + n], src)
                for c in range(0, FE, 256):
                    m = min(256, FE - c)
                    for hf in range(2):
                        load([part(uu, hf * 4 * P, 4, c, m, 0, 2 * m, D), part(ug, hf * 4 * P, 4, c, m, m, 2 * m, D)],
                             i, EXP)
                for k in range(0, FE // P, 2):
                    m = min(2, FE // P - k)
                    load([part(ud, k * P, m, 0, D, 0, D, FE)], i, EXP)
                pos[0] -= EXP

            with sp.Fori(0, NE) as i:
                expert(i)
            pos[0] += EXP * NE
            assert pos[0] == AT["spare"]
            for hf in range(2):
                load([rows_of(x_up[0], hf, slice(0, 256), 256, 0, W), rows_of(x_gate[0], hf, slice(0, 256), 256, 256, W)])
            assert pos[0] == AT["more"]
            sp.wait_ge(sem("counted"), 1)
            most = sp.value_load(count[0:1, NE:NE + 1])
            with sp.If(most > P):
                with sp.Fori(0, NE) as i:
                    n = sp.value_load(count[0:1, bass.ds(i, 1)])
                    with sp.If(n > P):
                        expert(i)
                    with sp.Else():
                        for s in range(pos[0], pos[0] + RAW):
                            step = LANDED[s + EXP] - LANDED[s]
                            sp.wait_ge(sem(f"landed{s % RAW}"), i * step + (LANDED[s] - 16 * plan[s][1]))
                            sp.sem_inc(sem(f"landed{s % RAW}"), step)
            sp.wait_ge(sem("y_copied"), 2 * NE + 1)
            sp.wait_ge(sem("y_psum"), 2 * (2 * NE + 1))
            sp.dma_start(TC[:, 0, :], fg_in.to_broadcast([P, D])).then_inc(sem("fg_landed"), 16)
            for t in range(NT):
                sp.wait_ge(sem("y_ready"), t + 1)
                sp.dma_start(out[0, t * P:(t + 1) * P, :], TA[:, t, :]).then_inc(sem("stored"), 16)
            sp.wait_ge(sem("stored"), 16 * NT)

        @block.gpsimd
        def _(g):
            def ada_lo(first):
                with g.Fori(0, ADA // RAW) as i:
                    for j in range(1, RAW, 2):
                        s = first + j
                        g.wait_ge(sem("hi_done"), i * RAW + (s + 1))
                        g.tensor_tensor(wlo[:, s % SPL, :], raw[:, s % RAW, :], whi[:, s % SPL, :].bitcast(F32), ALU.subtract)\
                            .then_inc(sem("pool_lo"), 1)

            g.memset(ident[:, :], 0.0).then_inc(sem("pool"), 1)
            g.memset(ones[:, :], 1.0).then_inc(sem("pool"), 1)
            g.memset(causal[:, :], 0.0).then_inc(sem("pool"), 1)
            g.memset(window[:, :], 0.0).then_inc(sem("pool"), 1)
            g.iota(iotai[:, :], [[1, P]], base=0, channel_multiplier=0).then_inc(sem("pool"), 1)
            g.wait_ge(sem("pool"), 5)
            g.affine_select(out=ident[:, :], in_=ident[:, :], compare_op=ALU.not_equal, fill=1.0, base=0,
                            pattern=[[-1, P]], channel_multiplier=1).then_inc(sem("consts"), 1)
            g.affine_select(out=tri[:, :], in_=ones[:, :], compare_op=ALU.is_ge, fill=0.0, base=0,
                            pattern=[[1, P]], channel_multiplier=-1).then_inc(sem("consts"), 1)
            g.affine_select(out=causal[:, P:S], in_=causal[:, P:S], compare_op=ALU.is_ge, fill=NEG, base=0,
                            pattern=[[-1, P]], channel_multiplier=1).then_inc(sem("consts"), 1)
            g.affine_select(out=window[:, P:S], in_=window[:, P:S], compare_op=ALU.is_ge, fill=NEG, base=0,
                            pattern=[[-1, P]], channel_multiplier=1).then_inc(sem("consts"), 1)
            g.affine_select(out=window[:, 0:P], in_=window[:, 0:P], compare_op=ALU.is_gt, fill=NEG, base=0,
                            pattern=[[1, P]], channel_multiplier=-1).then_inc(sem("consts"), 1)
            g.wait_ge(sem("h_added"), 4)
            g.dma_start(bias, toep_in).then_inc(sem("toep_landed"), 16)
            g.wait_ge(sem("toep_landed"), 16)
            g.memset(bias[0:DH, :, P + DH:S], NEG).then_inc(sem("bias_ready"), 1)
            ada_lo(AT["e_ada"])
            g.wait_ge(sem("rope_done"), 1)
            g.memset(sel8, 0.0).then_inc(sem("pool"), 1)
            g.wait_ge(sem("pool"), 6)
            g.affine_select(out=sel8, in_=sel8, compare_op=ALU.not_equal, fill=1.0, base=0,
                            pattern=[[-1, 8], [0, P]], channel_multiplier=1).then_inc(sem("sel_ready"), 1)
            ada_lo(AT["o_ada"])

        @block.tensor
        def _(pe):
            T = Tally()
            pos = [0]
            late_x = [False]

            def mm3(o, xh, xl, wh, wl, start, stop):
                pe.matmul(o, xh, wh, start=start, stop=False)
                pe.matmul(o, xh, wl, start=False, stop=False)
                return pe.matmul(o, xl, wh, start=False, stop=stop)

            def proj(pr_, width, tiles=NT, i=None, per=0, back=2, early=False):
                if T.n.get("acc", 0) - back > 0:
                    pe.wait_ge(sem("acc_free"), T("acc", back))
                for hf in range(2):
                    s = pos[0]
                    pos[0] += 1
                    if hf and late_x[0]:
                        pe.wait_ge(sem("x_ready"), T.up("x_ready", 2))
                        late_x[0] = False
                    wait_lo(pe, s, i, per)
                    wh = whi[:, s % SPL, 0:4 * width].rearrange("p (k n) -> p k n", k=4)
                    wl = wlo[:, s % SPL, 0:4 * width].rearrange("p (k n) -> p k n", k=4)
                    for t in range(tiles):
                        for k in range(4):
                            kk = 4 * hf + k
                            last = mm3(ps[:, 2 * pr_ + t, 0:width], xhi[:, kk, t * P:(t + 1) * P],
                                       xlo[:, kk, t * P:(t + 1) * P], wh[:, k, :], wl[:, k, :],
                                       kk == 0, kk == KT - 1)
                        if early and hf and t == 0:
                            last.then_inc(sem("t0_done"), 1)
                    last.then_inc(sem("w_used"), 1)
                T.up("acc")

            def down(kt, late=None):
                pe.wait_ge(sem("acc_free"), T("acc"))
                for j in range((kt + 1) // 2):
                    if j == 2:
                        late()
                    s = pos[0]
                    pos[0] += 1
                    pe.wait_ge(sem("a_ready"), T.up("a_ready"))
                    wait_lo(pe, s)
                    for t in range(NT):
                        for k in range(2 * j, min(2 * j + 2, kt)):
                            o = (k - 2 * j) * D
                            for n in range(2):
                                a, b = o + n * W, o + (n + 1) * W
                                last = mm3(ps[:, 2 * n + t, :], ahi[:, k, t * P:(t + 1) * P],
                                           alo[:, k, t * P:(t + 1) * P], whi[:, s % SPL, a:b], wlo[:, s % SPL, a:b],
                                           k == 0, k == kt - 1)
                        if t == 0 and j == (kt + 1) // 2 - 1:
                            last.then_inc(sem("t0_done"), 1)
                    last.then_inc(sem("w_used"), 1)
                T.up("acc", 2)

            def tail(src, wait=None):
                pe.wait_ge(sem("tr_free"), T("tr"))
                for t in range(NT):
                    if t and wait:
                        wait()
                    for k in range(4):
                        last = pe.transpose(trb(k // 2)[:, k % 2, t * P:(t + 1) * P], src[:, t, k * P:(k + 1) * P], ident[:, :])
                        if t and k % 2:
                            last.then_inc(sem("tr"), 1)
                            T.up("tr")
                for r in range(2):
                    pe.wait_ge(sem("tr_free"), T("tr", 1))
                    for t in range(NT):
                        for k in range(2):
                            kk = 4 + 2 * r + k
                            last = pe.transpose(trb(r)[:, k, t * P:(t + 1) * P], src[:, t, kk * P:(kk + 1) * P], ident[:, :])
                    last.then_inc(sem("tr"), 1)
                    T.up("tr")

            def rounds(srcs):
                for r in range(0, len(srcs), 2):
                    if T.n.get("tr", 0) - (r > 0) > 0:
                        pe.wait_ge(sem("tr_free"), T("tr", 1 if r else 0))
                    for k in range(r, min(r + 2, len(srcs))):
                        for t in range(NT):
                            last = pe.transpose(trb(r // 2 % 2)[:, k - r, t * P:(t + 1) * P], srcs[k](t), ident[:, :])
                    last.then_inc(sem("tr"), 1)
                    T.up("tr")

            def norm_tail(src):
                pe.wait_ge(sem("xn"), T.up("xn"))
                tail(src, lambda: pe.wait_ge(sem("xn"), T.up("xn")))

            def x_ready():
                pe.wait_ge(sem("x_ready"), T.up("x_ready", 2))
                late_x[0] = True

            def transposes(n, i=None):
                pe.wait_ge(sem("tok_ready"), T.up("tok_ready"))
                pe.wait_ge(sem("tr_free"), T("tr"))
                for f in range(n):
                    for t in range(NT):
                        last = pe.transpose(ps[:, 6 + f // 2, (f % 2) * S + t * P:(f % 2) * S + (t + 1) * P],
                                            ab[:, t, f * P:(f + 1) * P], ident[:, :])
                last.then_inc(sem("tr"), 1)
                T.up("tr")

            def gated_ffn(n_tr):
                n = FK // 2
                x_ready()
                proj(2, W, back=0)
                turns = (n - 2) // 3
                with pe.Fori(0, turns) as i:
                    T.loop(i, acc=3, tok_ready=3, tr=3)
                    for j in range(3):
                        proj(j, W, i=i, per=6)
                        transposes(n_tr)
                    T.end(turns)
                pos[0] += 6 * (turns - 1)
                proj(0, W)
                transposes(n_tr)
                down(FK, lambda: transposes(n_tr))

            def ada_slot(k, layer):
                c, hf = k // 2, k % 2
                s = pos[0]
                pos[0] += 1
                if hf and c:
                    ada_turn(c - 1, layer)
                wait_lo(pe, s)
                if hf == 0 and 12 * layer + c - 1 > 0:
                    pe.wait_ge(sem("ada_taken"), 12 * layer + c - 1)
                for kk in range(4):
                    for n, w in enumerate((whi, wlo)):
                        m = pe.matmul(ps[0:2, 4 + c % 2, :], c2[:, 4 * hf + kk, :], w[:, s % SPL, kk * W:(kk + 1) * W],
                                      start=hf == kk == n == 0, stop=hf == 1 and kk == 3 and n == 1)
                m.then_inc(sem("w_used"), 1)

            def ada_turn(c, layer):
                pe.wait_ge(sem("ada_row"), 12 * layer + c + 1)
                for j in range(4):
                    m = pe.matmul(ps[:, 4 + c % 2, j:j + 1], arow[:, c % 2, j * P:(j + 1) * P], ones[0:2, 0:1],
                                  start=True, stop=True)
                m.then_inc(sem("ada_cols"), 1)

            def broadcast_gates():
                pe.wait_ge(sem("gwide"), T.up("gwide"))
                pe.wait_ge(sem("acc_free"), T("acc"))
                for m_ in range(2 * KT):
                    m = pe.matmul(ps[:, m_ // 4, m_ % 4 * P:(m_ % 4 + 1) * P], gwide[:, m_, :], ident[:, :], start=True, stop=True)
                m.then_inc(sem("gates_psum"), 1)

            def attention(units, ada=None):
                for a in ("s", "n", "pt", "pv", "oc"):
                    T.n.setdefault("att_" + a, 0)
                b = {a: T.n["att_" + a] for a in ("s", "n", "pt", "pv", "oc")}
                U = [(a, t) for a in units for t in range(NT)]

                def scores(u):
                    a, t = U[u]
                    nk = (t + 1) * P
                    if u >= 2:
                        pe.wait_ge(sem("att_a"), b["s"] + u - 1)
                    r0 = a["h"] % 2 * DH
                    o = ps[:, u % 2, 0:nk]
                    m = pe.matmul(o, qT[r0:r0 + DH, a["q"], t * P:(t + 1) * P], kT[r0:r0 + DH, a["k"], 0:nk],
                                  start=True, stop=a["mask"] != "fox")
                    if a["mask"] == "fox":
                        m = pe.matmul(o, sel8[:, a["h"], :], ncT[:, 0:nk], start=False, stop=True)
                    m.then_inc(sem("att_s"), 1)

                def turn(u):
                    a, t = U[u]
                    pe.wait_ge(sem("att_n"), b["n"] + u + 1)
                    if u >= 2:
                        pe.wait_ge(sem("att_c"), b["pt"] + u - 1)
                    for kk in range(t + 1):
                        m = pe.transpose(ps[:, 6 + u % 2, kk * P:(kk + 1) * P], pr[:, u % 4, kk * P:(kk + 1) * P],
                                         ident[:, :])
                    m.then_inc(sem("att_pt"), 1)

                def values(u):
                    a, t = U[u]
                    pe.wait_ge(sem("att_c"), b["pt"] + u + 1)
                    p_ = a["h"] // 2
                    if u % 4 == 0 and p_ >= 2:
                        pe.wait_ge(sem("att_o"), b["oc"] + p_ - 1)
                    r0 = a["h"] % 2 * DH
                    for kk in range(t + 1):
                        m = pe.matmul(ps[r0:r0 + DH, 2 + p_ % 2, t * P:(t + 1) * P], v_of(a, kk),
                                      pT[:, u % 2, kk * P:(kk + 1) * P], start=kk == 0, stop=kk == t)
                    m.then_inc(sem("att_pv"), 1)

                n = len(U)
                for i in range(n + 4):
                    if i < n:
                        scores(i)
                    if 0 <= i - 3 < n:
                        turn(i - 3)
                    if ada is not None:
                        for k in ada_due(i):
                            ada_slot(k, ada)
                    if 0 <= i - 4 < n:
                        values(i - 4)
                if ada is not None:
                    ada_turn(ADA // 2 - 1, ada)
                for a in ("s", "n", "pt", "pv"):
                    T.up("att_" + a, n)
                T.up("att_oc", NH // 2)
                pe.wait_ge(sem("att_o"), T("att_oc"))

            pe.wait_ge(sem("consts"), 1)
            pe.wait_ge(sem("ws_landed"), 16)
            for g in range(KT):
                m = pe.transpose(ps[:, g // 4, (g % 4) * P:(g % 4 + 1) * P], ws[:, g, :], ident[:, :])
            m.then_inc(sem("wsT_psum"), 1)
            norm_tail(TA)
            x_ready()
            pe.wait_ge(sem("wsT_ready"), 1)
            for c in range(4):
                proj(c % 3, W)
            pe.wait_ge(sem("vn_ready"), NT)
            pe.wait_ge(sem("wsT_ready"), 2)
            pe.wait_ge(sem("acc_free"), 4)
            for g in range(KT):
                pe.matmul(ps[:, g // 2, (g % 2) * S:(g % 2 + 1) * S].rearrange("p (t c) -> p t c", t=NT),
                          wsT[:, g, :], TB[:, :, g * P:(g + 1) * P], start=True, stop=True).then_inc(sem("spatial"), 1)
            pe.wait_ge(sem("gz_ready"), KT)
            tail(TA)
            x_ready()
            for c in range(2):
                proj(c, W, early=c)
            norm_tail(TA)
            gated_ffn(4)
            norm_tail(TA)
            x_ready()
            for c in range(4):
                proj(c % 3, W, back=2 if c else 0)
            tail(TA)
            x_ready()
            for c in range(2):
                proj(1 + c, W)
            pe.wait_ge(sem("acc_free"), T("acc"))
            rounds([(lambda t, k=k: TB[:, t, k * P:(k + 1) * P]) for k in range(KT)])
            rounds([(lambda t, k=k: TA[:, t, k * P:(k + 1) * P]) for k in range(KT)])
            pe.wait_ge(sem("tr_free"), T("tr"))
            pe.wait_ge(sem("c_ready"), 1)
            attention(CHUNKED, 0)
            for c in range(2):
                proj(c, W, back=c, early=c)
            norm_tail(TA)
            gated_ffn(4)

            norm_tail(TA)
            broadcast_gates()
            x_ready()
            pe.wait_ge(sem("gates_ready"), 1)
            for n, (_, w) in enumerate(chunks_of(E_IN, E_ORDER)):
                proj(n % 3, w, back=0 if n == 0 else 2)
            pe.wait_ge(sem("acc_free"), T("acc"))
            pe.wait_ge(sem("logf"), 1)
            lgt = lgf[:, 4]
            pe.matmul(ps[:, 0, 0:8], tri[:, :], lgt[:, 0, :], start=True, stop=True)
            pe.matmul(ps[:, 0, 8:16], ones[:, :], lgt[:, 0, :], start=True, stop=False)
            pe.matmul(ps[:, 0, 8:16], tri[:, :], lgt[:, 1, :], start=False, stop=True)
            pe.matmul(ps[0:8, 1, 0:P], lgt[:, 0, :], tri[:, :], start=True, stop=True)
            pe.matmul(ps[0:8, 1, P:S], lgt[:, 0, :], ones[:, :], start=True, stop=False)
            pe.matmul(ps[0:8, 1, P:S], lgt[:, 1, :], tri[:, :], start=False, stop=True).then_inc(sem("cum_psum"), 1)
            pe.wait_ge(sem("kd_ready"), 1)
            tile_of = lambda c: (lambda t: te[:, t, c:c + P])
            rounds([tile_of(n * P) for n in range(4)] + [tile_of(1544 + n * P) for n in range(4)])
            rounds([tile_of(512 + n * P) for n in range(4)]
                   + [(lambda t, j=j: kd[:, t, j].rearrange("p c d -> p (c d)")) for j in range(2)])
            pe.wait_ge(sem("tr_free"), T("tr"))
            pe.wait_ge(sem("cum_ready"), 2)
            pe.wait_ge(sem("sel_ready"), 1)
            attention(EVEN, 1)
            for c in range(2):
                proj(c, W, back=c, early=c)
            norm_tail(TA)
            gated_ffn(2)
            norm_tail(TA)
            broadcast_gates()
            x_ready()
            pe.wait_ge(sem("gates_ready"), 2)
            width = [w for _, w in chunks_of(O_IN, O_ORDER)]
            for n in range(3):
                proj(n, width[n], back=0 if n == 0 else 2)
            tile_of = lambda c: (lambda t: to[:, t, c:c + P])
            pe.wait_ge(sem("kd_ready"), 2)
            rounds([tile_of(1536 + n * P) for n in range(4)] + [lambda t: ikd[:, t].rearrange("p c d -> p (c d)")])
            proj(0, width[3])
            pe.wait_ge(sem("tr_free"), T("tr"))
            pe.wait_ge(sem("acc_free"), T("acc", 1))
            for u in range(16):
                t, ih = u // 8, u % 8
                if u >= 4:
                    pe.wait_ge(sem("ix_read"), u - 3)
                r0 = ih % 2 * DH
                pe.matmul(ps[:, 2 + u % 4, 0:(t + 1) * P], iqT[r0:r0 + DH, ih // 2, t * P:(t + 1) * P],
                          ikT[r0:r0 + DH, 0:(t + 1) * P], start=True, stop=True).then_inc(sem("ix_psum"), 1)
            pe.wait_ge(sem("ix_read"), 14)
            proj(1, width[4])
            pe.wait_ge(sem("rope_done"), 3)
            rounds([tile_of(n * P) for n in range(8)])
            pe.wait_ge(sem("kd_ready"), 3)
            rounds([(lambda t, j=j: kd[:, t, j].rearrange("p c d -> p (c d)")) for j in range(4)])
            pe.wait_ge(sem("tr_free"), T("tr"))
            pe.wait_ge(sem("acc_free"), T("acc"))
            attention(ODD)
            for c in range(2):
                proj(c, W, back=c, early=c)
            norm_tail(TA)
            pe.wait_ge(sem("tr_free"), T("tr"))
            pe.wait_ge(sem("acc_free"), T("acc"))
            for t in range(NT):
                for k in range(KT):
                    m = pe.matmul(ps[:, 5, t * NE:(t + 1) * NE], xT_c[:, k, t * P:(t + 1) * P], rw[:, k, :],
                                  start=k == 0, stop=k == KT - 1)
            m.then_inc(sem("router"), 1)
            pe.wait_ge(sem("logits_taken"), 1)
            pe.wait_ge(sem("member"), 1)
            pe.matmul(ps[:, 5, 32:32 + NE], tri[:, :], member[:, 0, :], start=True, stop=True)
            pe.matmul(ps[:, 5, 40:40 + NE], ones[:, :], member[:, 0, :], start=True, stop=False)
            pe.matmul(ps[:, 5, 40:40 + NE], tri[:, :], member[:, 1, :], start=False, stop=True)
            pe.matmul(ps[:, 5, 48:48 + NE], ones[:, :], member[:, 0, :], start=True, stop=False)
            pe.matmul(ps[:, 5, 48:48 + NE], ones[:, :], member[:, 1, :], start=False, stop=True).then_inc(sem("ranks"), 1)
            T.n.update(x_acc=0, x_tr=0, x_g=0, x_y=0, x_s=0, x_a=0, x_gt=0)

            def gather():
                pe.wait_ge(sem("places"), T.up("x_g"))
                pe.wait_ge(sem("g_taken"), T("x_g"))
                for b in range(2):
                    for k in range(4):
                        for t in range(NT):
                            m = pe.matmul(ps[:, 5 + 2 * b, k * P:(k + 1) * P], TA[:, t, (4 * b + k) * P:(4 * b + k + 1) * P],
                                          G[:, t, :], start=t == 0, stop=t == NT - 1)
                    m.then_inc(sem("g_psum"), 1)

            def turn_places():
                for t in range(NT):
                    m = pe.transpose(ps[:, 2, t * P:(t + 1) * P], G[:, t, :], ident[:, :])
                m.then_inc(sem("gt_psum"), 1)
                T.up("x_gt")

            def scatter():
                pe.wait_ge(sem("y_copied"), T.up("x_y"))
                for n in range(2):
                    for t in range(NT):
                        b = (5, 7, 3, 4)[2 * n + t]
                        pe.matmul(ps[:, b, :], GT[:, t, :], yhi[:, 4 * n:4 * n + 4, :], start=True, stop=False)
                        m = pe.matmul(ps[:, b, :], GT[:, t, :], ylo[:, 4 * n:4 * n + 4, :], start=False, stop=True)
                    m.then_inc(sem("y_psum"), 1)

            def hidden(j, i):
                w = W if j < 5 else 256
                if j == 3:
                    pe.wait_ge(sem("gt_copied"), T("x_gt"))
                for hf in range(2):
                    s = pos[0]
                    pos[0] += 1
                    wait_lo(pe, s, i, EXP)
                    wh = whi[:, s % SPL, 0:4 * w].rearrange("p (k n) -> p k n", k=4)
                    wl = wlo[:, s % SPL, 0:4 * w].rearrange("p (k n) -> p k n", k=4)
                    for k in range(4):
                        kk = 4 * hf + k
                        m = mm3(ps[:, (2, 0, 1)[j % 3], 0:w], xhi[:, kk, 0:P], xlo[:, kk, 0:P], wh[:, k, :], wl[:, k, :],
                                kk == 0, kk == KT - 1)
                    m.then_inc(sem("w_used"), 1)

            def turn(j):
                pe.wait_ge(sem("x_tok"), T.up("x_acc") + 1)
                pe.wait_ge(sem("x_tr_free"), T("x_tr", -1))
                for f in range(2 if j < 5 else 1):
                    m = pe.transpose(ps[:, 6, f * P:(f + 1) * P], abx[:, j % 2, f * P:(f + 1) * P], ident[:, :])
                m.then_inc(sem("x_tr"), 1)
                T.up("x_tr")

            def out_of(i):
                for j in range(6):
                    if j == 2:
                        turn(5)
                    s = pos[0]
                    pos[0] += 1
                    pe.wait_ge(sem("x_a"), T.up("x_a"))
                    wait_lo(pe, s, i, EXP)
                    for k in range(2 * j, min(2 * j + 2, FE // P)):
                        for n in range(2):
                            a = (k - 2 * j) * D + n * W
                            m = mm3(ps[:, 3 + n, :], ahi[:, k, 0:P], alo[:, k, 0:P], whi[:, s % SPL, a:a + W],
                                    wlo[:, s % SPL, a:a + W], k == 0, k == FE // P - 1)
                    m.then_inc(sem("w_used"), 1)

            gather()
            with pe.Fori(0, NE) as i:
                T.loop(i, x_acc=6, x_tr=6, x_g=1, x_y=1, x_a=6, x_s=1, x_gt=1)
                pe.wait_ge(sem("xg_ready"), T.up("x_s"))
                hidden(0, i)
                scatter()
                hidden(1, i)
                turn(0)
                turn_places()
                for j in range(2, 6):
                    hidden(j, i)
                    if j == 5:
                        pe.wait_ge(sem("y_added"), T("x_y"))
                        gather()
                    turn(j - 1)
                out_of(i)
                T.end(NE)
            pos[0] += EXP * (NE - 1)
            scatter()
            wait_lo(pe, AT["more"] - 1)
            pe.drain()
            pe.sem_inc(sem("w_used"), AHEAD)
            pos[0] += AHEAD
            pe.wait_ge(sem("counted"), 1)
            most = pe.value_load(count[0:1, NE:NE + 1])
            with pe.If(most > P):
                with pe.Fori(0, NE) as i:
                    T.loop(i, x_acc=6, x_tr=6, x_g=1, x_y=1, x_a=6, x_s=1, x_gt=1)
                    n = pe.value_load(count[0:1, bass.ds(i, 1)])
                    with pe.If(n > P):
                        pe.wait_ge(sem("y_added"), T("x_y"))
                        gather()
                        pe.wait_ge(sem("xg_ready"), T.up("x_s"))
                        for j in range(6):
                            hidden(j, i)
                            if j:
                                turn(j - 1)
                            if j == 1:
                                turn_places()
                        out_of(i)
                        scatter()
                    with pe.Else():
                        pe.drain()
                        for name, k in (("g_psum", 2), ("x_tr", 6), ("gt_psum", 1), ("w_used", EXP), ("y_psum", 2)):
                            pe.sem_inc(sem(name), k)
                    T.end(NE)

            with pe.Else():
                pe.drain()
                pe.sem_inc(sem("y_psum"), 2 * NE)
        @block.scalar
        def _(act):
            T = Tally()
            act.dma_start(ws, ws_in.rearrange("o g i j -> i (o g) j")).then_inc(sem("ws_landed"), 16)
            act.dma_start(gates[:, 0, :], fg1_in.to_broadcast([P, D])).then_inc(sem("fg1_landed"), 16)
            act.dma_start(vg, vg_in.to_broadcast([P, D])).then_inc(sem("consts_landed"), 16)
            act.dma_start(rows[:, :], rows_in.to_broadcast([P, R_END])).then_inc(sem("consts_landed"), 16)
            act.dma_start(posi[:, :], pos_in).then_inc(sem("consts_landed"), 16)
            act.dma_start(rw[:, :, :], rw_in.rearrange("(k p) e -> p k e", p=P)).then_inc(sem("consts_landed"), 16)
            pos = [0]
            used = [0]

            top = [AT["end"]]

            def split(n, i=None, per=0):
                while pos[0] < min(n, top[0]):
                    s = pos[0]
                    pos[0] += 1
                    w = plan[s][0]
                    step = LANDED[s + per] - LANDED[s] if i is not None else 0
                    act.wait_ge(sem(f"landed{s % RAW}"), LANDED[s] if i is None else i * step + LANDED[s])
                    if s >= SPL:
                        act.wait_ge(sem("w_used"), s - SPL + 1 if i is None else i * per + (s - SPL + 1))
                    act.activation(whi[:, s % SPL, 0:w], raw[:, s % RAW, 0:w], ACT.Copy).then_inc(sem("hi_done"), 1)

            def chunk(i=None, per=0):
                used[0] += 2
                split(used[0] + AHEAD, i, per)
                act.wait_ge(sem("w_used"), used[0] if i is None else i * per + used[0])

            def stats(src, added=True):
                act.activation(st[:, 26:27], ones[:, 0:1], ACT.Sqrt)
                for t in range(NT):
                    if added:
                        act.wait_ge(sem("h_added"), T.up("h_added"))
                    if t:
                        act.wait_ge(sem("sq"), T("sq"))
                    T.up("sq")
                    act.activation(ps[:, 6:8, :], src[:, t, :].rearrange("p (a b) -> p a b", a=2),
                                   ACT.Square, accum_out=st[:, t:t + 1]).then_inc(sem("sq"), 1)
                for t in range(NT):
                    act.wait_ge(sem("ms"), T.up("ms"))
                    act.activation(st[:, 4 + t:5 + t], st[:, 2 + t:3 + t], ACT.Sqrt).then_inc(sem("rms"), 1)

            def tail(dst, scale=None, shift=None):
                for r in range(4):
                    act.wait_ge(sem("tr"), T.up("tr"))
                    if scale is None:
                        act.activation(dst[:, 2 * r:2 * r + 2, :], trb(r % 2), ACT.Copy).then_inc(sem("tr_free"), 1)
                        continue
                    for j in range(2):
                        k = 2 * r + j
                        kw = {} if shift is None else dict(bias=shift[:, k:k + 1])
                        m = act.activation(dst[:, k, :], trb(r % 2)[:, j, :], ACT.Identity, scale=scale[:, k:k + 1], **kw)
                    m.then_inc(sem("tr_free"), 1)

            def copies(dsts, scale=1.0):
                for r, d in enumerate(dsts):
                    act.wait_ge(sem("tr"), T.up("tr"))
                    src = trb(r % 2) if d.shape[1] == 2 else trb(r % 2)[:, 0:1, :]
                    act.activation(d, src, ACT.Copy, scale=scale).then_inc(sem("tr_free"), 1)

            def take(n, dst, func=ACT.Copy, w=W, scale=1.0):
                chunk()
                act.activation(dst, pair(n, w), func, scale=scale).then_inc(sem("acc_free"), 1)

            def residual():
                for _ in range(2):
                    used[0] += 2
                    split(used[0] + AHEAD)
                T.up("acc", 2)

            def down(kt, i=None, per=0):
                used[0] += (kt + 1) // 2
                split(used[0] + AHEAD, i, per)

            def conv_ffn(layer):
                n = FK // 2
                cw = C_CW + layer * 3 * 2 * FK
                cb = C_CB + layer * 2 * FK

                def evac(pr_, i=None, first=False):
                    chunk(i, 6)
                    if not first:
                        act.wait_ge(sem("tr"), T("tr", -1))
                    act.activation(ab, pair(pr_), ACT.Copy).then_inc(sem("tok_ready"), 1)

                def convolve(j, i=None):
                    act.wait_ge(sem("tr"), T.up("tr"))
                    act.wait_ge(sem("conv_used"), T("conv_used"))
                    for f in range(4):
                        c = (f % 2) + (f // 2) * FK + 2 * j
                        if i is None:
                            sc, bi = cols[:, cw + 4 * FK + c:cw + 4 * FK + c + 1], cols[:, cb + c:cb + c + 1]
                        else:
                            sc, bi = cols[:, bass.ds(i * 6 + (cw + 4 * FK + c), 1)], cols[:, bass.ds(i * 6 + (cb + c), 1)]
                        m = act.activation(conv[:, f, :], ps[:, 6 + f // 2, (f % 2) * S:(f % 2 + 1) * S], ACT.Identity,
                                           scale=sc, bias=bi)
                    m.then_inc(sem("conv_a"), 1)
                    act.wait_ge(sem("conv_b"), T.up("conv_b"))
                    act.activation(sg, conv[:, 2:4, :], ACT.Silu).then_inc(sem("silu"), 1)
                    T.up("conv_used")

                evac(2, first=True)
                turns = (n - 2) // 3
                with act.Fori(0, turns) as i:
                    T.loop(i, tr=3, conv_b=3, conv_used=3)
                    for j in range(3):
                        evac(j, i)
                        convolve(j, i)
                    T.end(turns)
                pos[0] += 6 * (turns - 1)
                used[0] += 6 * (turns - 1)
                evac(0)
                convolve(n - 2)
                split(used[0] + 4)
                convolve(n - 1)
                down(FK)

            def evac_gated(pr_, m, i=None, per=0):
                chunk(i, per)
                if T.n.get("sg_used", 0):
                    act.wait_ge(sem("sg_used"), T("sg_used"))
                act.activation(sg[:, :, 0:m], pair(pr_, 2 * m)[:, :, m:2 * m], ACT.Silu).then_inc(sem("silu"), 1)
                T.up("sg_used")

            def gated_ffn():
                n = FK // 2
                evac_gated(2, 256)
                turns = (n - 2) // 3
                with act.Fori(0, turns) as i:
                    T.loop(i, sg_used=3)
                    for j in range(3):
                        evac_gated(j, 256, i, 6)
                    T.end(turns)
                pos[0] += 6 * (turns - 1)
                used[0] += 6 * (turns - 1)
                evac_gated(0, 256)
                down(FK)
                T.up("tr", n)

            def ada_row(k, layer):
                c = k // 2
                act.wait_ge(sem("w_used"), used[0] + k + 1)
                if 12 * layer + c >= 2:
                    act.wait_ge(sem("ada_cols"), 12 * layer + c - 1)
                act.activation(arow[:, c % 2, :], ps[0:2, 4 + c % 2, :], ACT.Copy).then_inc(sem("ada_row"), 1)

            def attention(units, ada=None):
                U = [(a, t) for a in units for t in range(NT)]
                b = T.n.get("att", 0)

                def exps(u):
                    a, t = U[u]
                    act.wait_ge(sem("att_m"), b + u + 1)
                    nk = (t + 1) * P
                    m = act.activation(pr[:, u % 4, 0:nk], sm[:, u % 4, 0:nk], ACT.Exp, bias=neg_max(u), accum_out=total(u))
                    if a["mask"] == "swa":
                        c = R_SK + a["h"] - 8
                        m = act.activation(sink(u), rows[:, c:c + 1], ACT.Exp, bias=neg_max(u))
                    m.then_inc(sem("att_e"), 1)

                def copy(u):
                    a, t = U[u]
                    act.wait_ge(sem("att_pt"), b + u + 1)
                    if u >= 2:
                        act.wait_ge(sem("att_pv"), b + u - 1)
                    nk = (t + 1) * P
                    act.activation(pT[:, u % 2, 0:nk], ps[:, 6 + u % 2, 0:nk], ACT.Copy).then_inc(sem("att_c"), 1)

                n = len(U)
                for i in range(n + 3):
                    if ada is not None and i and ada_due(i - 1):
                        split(used[0] + ada_due(i - 1).stop + AHEAD)
                    if i < n:
                        exps(i)
                    if 0 <= i - 3 < n:
                        copy(i - 3)
                    if ada is not None:
                        for k in ada_due(i - 1) if i else ():
                            if k % 2:
                                ada_row(k, ada)
                T.up("att", n)
                if ada is not None:
                    used[0] += ADA

            T.up("conv_used")
            act.wait_ge(sem("consts"), 1)
            act.wait_ge(sem("x_landed"), 16)
            stats(h, False)
            split(2)
            act.wait_ge(sem("wsT_psum"), 1)
            act.activation(wsT.rearrange("p (b g) i -> p b (g i)", b=2), ps[:, 0:2, :], ACT.Copy).then_inc(sem("wsT_ready"), 1)
            act.wait_ge(sem("cols_landed"), 16)
            tail(xT_c, cols[:, C_GA:C_GA + KT])
            for n in range(4):
                dst = (TB if n < 2 else TA)[:, :, (n % 2) * W:(n % 2 + 1) * W]
                take(n % 3, dst, ACT.Gelu_apprx_tanh)
                T.up("acc")
                if n == 1:
                    act.wait_ge(sem("consts_landed"), 16 * 4)
                    act.wait_ge(sem("angle"), 1)
                    for table, k in ((sinT, 1), (cosT, 3)):
                        act.activation(table[:, :, :].rearrange("p t f -> p (t f)"), rot[:, k, :], ACT.Sin).then_inc(sem("tables"), 1)
                    act.activation(cs[:, :], cols[:, C_C:C_C + KT], ACT.Silu).then_inc(sem("cs"), 1)
                    act.wait_ge(sem("acc_free"), 2)
                    stats(TB, False)
            tail(xT_c)
            residual()
            stats(h)
            tail(xT_c, cols[:, C_GF0:C_GF0 + KT])
            conv_ffn(0)
            stats(h)
            tail(xT_c, cols[:, C_GKV:C_GKV + KT])
            for n in range(4):
                dst = (TB if n < 2 else TC)[:, :, (n % 2) * W:(n % 2 + 1) * W]
                take(n % 3, dst)
            tail(xT_b, cols[:, C_GB:C_GB + KT])
            for n in range(2):
                take(1 + n, TA[:, :, n * W:(n + 1) * W])
            copies([kT[:, 2 * r:2 * r + 2, :] for r in range(4)])
            copies([qT[:, 2 * r:2 * r + 2, :] for r in range(4)], scale=DH ** -0.5)
            attention(CHUNKED, 0)
            residual()
            stats(h)
            tail(xT_c, cols[:, C_GF1:C_GF1 + KT])
            conv_ffn(1)
            stats(h)

            def take_gates():
                act.wait_ge(sem("gates_psum"), T.up("gates_psum"))
                act.activation(gates[:, :, :].rearrange("p m (n c) -> p (m n) c", c=W), ps[:, 0:4, :], ACT.Copy)\
                    .then_inc(sem("gates_ready"), 1)

            act.wait_ge(sem("h_normed"), NT)
            stats(h, False)
            tail(xT_c, scl2[:, 0, 0, :], shf2[:, 0, 0, :])
            take_gates()
            for n, (c, w) in enumerate(chunks_of(E_IN, E_ORDER)):
                take(n % 3, te[:, :, c:c + w], w=w)
                if n == 1:
                    act.wait_ge(sem("lgf"), 1)
                    act.activation(lgf[:, 1], lgf[:, 2], ACT.Exp, scale=-1.0).then_inc(sem("lgf_act"), 1)
                    act.wait_ge(sem("lgf"), 2)
                    act.activation(lgf[:, 3], lgf[:, 2], ACT.Ln).then_inc(sem("lgf_act"), 1)
                if n == 3:
                    act.wait_ge(sem("rope_done"), 1)
                    for half in range(2):
                        m = act.activation(kd[:, :, 0:2, half, :], te[:, :, 2056:2184].rearrange("p t (j d) -> p t j d", j=2), ACT.Copy)
                    m.then_inc(sem("kd_ready"), 1)
            copies([qT[:, 2 * r:2 * r + 2, :] for r in range(4)], scale=DH ** -0.5)
            copies([kT[:, 2 * r:2 * r + 2, :] for r in range(3)])
            attention(EVEN, 1)
            residual()
            stats(h)
            tail(xT_c, scl2[:, 0, 1, :], shf2[:, 0, 1, :])
            gated_ffn()
            stats(h)
            tail(xT_c, scl2[:, 1, 0, :], shf2[:, 1, 0, :])
            take_gates()
            for n, (c, w) in enumerate(chunks_of(O_IN, O_ORDER)):
                take(n % 3 if n < 4 else 1, to[:, :, c:c + w], w=w)
                if n == 1:
                    act.wait_ge(sem("rope_done"), 2)
                    act.activation(ikd[:, :, 0, :], to[:, :, 2048:2112], ACT.Copy)
                    act.activation(ikd[:, :, 1, :], to[:, :, 2048:2112], ACT.Copy).then_inc(sem("kd_ready"), 1)
                if n == 2:
                    copies([iqT[:, 0:2, :], iqT[:, 2:4, :], ikT.unsqueeze(1)])
                if n == 3:
                    for u in range(16):
                        t = u // 8
                        act.wait_ge(sem("ix_psum"), u + 1)
                        if u >= 2:
                            act.wait_ge(sem("ix_added"), u - 1)
                        act.activation(relu[:, u % 2, 0:(t + 1) * P], ps[:, 2 + u % 4, 0:(t + 1) * P], ACT.Relu)\
                            .then_inc(sem("ix_read"), 1)
            copies([qT[:, 2 * r:2 * r + 2, :] for r in range(4)], scale=DH ** -0.5)
            act.wait_ge(sem("rope_done"), 4)
            for half in range(2):
                m = act.activation(kd[:, :, :, half, :], to[:, :, 1024:1280].rearrange("p t (j d) -> p t j d", j=4), ACT.Copy)
            m.then_inc(sem("kd_ready"), 1)
            copies([kT[:, 2 * r:2 * r + 2, :] for r in range(2)])
            attention(ODD)
            residual()
            stats(h)
            tail(xT_c, scl2[:, 1, 1, :], shf2[:, 1, 1, :])
            act.wait_ge(sem("g2"), 1)
            act.activation(g2[:, :, 1], g2[:, :, 0], ACT.Exp).then_inc(sem("g2_act"), 1)
            T.n.update(x_tr=0, x_g=0, x_y=0, x_sg=0, x_gt=0)

            def take_gathered(between=lambda: None):
                for b in range(2):
                    if b:
                        between()
                    act.wait_ge(sem("g_psum"), T.up("x_g"))
                    for k in range(4):
                        kk = 4 * b + k
                        m = act.activation(xg[:, kk, :], ps[:, 5 + 2 * b, k * P:(k + 1) * P], ACT.Identity,
                                           scale=scl2[:, 1, 1, kk:kk + 1], bias=shf2[:, 1, 1, kk:kk + 1])
                    m.then_inc(sem("xg"), 1)

            def silu(j, i):
                m = 256 if j < 5 else P
                used[0] += 2
                split(used[0] + AHEAD, i, EXP)
                act.wait_ge(sem("w_used"), i * EXP + used[0])
                act.wait_ge(sem("x_tok"), T("x_sg", -1))
                act.activation(sgx[:, 0:m], ps[:, (2, 0, 1)[j % 3], m:2 * m], ACT.Silu).then_inc(sem("x_silu"), 1)
                T.up("x_sg")

            def places():
                act.wait_ge(sem("gt_psum"), T.up("x_gt"))
                act.activation(GT, ps[:, 2, 0:S].rearrange("p (t i) -> p t i", t=NT), ACT.Copy).then_inc(sem("gt_copied"), 1)

            def hi_of(j):
                f = 2 if j < 5 else 1
                act.wait_ge(sem("x_tr"), T.up("x_tr"))
                act.activation(ahi[:, 2 * j:2 * j + f, 0:P], ps[:, 6, 0:f * P].rearrange("p (f s) -> p f s", f=f), ACT.Copy)\
                    .then_inc(sem("x_hi"), 1)

            def output(i):
                used[0] += 6
                split(used[0] + AHEAD, i, EXP)
                act.wait_ge(sem("w_used"), i * EXP + used[0])
                act.wait_ge(sem("y_psum"), T("x_y", -2))
                act.activation(yhi, ps[:, 3:5, :].rearrange("p n (k c) -> p (n k) c", c=P), ACT.Copy).then_inc(sem("y_hi"), 1)
                T.up("x_y", 2)

            take_gathered()
            with act.Fori(0, NE) as i:
                T.loop(i, x_tr=6, x_g=2, x_y=2, x_sg=6, x_gt=1)
                for j in range(6):
                    silu(j, i)
                    if j > 0:
                        hi_of(j - 1)
                    if j == 1:
                        places()
                split(used[0] + 3, i, EXP)
                take_gathered(lambda: split(used[0] + 4, i, EXP))
                hi_of(5)
                output(i)
                T.end(NE)
            pos[0] += EXP * (NE - 1)
            used[0] += EXP * (NE - 1) + AHEAD
            assert pos[0] == used[0] == AT["more"]
            act.wait_ge(sem("counted"), 1)
            most = act.value_load(count[0:1, NE:NE + 1])
            with act.If(most > P):
                with act.Fori(0, NE) as i:
                    T.loop(i, x_tr=6, x_g=2, x_y=2, x_sg=6, x_gt=1)
                    n = act.value_load(count[0:1, bass.ds(i, 1)])
                    with act.If(n > P):
                        top[0] = used[0] + EXP
                        take_gathered()
                        for j in range(6):
                            silu(j, i)
                            if j > 0:
                                hi_of(j - 1)
                            if j == 1:
                                places()
                        split(used[0] + 4, i, EXP)
                        hi_of(5)
                        output(i)
                    with act.Else():
                        act.drain()
                        for name, k in (("xg", 2), ("hi_done", EXP), ("x_silu", 6), ("gt_copied", 1), ("x_hi", 6), ("y_hi", 1)):
                            act.sem_inc(sem(name), k)
                    T.end(NE)
            stats(h)

        @block.vector
        def _(dve):
            T = Tally()
            pos = [0]
            used = [0]

            def link(ins):
                ins.then_inc(sem("dve"), 1)
                dve.wait_ge(sem("dve"), T.up("dve"))

            top = [AT["end"]]

            def split(n, i=None, per=0):
                while pos[0] < min(n, top[0]):
                    s = pos[0]
                    pos[0] += 1
                    w = plan[s][0]
                    if lo_made(s)[0] == "pool_lo":
                        continue
                    dve.wait_ge(sem("hi_done"), s + 1 if i is None else i * per + (s + 1))
                    dve.tensor_tensor(wlo[:, s % SPL, 0:w], raw[:, s % RAW, 0:w], whi[:, s % SPL, 0:w].bitcast(F32),
                                      ALU.subtract).then_inc(sem("lo_done"), 1)

            def chunk(i=None, per=0, wait=True):
                used[0] += 2
                split(used[0] + AHEAD, i, per)
                if wait:
                    dve.wait_ge(sem("w_used"), used[0] if i is None else i * per + used[0])

            def normalise(src, dst, gain=None, name="xn"):
                for t in range(NT):
                    dve.wait_ge(sem("sq"), T.up("sq"))
                    dve.tensor_scalar(st[:, 2 + t:3 + t], st[:, t:t + 1], 1.0 / D, EPS, ALU.mult, ALU.add).then_inc(sem("ms"), 1)
                for t in range(NT):
                    dve.wait_ge(sem("rms"), T.up("rms"))
                    link(dve.reciprocal(st[:, 6 + t:7 + t], st[:, 4 + t:5 + t]))
                    if gain is None:
                        m = dve.tensor_scalar(dst[:, t, :], src[:, t, :], st[:, 6 + t:7 + t], None, ALU.mult)
                    else:
                        m = dve.scalar_tensor_tensor(dst[:, t, :], src[:, t, :], st[:, 6 + t:7 + t], gain, ALU.mult, ALU.mult)
                    m.then_inc(sem(name), 1)

            def tail(src):
                if used[0]:
                    dve.wait_ge(sem("w_used"), used[0])
                for r in range(4):
                    dve.wait_ge(sem("tr_free"), T.up("tr"))
                    x = src[:, 2 * r:2 * r + 2, :]
                    link(dve.tensor_copy(xhi[:, 2 * r:2 * r + 2, :], x))
                    dve.tensor_tensor(xlo[:, 2 * r:2 * r + 2, :], x, xhi[:, 2 * r:2 * r + 2, :].bitcast(F32), ALU.subtract)\
                        .then_inc(sem("x_ready"), 1)

            def skip(n):
                for _ in range(n):
                    chunk(wait=False)

            def add_h(n, t, gate=None):
                hs = h[:, t, n * W:(n + 1) * W]
                if gate is None:
                    return dve.tensor_tensor(hs, ps[:, 2 * n + t, :], hs, ALU.add)
                tmp = TB[:, t, n * W:(n + 1) * W]
                link(dve.tensor_tensor(tmp, ps[:, 2 * n + t, :], gates[:, gate, n * W:(n + 1) * W], ALU.mult))
                return dve.tensor_tensor(hs, tmp, hs, ALU.add)

            def add_done():
                T.up("acc", 2)
                dve.wait_ge(sem("h_added"), T.up("h_added", NT))
                dve.sem_inc(sem("acc_free"), 2)

            def residual(gate=None):
                chunk()
                for t in range(NT):
                    add_h(0, t, gate)
                used[0] += 2
                split(used[0] + 1)
                for t in range(NT):
                    finished(t)
                    add_h(1, t, gate).then_inc(sem("h_added"), 1)
                add_done()

            def finished(t):
                if t == 0:
                    dve.wait_ge(sem("t0_done"), T.up("t0_done"))
                else:
                    dve.wait_ge(sem("w_used"), used[0])

            def down(kt, gate=None):
                used[0] += (kt + 1) // 2
                split(used[0] + 1)
                for t in range(NT):
                    finished(t)
                    for n in range(2):
                        m = add_h(n, t, gate)
                    m.then_inc(sem("h_added"), 1)
                add_done()

            def conv_ffn(layer):
                n = FK // 2
                cw = C_CW + layer * 3 * 2 * FK

                def convolve(j, i=None):
                    dve.wait_ge(sem("conv_a"), T.up("conv_a"))
                    for tap, d in ((1, 1), (0, 2)):
                        for f in range(4):
                            c = cw + tap * 2 * FK + (f % 2) + (f // 2) * FK + 2 * j
                            sc = cols[:, c:c + 1] if i is None else cols[:, bass.ds(i * 6 + c, 1)]
                            o = conv[:, f, d:S]
                            src = ps[:, 6 + f // 2, (f % 2) * S:(f % 2 + 1) * S - d]
                            m = dve.scalar_tensor_tensor(o, src, sc, o, ALU.mult, ALU.add)
                        if tap == 1:
                            link(m)
                        else:
                            m.then_inc(sem("conv_b"), 1)
                    dve.wait_ge(sem("conv_b"), T.up("conv_b"))
                    dve.sem_inc(sem("tr_free"), 1)
                    T.up("tr")
                    dve.wait_ge(sem("silu"), T.up("silu"))
                    m = dve.tensor_tensor(conv[:, 0:2, :], conv[:, 0:2, :], sg, ALU.mult)
                    link(m)
                    hi = ahi[:, 2 * j:2 * j + 2, :] if i is None else ahi[:, bass.ds(i * 6 + 2 * j, 2), :]
                    lo = alo[:, 2 * j:2 * j + 2, :] if i is None else alo[:, bass.ds(i * 6 + 2 * j, 2), :]
                    link(dve.tensor_copy(hi, conv[:, 0:2, :]))
                    dve.tensor_tensor(lo, conv[:, 0:2, :], hi.bitcast(F32), ALU.subtract).then_inc(sem("a_ready"), 1)
                    T.up("a_ready")
                    dve.wait_ge(sem("a_ready"), T("a_ready"))
                    dve.sem_inc(sem("conv_used"), 1)

                def evac(i=None):
                    chunk(i, 6, wait=False)
                    dve.wait_ge(sem("tok_ready"), T.up("tok_ready"))
                    dve.sem_inc(sem("acc_free"), 1)
                    T.up("acc")

                evac()
                turns = (n - 2) // 3
                with dve.Fori(0, turns) as i:
                    T.loop(i, tok_ready=3, conv_a=3, conv_b=3, silu=3, tr=3, dve=9, a_ready=3, acc=3)
                    for j in range(3):
                        evac(i)
                        convolve(j, i)
                    T.end(turns)
                pos[0] += 6 * (turns - 1)
                used[0] += 6 * (turns - 1)
                evac()
                convolve(n - 2)
                split(used[0] + 4)
                convolve(n - 1)
                down(FK)

            def turn_in(j, f, i=None):
                dve.wait_ge(sem("tr"), T.up("tr"))
                src = trb(0)[:, 0:f, :]
                hi = ahi[:, 2 * j:2 * j + f, :] if i is None else ahi[:, bass.ds(i * 6 + 2 * j, f), :]
                lo = alo[:, 2 * j:2 * j + f, :] if i is None else alo[:, bass.ds(i * 6 + 2 * j, f), :]
                link(dve.tensor_copy(hi, src))
                dve.tensor_tensor(lo, src, hi.bitcast(F32), ALU.subtract).then_inc(sem("a_ready"), 1)
                dve.wait_ge(sem("a_ready"), T.up("a_ready"))
                dve.sem_inc(sem("tr_free"), 1)

            def multiply(pr_, m, i=None, per=0, first=False):
                chunk(i, per, wait=False)
                dve.wait_ge(sem("silu"), T.up("silu"))
                if not first:
                    dve.wait_ge(sem("tr"), T("tr", -1))
                dve.tensor_tensor(ab[:, :, 0:m], pair(pr_, m), sg[:, :, 0:m], ALU.mult).then_inc(sem("tok_ready"), 1)
                dve.wait_ge(sem("tok_ready"), T.up("tok_ready"))
                dve.sem_inc(sem("acc_free"), 1)
                dve.sem_inc(sem("sg_used"), 1)
                T.up("acc")

            def gated_ffn(gate):
                n = FK // 2
                multiply(2, 256, first=True)
                turns = (n - 2) // 3
                with dve.Fori(0, turns) as i:
                    T.loop(i, tok_ready=3, silu=3, tr=3, dve=3, a_ready=3, acc=3)
                    for j in range(3):
                        multiply(j, 256, i, 6)
                        turn_in(j, 2, i)
                    T.end(turns)
                pos[0] += 6 * (turns - 1)
                used[0] += 6 * (turns - 1)
                multiply(0, 256)
                turn_in(n - 2, 2)
                split(used[0] + 4)
                turn_in(n - 1, 2)
                down(FK, gate)

            def ada_cols(c, layer):
                part, kind, half = c // 6, c // 2 % 3, 4 * (c % 2)
                dve.wait_ge(sem("ada_cols"), 12 * layer + c + 1)
                b0 = C_AB + layer * 6 * KT + c * 4
                dst = (shf2, scl2, gcol)[kind][:, layer, part, half:half + 4]
                m = dve.tensor_tensor(dst, ps[:, 4 + c % 2, 0:4], cols[:, b0:b0 + 4], ALU.add)
                if kind == 1:
                    link(m)
                    g0 = (C_GEM, C_GEF, C_GOM, C_GOF)[2 * layer + part] + half
                    m = dve.scalar_tensor_tensor(dst, dst, 1.0, cols[:, g0:g0 + 4], ALU.add, ALU.mult)
                m.then_inc(sem("ada_taken"), 1)

            def widen_gates(layer):
                dve.wait_ge(sem("ada_taken"), 12 * layer + 12)
                g = gcol[:, layer, :, :].rearrange("p m k -> p (m k)").unsqueeze(2).to_broadcast([P, 2 * KT, P])
                dve.tensor_copy(gwide, g).then_inc(sem("gwide"), 1)

            def attention(units, ada=None):
                U = [(a, t) for a in units for t in range(NT)]
                b = T.n.get("att", 0)

                def mask(u):
                    a, t = U[u]
                    nk = (t + 1) * P
                    lo_ = S - nk
                    dve.wait_ge(sem("att_s"), b + u + 1)
                    if u >= 4:
                        dve.wait_ge(sem("att_pt"), b + u - 3)
                    add = {"bias": lambda: bias[:, a["h"], lo_:S], "fox": lambda: causal[:, lo_:S],
                           "swa": lambda: window[:, lo_:S], "dsa": lambda: dsab[:, t, 0:nk]}[a["mask"]]()
                    o = sm[:, u % 4, 0:nk]
                    if a["mask"] == "fox":
                        m = dve.scalar_tensor_tensor(o, ps[:, u % 2, 0:nk], cum[:, t, a["h"]:a["h"] + 1], add, ALU.add, ALU.add)
                    else:
                        m = dve.tensor_tensor(o, ps[:, u % 2, 0:nk], add, ALU.add)
                    m.then_inc(sem("att_a"), 1)

                def maximum(u):
                    a, t = U[u]
                    dve.wait_ge(sem("att_a"), b + u + 1)
                    o = sm[:, u % 4, 0:(t + 1) * P]
                    nm = neg_max(u)
                    m = dve.tensor_reduce(nm, o, AXX, ALU.max, negate=True)
                    if a["mask"] == "swa":
                        link(m)
                        c = a["h"] - 8
                        m = dve.tensor_tensor(nm, nm, st[:, 16 + c:17 + c], ALU.min)
                    m.then_inc(sem("att_m"), 1)

                def invert(u):
                    dve.wait_ge(sem("att_e"), b + u + 1)
                    rs = total(u)
                    if U[u][0]["mask"] == "swa":
                        link(dve.tensor_tensor(rs, rs, sink(u), ALU.add))
                    dve.reciprocal(weight(u), rs).then_inc(sem("att_r"), 1)

                def weigh(u):
                    dve.wait_ge(sem("att_r"), b + u + 1)
                    o = pr[:, u % 4, 0:(U[u][1] + 1) * P]
                    dve.tensor_scalar(o, o, weight(u), None, ALU.mult).then_inc(sem("att_n"), 1)

                def gather(p_):
                    dve.wait_ge(sem("att_pv"), b + 4 * p_ + 4)
                    src = ps[:, 2 + p_ % 2, 0:S]
                    link(dve.tensor_copy(xhi[:, p_, :], src))
                    dve.tensor_tensor(xlo[:, p_, :], src, xhi[:, p_, :].bitcast(F32), ALU.subtract).then_inc(sem("att_o"), 1)

                n = len(U)
                for i in range(n + 5):
                    if ada is not None and i:
                        for k in ada_due(i - 1):
                            if k % 2 and k > 1:
                                ada_cols(k // 2 - 1, ada)
                    if i < n:
                        mask(i)
                    if 0 <= i - 2 < n:
                        invert(i - 2)
                    if i < n:
                        maximum(i)
                    if 0 <= i - 2 < n:
                        weigh(i - 2)
                    if i >= 8 and i % 4 == 0 and (i - 8) // 4 < n // 4:
                        gather((i - 8) // 4)
                    if ada is not None and i < n:
                        split(used[0] + ada_due(i).stop + 1)
                if ada is not None:
                    ada_cols(ADA // 2 - 1, ada)
                    used[0] += ADA
                T.up("att", n)
                T.up("att_o", n // 4)

            def rope(v, heads, t, rt=rt):
                x1, x2 = v[:, :, 0:DH // 2], v[:, :, DH // 2:DH]
                w = heads * DH // 2
                cb = cosT[:, t, :].unsqueeze(1).to_broadcast([P, heads, DH // 2])
                sb_ = sinT[:, t, :].unsqueeze(1).to_broadcast([P, heads, DH // 2])
                r = [x[:, 0:w].rearrange("p (h d) -> p h d", h=heads) for x in rt]
                dve.tensor_tensor(r[0], x1, cb, ALU.mult)
                dve.tensor_tensor(r[1], x2, sb_, ALU.mult)
                dve.tensor_tensor(r[2], x2, cb, ALU.mult)
                link(dve.tensor_tensor(r[3], x1, sb_, ALU.mult))
                dve.tensor_tensor(x1, r[0], r[1], ALU.subtract)
                link(dve.tensor_tensor(x2, r[2], r[3], ALU.add))

            dve.sem_inc(sem("conv_used"), 1)
            normalise(h, TA)
            split(2)
            dve.wait_ge(sem("wsT_ready"), 1)
            dve.memset(wsT[DH:P, :, 0:DH], 0.0).then_inc(sem("wsT_ready"), 1)
            tail(xT_c)
            skip(1)
            dve.wait_ge(sem("cols_landed"), 16)
            dve.wait_ge(sem("consts_landed"), 16 * 4)
            NF = DH // 2
            link(dve.tensor_copy(st[:, 24:26], posi[:, :]))
            for t in range(NT):
                m = dve.tensor_scalar(rot[:, 0, t * NF:(t + 1) * NF], rows[:, R_IF:R_IF + NF], st[:, 24 + t:25 + t], None, ALU.mult)
            link(m)
            for k, quarter in ((1, 0.0), (3, 0.25)):
                link(dve.tensor_scalar(rot[:, 2, :], rot[:, 0, :], 1.0 / (2 * PI), quarter, ALU.mult, ALU.add))
                link(dve.tensor_scalar(rot[:, 2, :], rot[:, 2, :], ROUND, -ROUND, ALU.add, ALU.add))
                link(dve.scalar_tensor_tensor(rot[:, k, :], rot[:, 2, :], -TWO_PI_A, rot[:, 0, :], ALU.mult, ALU.add))
                link(dve.scalar_tensor_tensor(rot[:, k, :], rot[:, 2, :], -TWO_PI_B, rot[:, k, :], ALU.mult, ALU.add))
                link(dve.scalar_tensor_tensor(rot[:, k, :], rot[:, 2, :], -TWO_PI_C, rot[:, k, :], ALU.mult, ALU.add))
                link(dve.tensor_scalar(rot[:, k, :], rot[:, k, :], quarter * 2 * PI, 3.1415925, ALU.add, ALU.min))
                m = dve.tensor_scalar(rot[:, k, :], rot[:, k, :], -3.1415925, None, ALU.max)
                if k == 1:
                    link(m)
            m.then_inc(sem("angle"), 1)
            dve.tensor_scalar(st[:, 16:24], rows[:, R_SK:R_SK + 8], -1.0, None, ALU.mult)
            dve.wait_ge(sem("pool"), 5)
            link(dve.tensor_copy(iota[:, :], iotai[:, :]))

            skip(1)
            normalise(TB, TB, vg, "vn_ready")
            skip(1)
            dve.wait_ge(sem("cs"), 1)
            link(dve.tensor_copy(c2[:, :, 0], cs[:, :]))
            dve.tensor_tensor(c2[:, :, 1], cs[:, :], c2[:, :, 0].bitcast(F32), ALU.subtract).then_inc(sem("c_ready"), 1)
            skip(1)
            T.up("acc", 4)
            dve.wait_ge(sem("acc_free"), 4)
            for g in range(KT):
                dve.wait_ge(sem("spatial"), g // 2 * 2 + 2)
                u = TA[:, :, g * P:(g + 1) * P]
                s_ = ps[:, g // 2, (g % 2) * S:(g % 2 + 1) * S].rearrange("p (t c) -> p t c", t=NT)
                dve.scalar_tensor_tensor(u, s_, cols[:, C_BS + g:C_BS + g + 1], u, ALU.add, ALU.mult).then_inc(sem("gz_ready"), 1)
            tail(xT_c)
            residual()
            normalise(h, TA)
            tail(xT_c)
            conv_ffn(0)
            normalise(h, TA)
            tail(xT_c)
            skip(4)
            T.up("acc", 4)
            tail(xT_b)
            skip(2)
            T.up("acc", 2)
            T.up("tr", 8)
            dve.wait_ge(sem("bias_ready"), 1)
            attention(CHUNKED, 0)
            residual()
            normalise(h, TA)
            tail(xT_c)
            conv_ffn(1)
            dve.wait_ge(sem("fg1_landed"), 16)
            normalise(h, h, gates[:, 0, :], "h_normed")
            normalise(h, TA)
            widen_gates(0)
            tail(xT_c)
            skip(2)
            T.up("acc", 2)
            dve.wait_ge(sem("acc_free"), T("acc"))
            fb = rows[:, R_FB:R_FB + 8].unsqueeze(1).to_broadcast([P, NT, 8])
            link(dve.tensor_tensor(lgf[:, 0], te[:, :, 1536:1544], fb, ALU.add))
            link(dve.tensor_scalar(lgf[:, 1], lgf[:, 0], -1.0, None, ALU.mult))
            dve.tensor_tensor(lgf[:, 2], lgf[:, 0], lgf[:, 1], ALU.max).then_inc(sem("lgf"), 1)
            dve.wait_ge(sem("lgf_act"), 1)
            dve.tensor_scalar(lgf[:, 2], lgf[:, 1], 1.0, None, ALU.add).then_inc(sem("lgf"), 1)
            dve.wait_ge(sem("lgf_act"), 2)
            link(dve.tensor_scalar(lgf[:, 0], lgf[:, 0], 0.0, None, ALU.min))
            dve.tensor_tensor(lgf[:, 4], lgf[:, 0], lgf[:, 3], ALU.subtract).then_inc(sem("logf"), 1)
            skip(1)
            dve.wait_ge(sem("tables"), 2)
            for t in range(NT):
                rope(te[:, t, 1544:2184].rearrange("p (h d) -> p h d", h=10), 10, t)
            dve.sem_inc(sem("rope_done"), 1)
            skip(2)
            T.up("acc", 3)
            dve.wait_ge(sem("cum_psum"), 1)
            dve.tensor_copy(cum, ps[:, 0, 0:16].rearrange("p (t h) -> p t h", t=NT)).then_inc(sem("cum_ready"), 1)
            dve.tensor_scalar(ncT, ps[0:8, 1, 0:S], -1.0, None, ALU.mult).then_inc(sem("cum_ready"), 1)
            T.up("tr", 7)
            dve.wait_ge(sem("cum_ready"), 2)
            attention(EVEN, 1)
            residual(0)
            normalise(h, TA)
            tail(xT_c)
            gated_ffn(1)
            normalise(h, TA)
            widen_gates(1)
            tail(xT_c)
            skip(2)
            T.up("acc", 2)
            dve.wait_ge(sem("acc_free"), T("acc"))
            for t in range(NT):
                rope(to[:, t, 1536:2112].rearrange("p (h d) -> p h d", h=9), 9, t, rt_o)
            dve.sem_inc(sem("rope_done"), 1)
            dve.tensor_scalar(st[:, 48:64].rearrange("p (t h) -> p t h", t=NT), to[:, :, 2112:2120],
                              8 ** -0.5 * DH ** -0.5, None, ALU.mult)
            def rotate(first, heads):
                dve.wait_ge(sem("acc_free"), T.up("acc"))
                for t in range(NT):
                    rope(to[:, t, first:first + heads * DH].rearrange("p (h d) -> p h d", h=heads), heads, t, rt_o)

            skip(1)
            rotate(0, 8)
            skip(1)
            for u in range(16):
                t, ih = u // 8, u % 8
                nk = (t + 1) * P
                dve.wait_ge(sem("ix_read"), u + 1)
                iw = st[:, 48 + u:49 + u]
                if ih == 0:
                    m = dve.tensor_scalar(score[:, t, 0:nk], relu[:, u % 2, 0:nk], iw, None, ALU.mult)
                else:
                    m = dve.scalar_tensor_tensor(score[:, t, 0:nk], relu[:, u % 2, 0:nk], iw, score[:, t, 0:nk],
                                                 ALU.mult, ALU.add)
                m.then_inc(sem("ix_added"), 1)
                dve.wait_ge(sem("ix_added"), u + 1)
            def both(op):
                for t in range(NT):
                    op(t, (t + 1) * P).then_inc(sem("dve"), 1)
                dve.wait_ge(sem("dve"), T.up("dve", NT))

            rotate(W, 8)
            dve.sem_inc(sem("rope_done"), 1)
            thr = lambda t: mx8[:, t, 7:8]
            both(lambda t, nk: dve.tensor_tensor(score[:, t, 0:nk], score[:, t, 0:nk], causal[:, S - nk:S], ALU.add))
            for n in range(TOPK // 8):
                src = score if n == 0 else left
                both(lambda t, nk: dve.max(mx8[:, t, :], src[:, t, 0:nk]))
                if n < TOPK // 8 - 1:
                    both(lambda t, nk: dve.match_replace(left[:, t, 0:nk], mx8[:, t, :], src[:, t, 0:nk], GONE))
                if n == 3:
                    rotate(2 * W, 4)
                    dve.sem_inc(sem("rope_done"), 1)
            skip(1)
            both(lambda t, nk: dve.tensor_scalar(gt[:, t, 0:nk], score[:, t, 0:nk], thr(t), None, ALU.is_gt))
            both(lambda t, nk: dve.tensor_scalar(eq[:, t, 0:nk], score[:, t, 0:nk], thr(t), None, ALU.is_equal))
            both(lambda t, nk: dve.reduce_sum(g2[:, t, 0:1], gt[:, t, 0:nk], AXX))
            both(lambda t, nk: dve.tensor_tensor_scan(left[:, t, 0:nk], eq[:, t, 0:nk], eq[:, t, 0:nk], g2[:, t, 0:1],
                                                      ALU.add, ALU.bypass))
            both(lambda t, nk: dve.scalar_tensor_tensor(eq[:, t, 0:nk], left[:, t, 0:nk], float(TOPK), eq[:, t, 0:nk],
                                                        ALU.is_le, ALU.mult))
            both(lambda t, nk: dve.tensor_tensor(gt[:, t, 0:nk], gt[:, t, 0:nk], eq[:, t, 0:nk], ALU.add))
            both(lambda t, nk: dve.tensor_scalar(gt[:, t, 0:nk], gt[:, t, 0:nk], -NEG, NEG, ALU.mult, ALU.add))
            both(lambda t, nk: dve.tensor_tensor(dsab[:, t, 0:nk], gt[:, t, 0:nk], causal[:, S - nk:S], ALU.min))
            T.up("tr", 3 + 4 + 2)
            attention(ODD)
            residual(0)
            normalise(h, TA)
            T.up("tr", 4)
            dve.wait_ge(sem("router"), 1)
            rb = rows[:, R_RB:R_RB + NE].unsqueeze(1).to_broadcast([P, NT, NE])
            dve.tensor_tensor(rt_logit, ps[:, 5, 0:NT * NE].rearrange("p (t e) -> p t e", t=NT), rb, ALU.add)\
                .then_inc(sem("logits_taken"), 1)
            dve.wait_ge(sem("logits_taken"), 1)
            for t in range(NT):
                link(dve.max(mx8[:, t, :], rt_logit[:, t, :]))
                link(dve.max_index(ix8[:, t, :], mx8[:, t, :], rt_logit[:, t, :]))
            dve.tensor_copy(idxf[:, :, :], ix8[:, :, :])
            dve.tensor_tensor(g2[:, :, 0], mx8[:, :, 1], mx8[:, :, 0], ALU.subtract).then_inc(sem("g2"), 1)
            dve.wait_ge(sem("g2_act"), 1)
            link(dve.tensor_scalar(g2[:, :, 2], g2[:, :, 1], 1.0, None, ALU.add))
            link(dve.reciprocal(g2[:, :, 2], g2[:, :, 2]))
            link(dve.tensor_tensor(g2[:, :, 3], g2[:, :, 1], g2[:, :, 2], ALU.mult))
            link(dve.memset(comb[:, :, 0:1], 0.0))
            for t in range(NT):
                cb = comb[:, t, 1:1 + NE]
                link(dve.tensor_scalar(cb, iota[:, 0:NE], idxf[:, t, 0:1], g2[:, t, 2:3], ALU.is_equal, ALU.mult))
                link(dve.tensor_scalar(eqe[:, t, :], iota[:, 0:NE], idxf[:, t, 1:2], g2[:, t, 3:4], ALU.is_equal, ALU.mult))
                link(dve.tensor_tensor(cb, cb, eqe[:, t, :], ALU.add))
                link(dve.tensor_scalar(member[:, t, :], iota[:, 0:NE], idxf[:, t, 0:1], None, ALU.is_equal))
                link(dve.tensor_scalar(eqe[:, t, :], iota[:, 0:NE], idxf[:, t, 1:2], None, ALU.is_equal))
                m = dve.tensor_tensor(member[:, t, :], member[:, t, :], eqe[:, t, :], ALU.add)
                if t == 0:
                    link(m)
            m.then_inc(sem("member"), 1)
            link(dve.memset(macc, 0.0))
            link(dve.tensor_copy(GT, macc[:, :, 0:P]))
            dve.wait_ge(sem("ranks"), 1)
            pl = place[:, :, 0:NE]
            link(dve.tensor_tensor(pl, ps[:, 5, 32:48].rearrange("p (t e) -> p t e", t=NT), member[:, :, :], ALU.mult))
            link(dve.tensor_scalar(pl, pl, -1.0, None, ALU.add))
            link(dve.tensor_scalar(place[:, :, NE:2 * NE], pl, -float(P), None, ALU.add))
            link(dve.tensor_reduce(st[0:1, 27:28], ps[0:1, 5, 48:48 + NE], AXX, ALU.max))
            link(dve.tensor_copy(count[:, 0:NE], ps[0:1, 5, 48:48 + NE]))
            dve.tensor_copy(count[:, NE:NE + 1], st[0:1, 27:28]).then_inc(sem("counted"), 1)
            dve.wait_ge(sem("counted"), 1)
            T.n.update(x_g=0, x_tr=0, x_xg=0, x_y=0, x_silu=0, x_tok=0, x_hi=0, x_a=0, x_added=0)

            def find_places(c):
                for t in range(NT):
                    m = dve.tensor_scalar(G[:, t, :], iota[:, :], place[:, t, c], None, ALU.is_equal)
                m.then_inc(sem("places"), 1)

            def split_gathered(between=lambda: None):
                for b in range(2):
                    if b:
                        between()
                    dve.wait_ge(sem("xg"), T.up("x_xg"))
                    k = slice(4 * b, 4 * b + 4)
                    link(dve.tensor_copy(xhi[:, k, 0:P], xg[:, k, :]))
                    m = dve.tensor_tensor(xlo[:, k, 0:P], xg[:, k, :], xhi[:, k, 0:P].bitcast(F32), ALU.subtract)
                m.then_inc(sem("xg_ready"), 1)
                T.up("xg_ready")
                dve.wait_ge(sem("xg_ready"), T("xg_ready"))
                dve.sem_inc(sem("g_taken"), 1)

            def product(j, i):
                m = 256 if j < 5 else P
                used[0] += 2
                split(used[0] + AHEAD, i, EXP)
                dve.wait_ge(sem("x_silu"), T.up("x_silu"))
                dve.tensor_tensor(abx[:, j % 2, 0:m], ps[:, (2, 0, 1)[j % 3], 0:m], sgx[:, 0:m], ALU.mult).then_inc(sem("x_tok"), 1)

            def lo_of(j):
                f = 2 if j < 5 else 1
                dve.wait_ge(sem("x_hi"), T.up("x_hi"))
                dve.tensor_tensor(alo[:, 2 * j:2 * j + f, 0:P], ps[:, 6, 0:f * P].rearrange("p (f s) -> p f s", f=f),
                                  ahi[:, 2 * j:2 * j + f, 0:P].bitcast(F32), ALU.subtract).then_inc(sem("x_a"), 1)
                dve.wait_ge(sem("x_a"), T.up("x_a"))
                dve.sem_inc(sem("x_tr_free"), 1)

            def lo_of_output():
                dve.wait_ge(sem("y_hi"), T.up("y_hi"))
                dve.tensor_tensor(ylo, ps[:, 3:5, :].rearrange("p n (k c) -> p (n k) c", c=P), yhi.bitcast(F32), ALU.subtract)\
                    .then_inc(sem("y_copied"), 1)

            def add_expert(i):
                for n in range(2):
                    dve.wait_ge(sem("y_psum"), T.up("x_y"))
                    for t in range(NT):
                        o = macc[:, t, n * W:(n + 1) * W]
                        m = dve.scalar_tensor_tensor(o, ps[:, (5, 7, 3, 4)[2 * n + t], :], comb[:, t, i], o, ALU.mult, ALU.add)
                m.then_inc(sem("y_added"), 1)

            for name in ("g_taken", "x_tr_free", "x_tok"):
                dve.sem_inc(sem(name), 1)
            T.n["xg_ready"] = 0
            find_places(bass.ds(0, 1))
            split(used[0] + AHEAD)
            split_gathered()
            dve.sem_inc(sem("y_copied"), 1)
            with dve.Fori(0, NE) as i:
                T.loop(i, x_xg=2, x_silu=6, x_hi=6, x_a=6, x_y=2, y_hi=1, dve=2, xg_ready=1, x_tr=0)
                product(0, i)
                add_expert(bass.ds(i, 1))
                for j in range(1, 6):
                    product(j, i)
                    lo_of(j - 1)
                    if j == 1:
                        dve.wait_ge(sem("gt_copied"), i + 1)
                        find_places(bass.ds(i + 1, 1))
                split(used[0] + 3, i, EXP)
                split_gathered(lambda: split(used[0] + 4, i, EXP))
                lo_of(5)
                used[0] += 6
                split(used[0] + AHEAD, i, EXP)
                lo_of_output()
                T.end(NE)
            pos[0] += EXP * (NE - 1)
            used[0] += EXP * (NE - 1) + AHEAD
            add_expert(slice(NE, NE + 1))
            most = dve.value_load(count[0:1, NE:NE + 1])
            with dve.If(most > P):
                with dve.Fori(0, NE) as i:
                    T.loop(i, x_xg=2, x_silu=6, x_hi=6, x_a=6, x_y=2, y_hi=1, dve=2, xg_ready=1)
                    n = dve.value_load(count[0:1, bass.ds(i, 1)])
                    with dve.If(n > P):
                        top[0] = used[0] + EXP
                        find_places(bass.ds(i + NE, 1))
                        split_gathered()
                        for j in range(6):
                            product(j, i)
                            if j:
                                lo_of(j - 1)
                        split(used[0] + 4, i, EXP)
                        lo_of(5)
                        used[0] += 6
                        split(used[0], i, EXP)
                        lo_of_output()
                        add_expert(bass.ds(i + 1, 1))
                    with dve.Else():
                        dve.drain()
                        for name, k in (("places", 1), ("dve", 2), ("xg_ready", 1), ("g_taken", 1), ("lo_done", EXP), ("x_tok", 6),
                                        ("x_a", 6), ("x_tr_free", 6), ("y_copied", 1), ("y_added", 1)):
                            dve.sem_inc(sem(name), k)
                    T.end(NE)
            with dve.Else():
                dve.drain()
                dve.sem_inc(sem("dve"), 2 * NE)
                dve.sem_inc(sem("y_copied"), NE)
                dve.sem_inc(sem("y_added"), NE)
            for t in range(NT):
                dve.wait_ge(sem("y_added"), 2 * NE + 1)
                link(dve.tensor_tensor(macc[:, t, :], macc[:, t, :], gates[:, 1, :], ALU.mult))
                dve.tensor_tensor(h[:, t, :], macc[:, t, :], h[:, t, :], ALU.add).then_inc(sem("h_added"), 1)
            dve.wait_ge(sem("fg_landed"), 16)
            normalise(h, TA, TC[:, 0, :], "y_ready")


_OUT = ((1, S, D), "float32")


def kernel(**inputs):
    import numpy as np
    import concourse.bacc as bacc
    from concourse.bass_utils import run_bass_kernel_spmd as run

    a = {k: np.asarray(v) for k, v in inputs.items()}

    def by_feature(v):
        v = v.reshape(-1, P)
        return v.T

    cols = np.concatenate([by_feature(v) for v in (
        a["a_norm_g"], a["kv_norm_g"], a["b_norm_g"], a["f_norm_g"][0], a["f_norm_g"][1],
        a["e_norm_mix_2"], a["e_norm_ffn_2"], a["o_norm_mix_2"], a["o_norm_ffn_2"],
        a["f_conv_w"], a["f_conv_b"], a["a_b_s"], a["e_ada_b_2"], a["o_ada_b_2"], a["c_2"])], axis=1)
    assert cols.shape == (P, C_END)
    half = DH // 2
    inv_freq = (ROPE_THETA ** (-np.arange(half, dtype=np.float32) / np.float32(half))).astype(np.float32)
    rows = np.concatenate([a["e_forget_b_2"].ravel(), a["e_sinks_2"].ravel(), a["o_router_b_2"].ravel(), inv_freq])[None]
    rel = np.clip(P + np.arange(P)[:, None] - np.arange(S)[None, :], -REL, REL) + REL
    arrays = {
        "x": a["x"], "cols": cols, "rows": rows, "vg": a["a_v_norm_g"], "fg1": a["final_norm_g"][None], "fg": a["final_norm_2"][None],
        "positions": by_feature(a["positions_2"]), "w_s": a["a_w_s"], "toep": a["b_rel_bias"][0][:, rel].transpose(1, 0, 2), "router": a["o_router_w_2"][0],
        "w_in": a["a_w_in"][0], "w_out": a["a_w_out"][0], "w_kv": a["w_kv"], "w_q": a["b_w_q"][0], "w_o": a["b_w_o"][0],
        "f_in": a["f_w_in"], "f_down": a["f_w_down"],
        "e_ada": a["e_ada_w_2"][0], "e_in": a["e_w_in_2"][0], "e_out": a["e_w_out_2"][0], "e_gate": a["e_ffn_gate_2"][0],
        "e_up": a["e_ffn_up_2"][0], "e_down": a["e_ffn_down_2"][0],
        "o_ada": a["o_ada_w_2"][0], "o_in": a["o_w_in_2"][0], "o_out": a["o_w_out_2"][0], "x_gate": a["o_exp_gate_2"][0],
        "x_up": a["o_exp_up_2"][0], "x_down": a["o_exp_down_2"][0],
    }
    arrays = {k: np.ascontiguousarray(v) for k, v in arrays.items()}
    nc = bacc.Bacc("TRN2", target_bir_lowering=False, num_devices=1)
    args = [nc.dram_tensor(f"{n}_dram", v.shape, mybir.dt.from_np(v.dtype), kind="ExternalInput").ap() for n, v in arrays.items()]
    args.append(nc.dram_tensor("y", _OUT[0], F32, kind="ExternalOutput").ap())
    build_program(nc, *args)
    return run(nc, [{f"{n}_dram": v for n, v in arrays.items()}], core_ids=[0]).results[0]["y"]
```
